# Optimizing a Trainium2 kernel written in Bass

```python
import jax, jax.numpy as jnp
from jax import lax
import numpy as np

D_MODEL = 1024
BATCH = 1
SEQ = 256
DEPTH = 1

FOX_HEADS = 8
FOX_HEAD_DIM = 64
FOX_WIDTH = FOX_HEADS * FOX_HEAD_DIM
QBLK = 128
HG_HEADS = 4
HG_DK = 64
HG_DV = 64
HG_KWIDTH = HG_HEADS * HG_DK
HG_WIDTH = HG_HEADS * HG_DV
HG_CHUNK = 64
POOL_WINDOWS = (2, 4, 8, 16)
POOL_GROUPS = 4
POOL_GROUP_DIM = 64
POOL_WIDTH = POOL_GROUPS * POOL_GROUP_DIM
MIX_WIDTH = FOX_WIDTH + HG_WIDTH + POOL_WIDTH
IN_COLS = 3 * FOX_WIDTH + FOX_HEADS + 2 * HG_KWIDTH + 2 * HG_WIDTH + POOL_WIDTH
N_EXPERTS = 32
TOP_K = 4
D_FF = 1024
SWIGLU_LIMIT = 7.0
SWIGLU_ALPHA = 1.702
MOE_BLOCK = 256
RMS_EPS = 1e-5

kernel_name = 'hybrid_fox_hgrn2_pool_moe_trunk'

def rmsnorm(x, g):
    xf = x.astype(jnp.float32)
    y = xf * lax.rsqrt(jnp.mean(xf * xf, axis=-1, keepdims=True) + RMS_EPS)
    return (y * g.astype(jnp.float32)).astype(x.dtype)

def split_projection(proj):
    sizes = (FOX_WIDTH, FOX_WIDTH, FOX_WIDTH, FOX_HEADS,
             HG_KWIDTH, HG_KWIDTH, HG_WIDTH, HG_WIDTH, POOL_WIDTH)
    points, acc = [], 0
    for s in sizes[:-1]:
        acc += s
        points.append(acc)
    return jnp.split(proj, points, axis=-1)

def fox_attention(q, k, v, logf):
    B, H, S, Dh = q.shape
    c = jnp.cumsum(logf, axis=-1)
    scale = 1.0 / math.sqrt(Dh) if False else Dh ** -0.5
    kpos = jnp.arange(S)
    nq = S // QBLK

    def block(i):
        start = i * QBLK
        qb = lax.dynamic_slice_in_dim(q, start, QBLK, axis=2)
        cb = lax.dynamic_slice_in_dim(c, start, QBLK, axis=2)
        s = jnp.einsum('bhqd,bhkd->bhqk', qb, k).astype(jnp.float32) * scale
        s = s + cb[..., None] - c[:, :, None, :]
        qpos = start + jnp.arange(QBLK)
        s = jnp.where(kpos[None, :] <= qpos[:, None], s, -jnp.inf)
        p = jax.nn.softmax(s, axis=-1)
        return jnp.einsum('bhqk,bhkd->bhqd', p.astype(v.dtype), v)

    o = lax.map(block, jnp.arange(nq))
    return o.transpose(1, 2, 0, 3, 4).reshape(B, H, S, Dh)

def hgrn2_chunked(q, f_logit, v, lb):
    B, S, H, Dk = q.shape
    Dv = v.shape[-1]
    C = HG_CHUNK
    nC = S // C
    fl = f_logit.astype(jnp.float32)
    lbf = lb.astype(jnp.float32)
    logf = jnp.logaddexp(jnp.log(lbf), jnp.log1p(-lbf) + jax.nn.log_sigmoid(fl))
    kk = (1.0 - lbf) * jax.nn.sigmoid(-fl)

    def chunks(t):
        return t.reshape(B, nC, C, H, t.shape[-1]).transpose(1, 0, 3, 2, 4)

    a = jnp.cumsum(chunks(logf), axis=3)
    causal = jnp.tril(jnp.ones((C, C), dtype=bool))

    def step(state, xs):
        qc, kc, vc, ac = xs
        o_inter = jnp.einsum('bhtk,bhkv->bhtv', qc * jnp.exp(ac), state)
        diff = ac[:, :, :, None, :] - ac[:, :, None, :, :]
        decay = jnp.exp(jnp.where(causal[:, :, None], diff, -jnp.inf))
        scores = jnp.einsum('bhtk,bhsk,bhtsk->bhts', qc, kc, decay)
        o = o_inter + jnp.einsum('bhts,bhsv->bhtv', scores, vc)
        a_last = ac[:, :, -1]
        new_state = jnp.exp(a_last)[..., None] * state + jnp.einsum(
            'bhsk,bhsv->bhkv', kc * jnp.exp(a_last[:, :, None] - ac), vc)
        return new_state, o

    init = jnp.zeros((B, H, Dk, Dv), jnp.float32)
    _, o = lax.scan(step, init, (chunks(q.astype(jnp.float32)), chunks(kk),
                                 chunks(v.astype(jnp.float32)), a))
    return o.transpose(1, 0, 3, 2, 4).reshape(B, S, H, Dv)

def pool_mixer(u, pool_w, pool_scale):
    B, S, _ = u.shape
    uf = u.astype(jnp.float32).reshape(B, S, POOL_GROUPS, POOL_GROUP_DIM)
    cs = jnp.cumsum(uf, axis=1)
    pos = jnp.arange(1, S + 1, dtype=jnp.float32)
    outs = []
    for g, w in enumerate(POOL_WINDOWS):
        c = cs[:, :, g]
        prev = jnp.pad(c[:, :-w], ((0, 0), (w, 0), (0, 0)))
        mean = (c - prev) / jnp.minimum(pos, float(w))[None, :, None]
        outs.append(mean - uf[:, :, g])
    pooled = jnp.stack(outs, axis=2)
    y = jnp.einsum('bsgc,gcd->bsgd', pooled, pool_w.astype(jnp.float32))
    y = y.reshape(B, S, POOL_WIDTH) * pool_scale.astype(jnp.float32)
    return y.astype(u.dtype)

def mixer(h, w_in, b_f, fox_gain, lb, hg_gain, pool_w, pool_scale, w_out):
    B, S, _ = h.shape
    proj = h @ w_in
    fq, fk, fv, ff, gq, gf, gi, gg, pu = split_projection(proj)

    def heads(t):
        return t.reshape(B, S, FOX_HEADS, FOX_HEAD_DIM).transpose(0, 2, 1, 3)
    logf = jax.nn.log_sigmoid((ff + b_f).astype(jnp.float32)).transpose(0, 2, 1)
    o_fox = fox_attention(heads(fq), heads(fk), heads(fv), logf)
    o_fox = rmsnorm(o_fox, fox_gain.reshape(FOX_HEADS, 1, FOX_HEAD_DIM))
    o_fox = o_fox.transpose(0, 2, 1, 3).reshape(B, S, FOX_WIDTH)

    o_hg = hgrn2_chunked(gq.reshape(B, S, HG_HEADS, HG_DK), gf.reshape(B, S, HG_HEADS, HG_DK),
                         gi.reshape(B, S, HG_HEADS, HG_DV), lb.reshape(HG_HEADS, HG_DK))
    o_hg = o_hg.astype(h.dtype)
    o_hg = rmsnorm(o_hg, hg_gain.reshape(HG_HEADS, HG_DV)) * jax.nn.silu(gg.reshape(B, S, HG_HEADS, HG_DV))
    o_hg = o_hg.reshape(B, S, HG_WIDTH)

    o_pool = pool_mixer(pu, pool_w, pool_scale)

    return jnp.concatenate([o_fox, o_hg, o_pool], axis=-1) @ w_out

def moe(h, w_router, b_router, w1, b1, w2, b2):
    B, S, D = h.shape
    T = B * S
    M = T * TOP_K
    xt = h.reshape(T, D)
    logits = xt.astype(jnp.float32) @ w_router.astype(jnp.float32) + b_router.astype(jnp.float32)
    top_val, top_idx = lax.top_k(logits, TOP_K)
    gate = jax.nn.softmax(top_val, axis=-1)
    e_flat = top_idx.reshape(M)
    order = jnp.argsort(e_flat, stable=True)
    e_sorted = e_flat[order]
    tok_sorted = order // TOP_K
    gate_sorted = gate.reshape(M)[order]
    counts = jnp.bincount(e_flat, length=N_EXPERTS)
    padded = (counts + MOE_BLOCK - 1) // MOE_BLOCK * MOE_BLOCK
    start = jnp.cumsum(counts) - counts
    pend = jnp.cumsum(padded)
    pstart = pend - padded
    dst = pstart[e_sorted] + (jnp.arange(M) - start[e_sorted])
    R = -(-M // MOE_BLOCK) * MOE_BLOCK + N_EXPERTS * MOE_BLOCK
    NB = R // MOE_BLOCK
    buf = jnp.zeros((R, D), h.dtype).at[dst].set(xt[tok_sorted])
    block_e = jnp.minimum(jnp.searchsorted(pend, jnp.arange(NB) * MOE_BLOCK, side='right'),
                          N_EXPERTS - 1)

    def expert_block(args):
        xb, e = args
        hh = xb @ w1[e] + b1[e]
        glu = jnp.minimum(hh[:, 0::2], SWIGLU_LIMIT)
        lin = jnp.clip(hh[:, 1::2], -SWIGLU_LIMIT, SWIGLU_LIMIT)
        act = glu * jax.nn.sigmoid(SWIGLU_ALPHA * glu) * (lin + 1.0)
        return act @ w2[e] + b2[e]

    yb = lax.map(expert_block, (buf.reshape(NB, MOE_BLOCK, D), block_e))
    y_sorted = yb.reshape(R, D)[dst] * gate_sorted[:, None].astype(h.dtype)
    out = jax.ops.segment_sum(y_sorted, tok_sorted, num_segments=T)
    return out.reshape(B, S, D)

def setup_inputs(seed: int = 0) -> dict:
    key = jax.random.key(seed)
    ks = jax.random.split(key, 18)
    nrm = jax.random.normal
    L, D, E, F = DEPTH, D_MODEL, N_EXPERTS, D_FF
    res_scale = (2 * DEPTH) ** -0.5
    return {
        'x': nrm(ks[0], (BATCH, SEQ, D), jnp.float32),
        'norm_mix': 1.0 + 0.02 * nrm(ks[1], (L, D), jnp.float32),
        'w_in': nrm(ks[2], (L, D, IN_COLS), jnp.float32) * D ** -0.5,
        'b_fox_f': 1.5 + 0.5 * nrm(ks[3], (L, FOX_HEADS), jnp.float32),
        'fox_gain': 1.0 + 0.02 * nrm(ks[4], (L, FOX_WIDTH), jnp.float32),
        'hgrn_lb': 0.1 * nrm(ks[5], (L, HG_KWIDTH), jnp.float32),
        'hgrn_gain': 1.0 + 0.02 * nrm(ks[6], (L, HG_WIDTH), jnp.float32),
        'pool_w': nrm(ks[7], (L, POOL_GROUPS, POOL_GROUP_DIM, POOL_GROUP_DIM), jnp.float32) * POOL_GROUP_DIM ** -0.5,
        'pool_scale': 1.0 + 0.1 * nrm(ks[8], (L, POOL_WIDTH), jnp.float32),
        'w_out': nrm(ks[9], (L, MIX_WIDTH, D), jnp.float32) * MIX_WIDTH ** -0.5 * res_scale,
        'norm_moe': 1.0 + 0.02 * nrm(ks[10], (L, D), jnp.float32),
        'w_router': nrm(ks[11], (L, D, E), jnp.float32) * D ** -0.5,
        'b_router': 0.01 * nrm(ks[12], (L, E), jnp.float32),
        'w1': nrm(ks[13], (L, E, D, 2 * F), jnp.float32) * D ** -0.5,
        'b1': 0.01 * nrm(ks[14], (L, E, 2 * F), jnp.float32),
        'w2': nrm(ks[15], (L, E, F, D), jnp.float32) * F ** -0.5 * res_scale,
        'b2': 0.01 * nrm(ks[16], (L, E, D), jnp.float32),
        'norm_final': 1.0 + 0.02 * nrm(ks[17], (D,), jnp.float32),
    }

def reference(x, norm_mix, w_in, b_fox_f, fox_gain, hgrn_lb, hgrn_gain, pool_w, pool_scale,
              w_out, norm_moe, w_router, b_router, w1, b1, w2, b2, norm_final):
    p = jax.nn.softmax(hgrn_lb.astype(jnp.float32), axis=0)
    cs = jnp.cumsum(p, axis=0)
    lbs = cs - cs[0:1]
    h = x
    for l in range(DEPTH):
        h = h + mixer(rmsnorm(h, norm_mix[l]), w_in[l], b_fox_f[l], fox_gain[l], lbs[l],
                      hgrn_gain[l], pool_w[l], pool_scale[l], w_out[l])
        h = h + moe(rmsnorm(h, norm_moe[l]), w_router[l], b_router[l], w1[l], b1[l], w2[l], b2[l])
    return rmsnorm(h, norm_final)


_drawn_inputs = setup_inputs


def setup_inputs(seed=0):
    import zlib

    import numpy as np

    out = dict(_drawn_inputs(seed))
    spreads = {}
    factors = {'fox_gain': 8.865,
     'hgrn_gain': 20.898,
     'b_router': 11.168,
     'b1': 27.059,
     'b2': 66.039,
     'norm_final': 23.681,
     'pool_scale': 3.257,
     'norm_moe': 4.41}
    for name, (base, spread) in spreads.items():
        noise = np.random.default_rng([zlib.crc32(name.encode()), seed]).standard_normal(out[name].shape)
        drawn = base * np.exp(spread * noise) if base else spread * noise
        out[name] = __import__('jax').numpy.asarray(drawn.astype(out[name].dtype))
    for name, factor in factors.items():
        out[name] = (out[name] * factor).astype(out[name].dtype)
    return out
```

```python
from contextlib import ExitStack

import concourse.bass as bass
from concourse import mybir

F32 = mybir.dt.float32
BF16 = mybir.dt.bfloat16
I16 = mybir.dt.int16
I32 = mybir.dt.int32
ALU = mybir.AluOpType
ACT = mybir.ActivationFunctionType
AX = mybir.AxisListType.X

P = 128
D = 1024
T = 256
TC = T // P
KC = D // P
FOX_H, HG_H, HD = 8, 4, 64
CHUNK = 64
WINDOWS = (2, 4, 8, 16)
E, TOPK, F = 32, 4, 1024
LIMIT, ALPHA = 7.0, 1.702
EPS = 1e-5
SLOTS = 64
PASSES = T // SLOTS
NEG = -1e30

BLOCKS = [("gf", 1800, True), ("gq", 1544, True), ("gi", 2056, False), ("pu", 2568, True), ("gg", 2312, False),
          ("fk0", 512, True), ("fk1", 768, True), ("fq0", 0, True), ("fq1", 256, True),
          ("fv0", 1024, False), ("fv1", 1280, False)]
FF_COL = 1536
BN = 256
NB = len(BLOCKS)
LEVELS = (64, 32, 16, 8, 4, 2, 1, 0)
NL = len(LEVELS)


def build(nc, x, norm_mix, w_in, b_fox_f, fox_gain, hgrn_lb, hgrn_gain, pool_w, pool_scale, w_out,
          norm_moe, w_router, b_router, w1, b1, w2, b2, norm_final, out):
    with ExitStack() as ctx:
        def sb(name, shape, dt=F32):
            return ctx.enter_context(nc.sbuf_tensor(name, shape, dt))

        def sem(name):
            return ctx.enter_context(nc.semaphore(name))

        w1_ring = sb("w1_ring", [P, KC, 2 * F])
        w2_ring = sb("w2_ring", [P, 2, KC, D])
        h = sb("h", [P, TC, D])
        xn = sb("xn", [P, TC, D])
        gain_a = sb("gain_a", [P, D])
        gain_b = sb("gain_b", [P, D])
        arena = sb("arena", [P, 8960])
        ident = sb("ident", [P, P])
        iota2 = sb("iota2", [P, 2, SLOTS])
        b1_parts = sb("b1_parts", [3 * E, 2 * F], BF16)
        b2_sb = sb("b2_sb", [E, D])
        wr_sb = sb("wr_sb", [P, KC, E])
        wff = sb("wff", [P, KC, P])
        before = sb("before", [P, P], BF16)
        ones_bf = sb("ones_bf", [P, P], BF16)
        lvl_mask = sb("lvl_mask", [P, NL, P], BF16)
        causal = sb("causal", [P, 2 * P])
        restart = sb("restart", [P, 2 * T], BF16)
        poolw_sb = sb("poolw_sb", [P, 2, HD])
        mix_gain = sb("mix_gain", [P, KC])
        br_sb = sb("br_sb", [P, E])
        small = sb("small", [P, 256])
        expert_id = sb("expert_id", [3 * E, PASSES * E], BF16)
        extra_pairs = sb("extra_pairs", [1, 1], I32)
        psum = ctx.enter_context(nc.psum_tensor("psum", [P, 8, 512], F32))

        at = [0]

        def take(*shape, start=None):
            if start is not None:
                at[0] = start
            n = 1
            for s in shape:
                n *= s
            v = arena[:, at[0]:at[0] + n]
            at[0] += n
            assert at[0] <= 8960
            if len(shape) == 2:
                v = v.rearrange("p (a b) -> p a b", a=shape[0])
            if len(shape) == 3:
                v = v.rearrange("p (a b c) -> p a b c", a=shape[0], b=shape[1])
            return v

        hT = take(KC, T)
        qT = take(4, T)
        kT = take(4, T)
        v_sb = take(TC, 512)
        gfT = take(2, T)
        gqT = take(2, T)
        gi = take(TC, T)
        gg = take(TC, T)
        puT = take(2, T)
        fox_r = take(4, T)
        fox_l = take(1, T)[:, 0, :]
        fox_o = take(TC, 512, start=0)
        fox_sq = take(TC, 512)
        scratch = w2_ring[:, 1, :, :].rearrange("p k n -> p (k n)")
        hg_a = scratch[:, 0:512]
        hg_k = scratch[:, 512:1024]
        hg_e = scratch[:, 1024:2048].rearrange("p (a b) -> p a b", a=2)
        hg_d = scratch[:, 2048:3072].rearrange("p (a b) -> p a b", a=2)
        hg_s = scratch[:, 3072:4096].rearrange("p (a b) -> p a b", a=8)
        hg_x = scratch[:, 4096:4608].rearrange("p (a b) -> p a b", a=4)
        hg_x_rows = scratch[:, 4096:4608].rearrange("p (a b) -> p a b", a=2)
        fox_pt = scratch[:, 4608:5376].rearrange("p (a b) -> p a b", a=2)
        hg_t = scratch[:, 5376:5888]
        ff_t = scratch[:, 5888:6144]
        oT = scratch[:, 6144:8192].rearrange("p (k t) -> p k t", k=KC)
        b1_tmp = scratch[0:3 * E, 6144:8192]
        xflat = xn[:, :, :].rearrange("p c n -> p (c n)")
        win_a = xflat[:, 0:512].rearrange("p (a b) -> p a b", a=2)
        win_b = xflat[:, 512:1024].rearrange("p (a b) -> p a b", a=2)
        win_inv = xflat[:, 1024:1536].rearrange("p (a b) -> p a b", a=2)
        fox_p = xflat[:, 0:1536].rearrange("p (a b) -> p a b", a=4)
        hg_o = xflat[:, 1536:2048]
        h2T = take(KC, T, start=0)
        xe = take(KC, SLOTS)
        put = take(2, TC, P)
        pick = take(2, TC, SLOTS)
        comb = take(TC, P)
        glu = take(512)
        lin = take(512)
        sig = take(512)
        act_r = take(512)
        actT = take(4, P)
        y_sb = take(512)
        rank_t = take(TC, PASSES * E)
        gate_t = take(TC, PASSES * E)
        which = take(SLOTS).bitcast(BF16).rearrange("p (a b) -> p a b", a=2)[0:3 * E]
        gateT = take(T)[0:E]
        logit = take(TC, E)
        strict = take(TC, E)
        tie = take(TC, E)
        tie_n = take(TC, E)
        chosen = take(TC, E)
        expo = take(TC, E)
        chosen_b = take(TC * E // 2).bitcast(BF16).rearrange("p (c e) -> p c e", c=TC)
        cnt = take(E)

        col = [0]

        def cols(n):
            col[0] += n
            return small[:, col[0] - n:col[0]]

        ss, ms, rstd = cols(TC), cols(TC), cols(TC)
        neg_half = cols(16)
        ffb = cols(1)
        l_scale, l_shift = cols(1), cols(1)
        r_neg, r_one = cols(4), cols(4)
        rowsum, rowinv = cols(16), cols(16)
        fox_ms, fox_r2 = cols(16), cols(16)
        hg_ms, hg_r2 = cols(8), cols(8)
        negmax = cols(16)
        lbraw, lbe, lbp, lb, one_lb = cols(2), cols(2), cols(2), cols(2), cols(2)
        ref2 = cols(2)
        top8 = cols(16).rearrange("p (c k) -> p c k", c=TC)
        nstrict, need, negtop, gsum, ginv = cols(2), cols(2), cols(2), cols(2), cols(2)
        nmax, over = cols(1), cols(3)

        x_in = [sem(f"x_in{c}") for c in range(TC)]
        mixgain_in, small_in = sem("mixgain_in"), sem("small_in")
        wff_in, ffb_in, b1_in, late_in = sem("wff_in"), sem("ffb_in"), sem("b1_in"), sem("late_in")
        block_in = [sem(f"block_in{n}") for n in range(NB)]
        wout_in = [sem(f"wout_in{n}") for n in range(4)]
        w1_in = [sem(f"w1_in{k}") for k in range(KC)]
        w2_in = [[sem(f"w2_in{b}_{k}") for k in range(4)] for b in range(2)]
        finalgain_in, out_done = sem("finalgain_in"), sem("out_done")
        pool_chain, dve_chain, act_chain = sem("pool_chain"), sem("dve_chain"), sem("act_chain")
        consts, wff_zero, wff_ready, b1_split = sem("consts"), sem("wff_zero"), sem("wff_ready"), sem("b1_split")
        sumsq, rstd_ready, xn_ready, xT_done, hT_ready = (sem("sumsq"), sem("rstd_ready"), sem("xn_ready"),
                                                          sem("xT_done"), sem("hT_ready"))
        ff_done, ff_z, ff_ln, fox_lr = sem("ff_done"), sem("ff_z"), sem("ff_ln"), sem("fox_lr")
        proj_done, proj_out = sem("proj_done"), sem("proj_out")
        hg_ln, hg_karg, hg_kexp, hg_targ, hg_tln = (sem("hg_ln"), sem("hg_karg"),
                                                          sem("hg_kexp"), sem("hg_targ"), sem("hg_tln"))
        lvl_arg, lvl_exp, lvl_dec, lvl_mm, lvl_taken = (sem("lvl_arg"), sem("lvl_exp"), sem("lvl_dec"),
                                                        sem("lvl_mm"), sem("lvl_taken"))
        pooled_ready, pool_mm, pool_out = sem("pooled_ready"), sem("pool_mm"), sem("pool_out")
        score_mm, score_max, prob_ready, probT_mm, probT_ready, pv_mm = (
            sem("score_mm"), sem("score_max"), sem("prob_ready"), sem("probT_mm"), sem("probT_ready"), sem("pv_mm"))
        hg_mm, hg_copied, hg_sq, hg_var, hg_rstd = (sem("hg_mm"), sem("hg_copied"), sem("hg_sq"),
                                                  sem("hg_var"), sem("hg_rstd"))
        silu_exp, hg_ready, hgT_mm, hgT_out = sem("silu_exp"), sem("hg_ready"), sem("hgT_mm"), sem("hgT_out")
        fox_div, fox_sqd, fox_var, fox_rstd, fox_ready, foxT_mm, foxT_out = (
            sem("fox_div"), sem("fox_sqd"), sem("fox_var"), sem("fox_rstd"), sem("fox_ready"), sem("foxT_mm"),
            sem("foxT_out"))
        mix_mm, h1_ready, sumsq2, rstd2, xn2_ready, x2T_mm, h2T_out = (
            sem("mix_mm"), sem("h1_ready"), sem("sumsq2"), sem("rstd2"), sem("xn2_ready"), sem("x2T_mm"),
            sem("h2T_out"))
        logit_mm, top_ready, gate_exp, chosen_ready, rank_mm, count_ready = (
            sem("logit_mm"), sem("top_ready"), sem("gate_exp"), sem("chosen_ready"), sem("rank_mm"),
            sem("count_ready"))
        gate_ready, gateT_mm, gateT_out, bias2_mm, bias2_added = (
            sem("gate_ready"), sem("gateT_mm"), sem("gateT_out"), sem("bias2_mm"), sem("bias2_added"))
        sel_ready, gather_mm, xe_ready, actT_mm, actT_ready, comb_mm, comb_ready = (
            sem("sel_ready"), sem("gather_mm"), sem("xe_ready"), sem("actT_mm"), sem("actT_ready"),
            sem("comb_mm"), sem("comb_ready"))
        glu_ready, lin_ready, sig_ready, gated, act_ready = (
            sem("glu_ready"), sem("lin_ready"), sem("sig_ready"), sem("gated"), sem("act_ready"))
        y_ready, put_mm, put_added = sem("y_ready"), sem("put_mm"), sem("put_added")
        w1_used, w2_used = sem("w1_used"), sem("w2_used")
        sumsq3, rstd3, final_ready = sem("sumsq3"), sem("rstd3"), sem("final_ready")

        x_v = x[0].rearrange("(c p) n -> p c n", p=P)
        out_v = out[0].rearrange("(c p) n -> p c n", p=P)
        w_in_v = w_in[0].rearrange("(k p) n -> p k n", p=P)
        w_out_v = w_out[0].rearrange("(k p) n -> p k n", p=P)
        w1_v = w1[0].rearrange("e (k p) n -> e p k n", p=P)
        w2_v = w2[0].rearrange("e (k p) n -> e p k n", p=P)

        def block_sb(n):
            if n < 3:
                return w2_ring[:, 0, 2 * n:2 * n + 2, :].rearrange("p a (b n) -> p (a b) n", n=BN)
            return w1_ring[:, n - 3, :].rearrange("p (k n) -> p k n", n=BN)

        block = ctx.enter_context(nc.Block())

        @block.sync
        def _(sp):
            for c in range(TC):
                sp.dma_start(h[:, c, :], x_v[:, c, :]).then_inc(x_in[c], 16)
            for n, (_, c0, _) in enumerate(BLOCKS):
                sp.dma_start(block_sb(n), w_in_v[:, :, c0:c0 + BN]).then_inc(block_in[n], 16)
            sp.wait_ge(proj_done, 3)
            for n in range(4):
                sp.dma_start(w2_ring[:, 0, 2 * n:2 * n + 2, :], w_out_v[:, 2 * n:2 * n + 2, :]).then_inc(wout_in[n], 16)
            for k in range(KC):
                sp.wait_ge(proj_done, 4 + k)
                sp.dma_start(w1_ring[:, k, :], w1_v[0, :, k, :]).then_inc(w1_in[k], 16)
            sp.wait_ge(mix_mm, TC)
            for k in range(4):
                sp.dma_start(w2_ring[:, 0, 2 * k:2 * k + 2, :], w2_v[0, :, 2 * k:2 * k + 2, :]).then_inc(w2_in[0][k], 16)
            for k in range(4):
                sp.dma_start(w2_ring[:, 1, 2 * k:2 * k + 2, :], w2_v[1, :, 2 * k:2 * k + 2, :]).then_inc(w2_in[1][k], 16)

            def load_w1(i):
                e = i % E
                for k in range(KC):
                    sp.wait_ge(w1_used, KC * (i - 1) + k + 1)
                    sp.dma_start(w1_ring[:, k, :], w1_v[bass.ds(e, 1), :, k, :].rearrange("e p n -> (e p) n")
                                 ).then_inc(w1_in[k], 16)

            def load_w2(i, b):
                e = i % E
                for k in range(4):
                    sp.wait_ge(w2_used, 4 * (i - 2) + k + 1)
                    sp.dma_start(w2_ring[:, b, 2 * k:2 * k + 2, :],
                                 w2_v[bass.ds(e, 1), :, 2 * k:2 * k + 2, :].rearrange("e p k n -> (e p) k n")
                                 ).then_inc(w2_in[b][k], 16)

            sp.wait_ge(count_ready, 1)
            extra = sp.value_load(extra_pairs[0:1, 0:1], min_val=0, max_val=(PASSES - 1) * E // 2)
            pairs = extra + E // 2
            n = extra * 2 + E
            load_w1(1)
            with sp.Fori(1, pairs) as j:
                i = j * 2
                load_w1(i)
                load_w2(i, 0)
                load_w1(i + 1)
                load_w2(i + 1, 1)
            for c in range(TC):
                sp.wait_ge(final_ready, c + 1)
                sp.dma_start(out_v[:, c, :], xn[:, c, :]).then_inc(out_done, 16)
            sp.wait_ge(out_done, 16 * TC)

        @block.gpsimd
        def _(pool):
            done = [0]

            def link(ins):
                done[0] += 1
                ins.then_inc(pool_chain, 1)
                pool.wait_ge(pool_chain, done[0])

            def band(v, op_base, pattern, mult, op=ALU.is_ge):
                link(pool.affine_select(out=v, in_=v, pattern=pattern, compare_op=op, fill=0.0, base=op_base,
                                        channel_multiplier=mult))

            link(pool.memset(neg_half, -0.5))
            link(pool.memset(ident[:, :], 0.0))
            link(pool.affine_select(out=ident[:, :], in_=ident[:, :], compare_op=ALU.not_equal, fill=1.0, base=0,
                                    pattern=[[-1, P]], channel_multiplier=1))
            link(pool.memset(ffb, 0.0))
            link(pool.memset(wff[:, :, :], 0.0))
            for r in range(4):
                pool.dma_start(wff[:, :, 32 * r:32 * r + FOX_H], w_in_v[:, :, FF_COL:FF_COL + FOX_H]).then_inc(wff_in, 16)
                pool.dma_start(ffb[32 * r:32 * r + FOX_H], b_fox_f.rearrange("a n -> n a")).then_inc(ffb_in, 16)
            for r in range(3):
                pool.dma_start(b1_tmp[E * r:E * r + E, :], b1[0]).then_inc(b1_in, 16)
            link(pool.memset(l_scale, 0.0))
            link(pool.memset(l_shift, 0.0))
            link(pool.memset(r_neg, 0.0))
            link(pool.memset(r_one, 0.0))
            for q in range(4):
                rows = slice(32 * q, 32 * q + 32)
                link(pool.memset((l_scale if q % 2 == 0 else l_shift)[rows], 1.0))
                target = (r_one if q % 2 == 0 else r_neg)[rows]
                link(pool.memset(target, 1.0 if q % 2 == 0 else -1.0))
                band(target, -(q // 2), [[-2, 4]], 1, ALU.is_equal)
            link(pool.memset(restart[:, :], 1.0))
            link(pool.affine_select(out=restart[:, :].rearrange("p (a b) -> p a b", b=CHUNK),
                                    in_=restart[:, :].rearrange("p (a b) -> p a b", b=CHUNK),
                                    compare_op=ALU.not_equal, fill=0.0, base=0, pattern=[[0, 2 * T // CHUNK], [1, CHUNK]],
                                    channel_multiplier=0))
            link(pool.memset(lvl_mask[:, :, :], 0.0))
            for n, half in enumerate(LEVELS):
                if half == 0:
                    link(pool.memset(lvl_mask[:, n, :], 1.0))
                    band(lvl_mask[:, n, :], 0, [[-1, P]], 1, ALU.is_equal)
                    continue
                nb = P // (2 * half)
                v = lvl_mask[:, n, :].rearrange("p (a b) -> p a b", b=2 * half)[:, :, half:2 * half]
                link(pool.memset(v, 1.0))
                band(v, 0, [[-2 * half, nb], [0, half]], 1)
                band(v, half - 1, [[2 * half, nb], [0, half]], -1)
            link(pool.memset(causal[:, :], 0.0))
            link(pool.affine_select(out=causal[:, P:], in_=causal[:, P:], compare_op=ALU.is_ge, fill=NEG, base=0,
                                    pattern=[[-1, P]], channel_multiplier=1))
            link(pool.memset(hg_s, 0.0))
            link(pool.memset(ones_bf[:, :], 1.0))
            pool.memset(before[:, :], 1.0).then_inc(consts, 1)
            pool.wait_ge(consts, 1)
            pool.wait_ge(sumsq, TC)
            link(pool.tensor_scalar(ms, ss, 1.0 / D, EPS, ALU.mult, ALU.add))
            pool.tensor_tensor(rstd, ms, neg_half[:, 0:TC], ALU.pow).then_inc(rstd_ready, 1)
            pool.wait_ge(rstd_ready, 1)
            band(before[:, :], -1, [[1, P]], -1)
            link(pool.iota(iota2[:, :, :], pattern=[[0, 2], [1, SLOTS]], base=0, channel_multiplier=0,
                           allow_small_or_imprecise_dtypes=True))
            link(pool.memset(expert_id[:, :], 1.0))
            for r in range(3):
                v = expert_id[E * r:E * r + E, :].rearrange("p (a e) -> p a e", e=E)
                band(v, 0, [[0, PASSES], [-1, E]], 1, ALU.is_equal)
            pool.wait_ge(xT_done, TC)
            link(pool.iota(win_inv, pattern=[[0, 2], [1, T]], base=1, channel_multiplier=0,
                           allow_small_or_imprecise_dtypes=True))
            for g, w in enumerate(WINDOWS):
                rows = slice(HD * (g % 2), HD * (g % 2) + HD)
                ins = pool.memset(win_inv[rows, g // 2, w:T], float(w))
                if g < 3:
                    link(ins)
            ins.then_inc(consts, 1)
            pool.wait_ge(consts, 2)
            pool.wait_ge(b1_in, 48)
            for r in range(3):
                rows = slice(E * r, E * r + E)
                for step in range(r + 1):
                    if step:
                        link(pool.tensor_tensor(b1_tmp[rows], b1_tmp[rows], b1_parts[rows, :], ALU.subtract))
                    ins = pool.tensor_copy(b1_parts[rows, :], b1_tmp[rows])
                    if (r, step) != (2, 2):
                        link(ins)
            ins.then_inc(b1_split, 1)
            pool.wait_ge(b1_split, 1)
            pool.wait_ge(proj_out, 4)
            pool.wait_ge(pooled_ready, 1)
            src = puT
            for step, w in enumerate(WINDOWS):
                sh = w // 2
                dst = (win_a, win_b)[step % 2]
                if step >= 1:
                    link(pool.tensor_copy(dst[:, :, :], src[:, :, :]))
                for g in range(step, 4):
                    rows = slice(HD * (g % 2), HD * (g % 2) + HD)
                    link(pool.tensor_tensor(dst[rows, g // 2, sh:T], src[rows, g // 2, sh:T],
                                            src[rows, g // 2, 0:T - sh], ALU.add))
                    if step == 0:
                        link(pool.tensor_copy(dst[rows, g // 2, 0:sh], src[rows, g // 2, 0:sh]))
                src = dst
            link(pool.tensor_tensor(win_a, src, win_inv, ALU.mult))
            pool.tensor_tensor(win_b, win_a, puT, ALU.subtract).then_inc(pooled_ready, 1)
            pool.wait_ge(pooled_ready, 2)
            pool.wait_ge(hg_var, 1)
            pool.tensor_tensor(hg_r2, hg_ms, neg_half[:, 0:8], ALU.pow).then_inc(hg_rstd, 1)
            pool.wait_ge(hg_rstd, 1)
            pool.wait_ge(fox_var, 1)
            pool.tensor_tensor(fox_r2, fox_ms, neg_half, ALU.pow).then_inc(fox_rstd, 1)
            for which_norm, (got, give) in enumerate(((sumsq2, rstd2), (sumsq3, rstd3))):
                pool.wait_ge((fox_rstd, rstd2)[which_norm], 1 + which_norm)
                for c in range(TC):
                    if c:
                        pool.wait_ge(give, c)
                    pool.wait_ge(got, c + 1)
                    link(pool.tensor_scalar(ms[:, c:c + 1], ss[:, c:c + 1], 1.0 / D, EPS, ALU.mult, ALU.add))
                    pool.tensor_tensor(rstd[:, c:c + 1], ms[:, c:c + 1], neg_half[:, 0:1], ALU.pow).then_inc(give, 1)

        @block.scalar
        def _(act):
            done = [0]

            def link(ins):
                done[0] += 1
                ins.then_inc(act_chain, 1)
                act.wait_ge(act_chain, done[0])

            act.dma_start(gain_a[:, :], norm_mix[0].partition_broadcast(P)).then_inc(mixgain_in, 16)
            act.dma_start(lbraw, hgrn_lb[0].rearrange("(c p) -> p c", p=P), allow_slow_non_contiguous=True).then_inc(small_in, 16)
            act.dma_start(mix_gain[:, 0:4], fox_gain[0].rearrange("(c p) -> p c", p=P), allow_slow_non_contiguous=True).then_inc(small_in, 16)
            act.dma_start(mix_gain[:, 4:6], hgrn_gain[0].rearrange("(c p) -> p c", p=P), allow_slow_non_contiguous=True).then_inc(small_in, 16)
            act.dma_start(mix_gain[:, 6:8], pool_scale[0].rearrange("(c p) -> p c", p=P), allow_slow_non_contiguous=True).then_inc(small_in, 16)
            for a in range(2):
                act.dma_start(poolw_sb[:, a, :], pool_w[0, 2 * a:2 * a + 2].rearrange("g c d -> (g c) d")).then_inc(small_in, 16)
            act.dma_start(gain_b[:, :], norm_moe[0].partition_broadcast(P)).then_inc(late_in, 16)
            act.dma_start(wr_sb[:, :, :], w_router[0].rearrange("(k p) e -> p k e", p=P)).then_inc(late_in, 16)
            act.dma_start(br_sb[:, :], b_router[0].partition_broadcast(P)).then_inc(late_in, 16)
            act.dma_start(b2_sb[:, :], b2[0]).then_inc(late_in, 16)
            for c in range(TC):
                act.wait_ge(x_in[c], 16)
                act.activation(xn[:, c, :], h[:, c, :], ACT.Square, accum_out=ss[:, c:c + 1]).then_inc(sumsq, 1)
            act.wait_ge(xT_done, TC)
            act.dma_start(gain_a[:, :], norm_final.partition_broadcast(P)).then_inc(finalgain_in, 16)
            for b in range(2):
                act.activation(hT[:, 2 * b:2 * b + 2, :], psum[:, 2 + b, :].rearrange("p (a t) -> p a t", a=2),
                               ACT.Copy).then_inc(hT_ready, 1)
            act.wait_ge(ff_z, 1)
            link(act.activation(ff_t, fox_l, ACT.Abs))
            link(act.activation(ff_t, ff_t, ACT.Exp, scale=-1.0))
            act.activation(ff_t, ff_t, ACT.Ln, bias=1.0).then_inc(ff_ln, 1)

            def take_block(n, dst, scale=1.0):
                act.wait_ge(proj_done, n + 1)
                act.activation(dst, psum[:, n % 2, :].rearrange("p (a t) -> p a t", a=2), ACT.Copy,
                               scale=scale).then_inc(proj_out, 1)

            def lvl(n):
                act.wait_ge(lvl_arg, n + 1)
                act.activation(hg_e[:, n % 2, :], hg_e[:, n % 2, :], ACT.Exp).then_inc(lvl_exp, 1)

            take_block(0, gfT)
            act.wait_ge(proj_out, 1)
            link(act.activation(hg_t, gfT.rearrange("p a t -> p (a t)"), ACT.Abs))
            link(act.activation(hg_t, hg_t, ACT.Exp, scale=-1.0))
            act.activation(hg_t, hg_t, ACT.Ln, bias=1.0).then_inc(hg_ln, 1)
            act.wait_ge(hg_karg, 1)
            act.activation(hg_k, hg_k, ACT.Exp).then_inc(hg_kexp, 1)
            act.wait_ge(hg_targ, 1)
            act.activation(hg_t, hg_t, ACT.Exp).then_inc(hg_tln, 1)
            act.wait_ge(hg_targ, 2)
            act.activation(hg_t, hg_t, ACT.Ln).then_inc(hg_tln, 1)
            take_block(1, gqT)
            take_block(2, gi)
            lvl(0)
            take_block(3, puT)
            lvl(1)
            take_block(4, gg)
            lvl(2)
            take_block(5, kT[:, 0:2, :])
            lvl(3)
            take_block(6, kT[:, 2:4, :])
            lvl(4)
            take_block(7, qT[:, 0:2, :], HD ** -0.5)
            lvl(5)
            take_block(8, qT[:, 2:4, :], HD ** -0.5)
            lvl(6)
            act.wait_ge(proj_out, 5)
            act.wait_ge(hg_karg, 2)
            act.activation(hg_t, gg.rearrange("p c n -> p (c n)"), ACT.Exp, scale=-1.0).then_inc(silu_exp, 1)
            lvl(7)
            take_block(9, v_sb[:, :, 0:BN])
            take_block(10, v_sb[:, :, BN:2 * BN])
            act.wait_ge(b1_split, 1)
            act.wait_ge(pool_mm, 1)
            act.wait_ge(small_in, 96)
            for g in range(2):
                for a in range(2):
                    rows = slice(HD * g, HD * g + HD)
                    act.activation(oT[rows, 6 + a, :], psum[rows, 7 - g, a * T:(a + 1) * T], ACT.Copy,
                                   scale=mix_gain[rows, 6 + a:7 + a]).then_inc(pool_out, 1)
            for hd in range(FOX_H):
                act.wait_ge(score_max, hd + 1)
                for c in range(TC):
                    v = fox_p[:, hd % 4, P * c:P * c + P * (c + 1)]
                    g = c * FOX_H + hd
                    act.activation(v, v, ACT.Exp, bias=negmax[:, g:g + 1],
                                   accum_out=rowsum[:, g:g + 1]).then_inc(prob_ready, 1)
            act.wait_ge(hg_copied, 1)
            act.activation(hg_e[:, 0, :], hg_o, ACT.Square).then_inc(hg_sq, 1)
            act.wait_ge(hgT_mm, 1)
            for a in range(2):
                act.activation(oT[:, 4 + a, :], psum[:, 3, a * T:(a + 1) * T], ACT.Copy,
                               scale=mix_gain[:, 4 + a:5 + a]).then_inc(hgT_out, 1)
            act.wait_ge(fox_div, 1)
            act.activation(fox_sq, fox_o, ACT.Square).then_inc(fox_sqd, 1)
            act.wait_ge(foxT_mm, 1)
            for a in range(2):
                act.activation(oT[:, a, :], psum[:, 0, a * T:(a + 1) * T], ACT.Copy,
                               scale=mix_gain[:, a:a + 1]).then_inc(foxT_out, 1)
            for c in range(TC):
                act.wait_ge(h1_ready, c + 1)
                act.activation(xn[:, c, :], h[:, c, :], ACT.Square, accum_out=ss[:, c:c + 1]).then_inc(sumsq2, 1)
            for c in range(TC):
                act.wait_ge(x2T_mm, c + 1)
                act.activation(h2T[:, 0:4, P * c:P * c + P], psum[:, (0, 2)[c], :].rearrange("p (a t) -> p a t", a=4),
                               ACT.Copy).then_inc(h2T_out, 1)
            for c in range(TC):
                act.wait_ge(top_ready, c + 1)
                act.activation(expo[:, c, :], logit[:, c, :], ACT.Exp, bias=negtop[:, c:c + 1]).then_inc(gate_exp, 1)
            act.wait_ge(gateT_mm, 1)
            act.activation(gateT, psum[0:E, 3, 0:T], ACT.Copy).then_inc(gateT_out, 1)

            def before_down(i, first=False):
                act.wait_ge(gather_mm, i + 1)
                act.activation(xe, psum[:, 0, :].rearrange("p (k s) -> p k s", k=KC), ACT.Copy).then_inc(xe_ready, 1)
                if not first:
                    transposed(i - 1)

            def transposed(i):
                act.wait_ge(actT_mm, i + 1)
                act.activation(actT, psum[:, 1, :].rearrange("p (j s) -> p j s", j=4), ACT.Copy).then_inc(actT_ready, 1)
                act.wait_ge(comb_mm, i + 1)
                act.activation(comb, psum[:, 2, 0:T].rearrange("p (c t) -> p c t", c=TC), ACT.Copy).then_inc(comb_ready, 1)

            def sigmoid(i):
                act.wait_ge(glu_ready, i + 1)
                act.activation(sig, glu, ACT.Sigmoid, scale=ALPHA).then_inc(sig_ready, 1)

            def y_copy(i):
                act.wait_ge(w2_used, 4 * i + 4)
                act.activation(y_sb, psum[:, 5, :], ACT.Copy).then_inc(y_ready, 1)

            act.wait_ge(count_ready, 1)
            extra = act.value_load(extra_pairs[0:1, 0:1], min_val=0, max_val=(PASSES - 1) * E // 2)
            pairs = extra + E // 2
            n = extra * 2 + E
            before_down(0, first=True)
            sigmoid(0)
            before_down(1)
            sigmoid(1)
            y_copy(0)
            with act.Fori(2, n) as i:
                before_down(i)
                sigmoid(i)
                y_copy(i - 1)
            transposed(n - 1)
            y_copy(n - 1)
            for c in range(TC):
                act.wait_ge(put_added, TC * n - 1 + c)
                act.activation(xn[:, c, :], h[:, c, :], ACT.Square, accum_out=ss[:, c:c + 1]).then_inc(sumsq3, 1)

        @block.vector
        def _(dve):
            done = [0]

            def link(ins):
                done[0] += 1
                ins.then_inc(dve_chain, 1)
                dve.wait_ge(dve_chain, done[0])

            dve.wait_ge(mixgain_in, 16)
            dve.wait_ge(rstd_ready, 1)
            for c in range(TC):
                dve.scalar_tensor_tensor(out=xn[:, c, :], in0=h[:, c, :], scalar=rstd[:, c:c + 1], in1=gain_a[:, :],
                                         op0=ALU.mult, op1=ALU.mult).then_inc(xn_ready, 1)
            dve.wait_ge(small_in, 96)
            link(dve.tensor_tensor(lbe, lbraw, lbraw, ALU.subtract))
            link(dve.tensor_scalar(lbe, lbe, 1.0, None, ALU.add))
            link(dve.reciprocal(lbp, lbe))
            link(dve.tensor_tensor(lbp, lbe, lbp, ALU.mult))
            link(dve.tensor_tensor(lb, lbp, lbp, ALU.subtract))
            link(dve.tensor_scalar(one_lb, lb, -1.0, 1.0, ALU.mult, ALU.add))
            dve.wait_ge(xT_done, TC)
            for b in range(2, 4):
                dve.tensor_copy(hT[:, 2 * b:2 * b + 2, :],
                                psum[:, 2 + b, :].rearrange("p (a t) -> p a t", a=2)).then_inc(hT_ready, 1)
            dve.wait_ge(ff_done, 1)
            dve.wait_ge(ffb_in, 64)
            dve.wait_ge(consts, 1)
            dve.tensor_scalar(fox_l, psum[:, 6, 0:T], ffb, None, ALU.add).then_inc(ff_z, 1)
            dve.wait_ge(consts, 2)
            dve.reciprocal(win_inv, win_inv).then_inc(pooled_ready, 1)
            dve.wait_ge(ff_ln, 1)
            link(dve.scalar_tensor_tensor(out=ff_t, in0=fox_l, scalar=0.0, in1=ff_t, op0=ALU.min, op1=ALU.subtract))
            link(dve.memset(hg_a[:, 0:T], 1.0))
            link(dve.tensor_tensor_scan(fox_l, hg_a[:, 0:T], ff_t, 0.0, ALU.mult, ALU.add))
            for j in range(4):
                dve.tensor_scalar(fox_r[:, j, :], fox_l, r_neg[:, j:j + 1], r_one[:, j:j + 1], ALU.mult, ALU.add
                                  ).then_inc(fox_lr, 1)
            dve.wait_ge(fox_lr, 4)
            dve.tensor_scalar(fox_l, fox_l, l_scale, l_shift, ALU.mult, ALU.add).then_inc(fox_lr, 1)
            gf = gfT.rearrange("p a t -> p (a t)")
            dve.wait_ge(hg_ln, 1)
            link(dve.scalar_tensor_tensor(out=hg_a, in0=gf, scalar=0.0, in1=hg_t, op0=ALU.min, op1=ALU.subtract))
            dve.tensor_tensor(hg_k, hg_a, gf, ALU.subtract).then_inc(hg_karg, 1)
            dve.tensor_scalar(hg_t, hg_a, -1.0, 40.0, ALU.mult, ALU.min).then_inc(hg_targ, 1)
            dve.wait_ge(hg_tln, 1)
            for a in range(2):
                v = hg_t[:, a * T:(a + 1) * T]
                ins = dve.tensor_scalar(v, v, lb[:, a:a + 1], one_lb[:, a:a + 1], ALU.mult, ALU.add)
            ins.then_inc(hg_targ, 1)
            dve.wait_ge(hg_kexp, 1)
            for a in range(2):
                v = hg_k[:, a * T:(a + 1) * T]
                link(dve.tensor_scalar(v, v, one_lb[:, a:a + 1], None, ALU.mult))
            dve.wait_ge(hg_tln, 2)
            link(dve.tensor_tensor(gf, hg_a, hg_t, ALU.add))
            dve.tensor_tensor_scan(hg_a, restart[:, :], gf, 0.0, ALU.mult, ALU.add).then_inc(hg_karg, 1)
            dve.wait_ge(hg_karg, 2)

            gq = gqT.rearrange("p a t -> p (a t)")

            def halves(v, half):
                w = v.rearrange("p (n b) -> p n b", b=2 * half)
                return w[:, :, 0:half], w[:, :, half:2 * half]

            def level_args(n):
                half = LEVELS[n]
                if n >= 2:
                    dve.wait_ge(lvl_dec, n - 1)
                lo_a, hi_a = halves(hg_a, half)
                lo_e, hi_e = halves(hg_e[:, n % 2, :], half)
                end = lo_a[:, :, half - 1:half].to_broadcast([P, 2 * T // (2 * half), half])
                dve.tensor_tensor(lo_e, end, lo_a, ALU.subtract)
                if half == CHUNK:
                    dve.tensor_copy(hi_e, hi_a).then_inc(lvl_arg, 1)
                else:
                    dve.tensor_tensor(hi_e, hi_a, end, ALU.subtract).then_inc(lvl_arg, 1)

            def level_decayed(n):
                half = LEVELS[n]
                dve.wait_ge(lvl_exp, n + 1)
                if n >= 2:
                    dve.wait_ge(lvl_mm, n - 1)
                lo_e, hi_e = halves(hg_e[:, n % 2, :], half)
                lo_d, hi_d = halves(hg_d[:, n % 2, :], half)
                dve.tensor_tensor(lo_d, halves(hg_k, half)[0], lo_e, ALU.mult)
                dve.tensor_tensor(hi_d, halves(gq, half)[1], hi_e, ALU.mult).then_inc(lvl_dec, 1)

            def level_take(n):
                dve.wait_ge(lvl_mm, n + 1)
                mask = lvl_mask[:, n, :].bitcast(I16).unsqueeze(1).to_broadcast([P, 8, P])
                dve.copy_predicated(hg_s, mask, psum[:, 3:5, :].rearrange("p a (b t) -> p (a b) t", t=P)
                                    ).then_inc(lvl_taken, 1)

            def cross_args(n):
                a2 = hg_a.rearrange("p (a t) -> p a t", a=2)
                e2 = hg_e[:, n % 2, :].rearrange("p (a t) -> p a t", a=2)
                end0 = a2[:, :, 63:64]
                end1 = a2[:, :, 127:128]
                link(dve.tensor_tensor(ref2.unsqueeze(2), end0, end1, ALU.add))
                dve.tensor_tensor(e2[:, :, 0:64], ref2.unsqueeze(2).to_broadcast([P, 2, 64]), a2[:, :, 0:64], ALU.subtract)
                dve.tensor_tensor(e2[:, :, 64:128], end1.to_broadcast([P, 2, 64]), a2[:, :, 64:128], ALU.subtract)
                dve.tensor_copy(e2[:, :, 128:192], a2[:, :, 128:192])
                dve.tensor_tensor(e2[:, :, 192:256], a2[:, :, 192:256], a2[:, :, 191:192].to_broadcast([P, 2, 64]),
                                  ALU.add).then_inc(lvl_arg, 1)

            def cross_decayed(n):
                dve.wait_ge(lvl_exp, n + 1)
                dve.wait_ge(lvl_mm, n - 1)
                e2 = hg_e[:, n % 2, :].rearrange("p (a t) -> p a t", a=2)
                d2 = hg_d[:, n % 2, :].rearrange("p (a t) -> p a t", a=2)
                dve.tensor_tensor(d2[:, :, 0:P], hg_k.rearrange("p (a t) -> p a t", a=2)[:, :, 0:P], e2[:, :, 0:P], ALU.mult)
                dve.tensor_tensor(d2[:, :, P:T], gqT[:, :, P:T], e2[:, :, P:T], ALU.mult).then_inc(lvl_dec, 1)

            dve.wait_ge(proj_out, 2)
            level_args(0)
            for n in range(7):
                if n < 6:
                    level_args(n + 1)
                else:
                    dve.wait_ge(lvl_dec, 6)
                    cross_args(7)
                level_decayed(n)
                if n >= 1:
                    level_take(n - 1)
            cross_decayed(7)
            level_take(6)
            level_take(7)

            dve.wait_ge(silu_exp, 1)
            link(dve.tensor_scalar(hg_t, hg_t, 1.0, None, ALU.add))
            link(dve.reciprocal(hg_t, hg_t))
            link(dve.tensor_tensor(hg_t, hg_t, gg.rearrange("p c n -> p (c n)"), ALU.mult))
            dve.wait_ge(lvl_mm, 9)
            dve.tensor_copy(hg_x_rows, psum[:, 3:5, 0:T]).then_inc(lvl_taken, 1)

            def masked_max(hd):
                dve.wait_ge(score_mm, hd + 1)
                for c in range(TC):
                    g = c * FOX_H + hd
                    v = fox_p[:, hd % 4, P * c:P * c + P * (c + 1)]
                    ins = dve.tensor_tensor_reduce(out=v, in0=psum[:, hd % 2, P * c:P * c + P * (c + 1)],
                                                   in1=causal[:, P * (1 - c):], scale=1.0, scalar=-3e38,
                                                   op0=ALU.add, op1=ALU.max, accum_out=negmax[:, g:g + 1])
                    link(ins)
                    ins = dve.tensor_scalar(negmax[:, g:g + 1], negmax[:, g:g + 1], -1.0, None, ALU.mult)
                ins.then_inc(score_max, 1)

            def probT_copy(hd):
                dve.wait_ge(probT_mm, hd + 1)
                if hd >= 2:
                    dve.wait_ge(pv_mm, hd - 1)
                dve.tensor_copy(fox_pt[:, hd % 2, :], psum[:, 2, 0:3 * P]).then_inc(probT_ready, 1)

            dve.wait_ge(pool_mm, 1)
            for hd in range(FOX_H + 1):
                if hd < FOX_H:
                    masked_max(hd)
                if hd >= 1:
                    probT_copy(hd - 1)
                if hd == 4:
                    dve.wait_ge(hg_mm, 1)
                    dve.tensor_copy(hg_o, psum[:, 7, :]).then_inc(hg_copied, 1)
            dve.wait_ge(hg_sq, 1)
            link(dve.tensor_reduce(hg_ms, hg_e[:, 0, :].rearrange("p (g d) -> p g d", d=HD), AX, ALU.add))
            dve.tensor_scalar(hg_ms, hg_ms, 1.0 / HD, EPS, ALU.mult, ALU.add).then_inc(hg_var, 1)
            link(dve.tensor_tensor(hg_t, hg_o, hg_t, ALU.mult))
            dve.wait_ge(pv_mm, FOX_H)
            link(dve.reciprocal(rowinv, rowsum))
            dve.tensor_tensor(fox_o.rearrange("p c (g d) -> p (c g) d", d=HD),
                              psum[:, 5:7, :].rearrange("p c (g d) -> p (c g) d", d=HD),
                              rowinv.unsqueeze(2).to_broadcast([P, 16, HD]), ALU.mult).then_inc(fox_div, 1)
            dve.wait_ge(hg_rstd, 1)
            dve.tensor_tensor(hg_o.rearrange("p (g d) -> p g d", d=HD), hg_t.rearrange("p (g d) -> p g d", d=HD),
                              hg_r2.unsqueeze(2).to_broadcast([P, 8, HD]), ALU.mult).then_inc(hg_ready, 1)
            dve.wait_ge(fox_sqd, 1)
            link(dve.tensor_reduce(fox_ms, fox_sq.rearrange("p c (g d) -> p (c g) d", d=HD), AX, ALU.add))
            dve.tensor_scalar(fox_ms, fox_ms, 1.0 / HD, EPS, ALU.mult, ALU.add).then_inc(fox_var, 1)
            dve.wait_ge(fox_rstd, 1)
            dve.tensor_tensor(fox_o.rearrange("p c (g d) -> p (c g) d", d=HD),
                              fox_o.rearrange("p c (g d) -> p (c g) d", d=HD),
                              fox_r2.unsqueeze(2).to_broadcast([P, 16, HD]), ALU.mult).then_inc(fox_ready, 1)
            dve.wait_ge(foxT_mm, 2)
            for a in range(2):
                dve.tensor_scalar(oT[:, 2 + a, :], psum[:, 1, a * T:(a + 1) * T], mix_gain[:, 2 + a:3 + a], None,
                                  ALU.mult).then_inc(foxT_out, 1)
            for c in range(TC):
                dve.wait_ge(mix_mm, c + 1)
                dve.tensor_tensor(h[:, c, :], h[:, c, :], psum[:, (5, 3)[c]:(7, 5)[c], :].rearrange("p a n -> p (a n)"),
                                  ALU.add).then_inc(h1_ready, 1)
            dve.wait_ge(late_in, 64)
            for c in range(TC):
                dve.wait_ge(rstd2, c + 1)
                dve.scalar_tensor_tensor(out=xn[:, c, :], in0=h[:, c, :], scalar=rstd[:, c:c + 1], in1=gain_b[:, :],
                                         op0=ALU.mult, op1=ALU.mult).then_inc(xn2_ready, 1)
            for c in range(TC):
                dve.wait_ge(x2T_mm, c + 1)
                dve.tensor_copy(h2T[:, 4:8, P * c:P * c + P], psum[:, (1, 7)[c], :].rearrange("p (a t) -> p a t", a=4)
                                ).then_inc(h2T_out, 1)
            for c in range(TC):
                dve.wait_ge(logit_mm, TC)
                link(dve.tensor_tensor(logit[:, c, :], psum[:, 5, c * E:(c + 1) * E], br_sb[:, :], ALU.add))
                link(dve.max(out=top8[:, c, :], in_=logit[:, c, :]))
                dve.tensor_scalar(negtop[:, c:c + 1], top8[:, c, 0:1], -1.0, None, ALU.mult).then_inc(top_ready, 1)
                fourth = top8[:, c, TOPK - 1:TOPK]
                dve.tensor_scalar(strict[:, c, :], logit[:, c, :], fourth, None, ALU.is_gt)
                link(dve.tensor_scalar(tie[:, c, :], logit[:, c, :], fourth, None, ALU.is_equal))
                dve.tensor_reduce(nstrict[:, c:c + 1], strict[:, c, :], AX, ALU.add)
                link(dve.tensor_tensor_scan(tie_n[:, c, :], restart[:, 1:1 + E], tie[:, c, :], 0.0, ALU.mult, ALU.add))
                link(dve.tensor_scalar(need[:, c:c + 1], nstrict[:, c:c + 1], -1.0, float(TOPK), ALU.mult, ALU.add))
                link(dve.scalar_tensor_tensor(out=tie[:, c, :], in0=tie_n[:, c, :], scalar=need[:, c:c + 1],
                                              in1=tie[:, c, :], op0=ALU.is_le, op1=ALU.mult))
                link(dve.tensor_tensor(chosen[:, c, :], strict[:, c, :], tie[:, c, :], ALU.add))
                dve.tensor_copy(chosen_b[:, c, :], chosen[:, c, :]).then_inc(chosen_ready, 1)
            for c in range(TC):
                dve.wait_ge(gate_exp, c + 1)
                link(dve.tensor_tensor(expo[:, c, :], expo[:, c, :], chosen[:, c, :], ALU.mult))
                link(dve.tensor_reduce(gsum[:, c:c + 1], expo[:, c, :], AX, ALU.add))
                link(dve.reciprocal(ginv[:, c:c + 1], gsum[:, c:c + 1]))
                dve.tensor_scalar(gate_t[:, c, :].rearrange("p (a e) -> p a e", e=E),
                                  expo[:, c, :].unsqueeze(1).to_broadcast([P, PASSES, E]), ginv[:, c:c + 1], None,
                                  ALU.mult).then_inc(gate_ready, 1)
            dve.wait_ge(rank_mm, 1)
            link(dve.tensor_copy(cnt, psum[:, 5, 4 * E:5 * E]))
            link(dve.tensor_reduce(nmax, cnt, AX, ALU.max))
            for b in range(1, PASSES):
                ins = dve.tensor_scalar(over[:, b - 1:b], nmax, float(SLOTS * b), float(E // 2), ALU.is_gt, ALU.mult)
            link(ins)
            link(dve.tensor_reduce(nmax, over, AX, ALU.add))
            dve.tensor_copy(extra_pairs[0:1, :], nmax[0:1, :]).then_inc(count_ready, 1)
            for c in range(TC):
                link(dve.scalar_tensor_tensor(out=tie[:, c, :], in0=psum[:, 5, (2 + c) * E:(3 + c) * E], scalar=1.0,
                                              in1=chosen[:, c, :], op0=ALU.add, op1=ALU.mult))
                for b in range(PASSES):
                    ins = dve.tensor_scalar(rank_t[:, c, b * E:(b + 1) * E], tie[:, c, :], float(-1 - SLOTS * b), None,
                                            ALU.add)
                link(ins)
            for c in range(TC):
                dve.wait_ge(bias2_mm, c + 1)
                dve.tensor_tensor(h[:, c, :], h[:, c, :], psum[:, (6, 1)[c]:(8, 3)[c], :].rearrange("p a n -> p (a n)"),
                                  ALU.add).then_inc(bias2_added, 1)
            dve.wait_ge(bias2_added, 2)

            def select(i, b, reuse=True):
                if reuse:
                    dve.wait_ge(comb_mm, i - 1)
                for c in range(TC):
                    dve.tensor_scalar(pick[:, b, c, :], iota2[:, 0, :], rank_t[:, c, bass.ds(i, 1)], None, ALU.is_equal)
                    dve.tensor_scalar(put[:, b, c, :].rearrange("p (a s) -> p a s", a=2), iota2[:, :, :],
                                      rank_t[:, c, bass.ds(i, 1)], gate_t[:, c, bass.ds(i, 1)], ALU.is_equal, ALU.mult)
                dve.tensor_scalar(which[:, b, :], ones_bf[0:3 * E, 0:SLOTS], expert_id[:, bass.ds(i, 1)], None,
                                  ALU.mult).then_inc(sel_ready, 1)

            def activate(i, reuse=True):
                pairs = psum[:, 3:5, :].rearrange("p a (f two) -> p (a f) two", two=2)
                dve.wait_ge(w1_used, KC * i + KC)
                if reuse:
                    dve.wait_ge(act_ready, i)
                dve.tensor_scalar(glu, pairs[:, :, 0], LIMIT, None, ALU.min).then_inc(glu_ready, 1)
                dve.tensor_scalar(lin, pairs[:, :, 1], -LIMIT, LIMIT, ALU.max, ALU.min).then_inc(lin_ready, 1)
                dve.wait_ge(lin_ready, i + 1)
                dve.wait_ge(glu_ready, i + 1)
                dve.scalar_tensor_tensor(out=lin, in0=lin, scalar=1.0, in1=glu, op0=ALU.add, op1=ALU.mult
                                         ).then_inc(gated, 1)
                dve.wait_ge(gated, i + 1)
                dve.wait_ge(sig_ready, i + 1)
                if reuse:
                    dve.wait_ge(actT_mm, i)
                dve.tensor_tensor(act_r, lin, sig, ALU.mult).then_inc(act_ready, 1)

            def add_up(i, reuse=True):
                for c in range(TC):
                    dve.wait_ge(put_mm, TC * i + c + 1)
                    dve.tensor_tensor(h[:, c, :], h[:, c, :],
                                      psum[:, (6, 1)[c]:(8, 3)[c], :].rearrange("p a n -> p (a n)"), ALU.add
                                      ).then_inc(put_added, 1)
                dve.wait_ge(put_added, TC * i + TC)

            extra = dve.value_load(extra_pairs[0:1, 0:1], min_val=0, max_val=(PASSES - 1) * E // 2)
            pairs = extra + E // 2
            n = extra * 2 + E
            select(0, 0, reuse=False)
            activate(0, reuse=False)
            select(1, 1, reuse=False)
            activate(1)
            with dve.Fori(1, pairs) as j:
                i = j * 2
                for b in range(2):
                    select(i + b, b)
                    add_up(i + b - 2)
                    activate(i + b)
            add_up(n - 2)
            add_up(n - 1)
            dve.wait_ge(finalgain_in, 16)
            for c in range(TC):
                dve.wait_ge(rstd3, c + 1)
                dve.scalar_tensor_tensor(out=xn[:, c, :], in0=h[:, c, :], scalar=rstd[:, c:c + 1], in1=gain_a[:, :],
                                         op0=ALU.mult, op1=ALU.mult).then_inc(final_ready, 1)

        @block.tensor
        def _(pe):
            pe.wait_ge(consts, 1)
            for c in range(TC):
                pe.wait_ge(xn_ready, c + 1)
                for k in range(KC):
                    last = pe.transpose(psum[:, 2 + k // 2, (k % 2) * T + c * P:(k % 2) * T + (c + 1) * P],
                                        xn[:, c, k * P:(k + 1) * P], ident[:, :])
                last.then_inc(xT_done, 1)
            pe.wait_ge(hT_ready, 4)
            pe.wait_ge(wff_in, 64)
            for k in range(KC):
                last = pe.matmul(psum[:, 6, 0:T], wff[:, k, :], hT[:, k, :], start=k == 0, stop=k == KC - 1)
            last.then_inc(ff_done, 1)

            def project(n):
                _, _, transposed = BLOCKS[n]
                w = block_sb(n)
                pe.wait_ge(block_in[n], 16)
                if n >= 2:
                    pe.wait_ge(proj_out, n - 1)
                for half in range(2):
                    for k in range(KC):
                        if transposed:
                            lhs, rhs = w[:, k, half * P:(half + 1) * P], hT[:, k, :]
                        else:
                            lhs, rhs = hT[:, k, half * P:(half + 1) * P], w[:, k, :]
                        last = pe.matmul(psum[:, n % 2, half * T:(half + 1) * T], lhs, rhs, start=k == 0,
                                         stop=k == KC - 1)
                last.then_inc(proj_done, 1)

            def level(n):
                if n < 7:
                    pe.wait_ge(lvl_dec, n + 1)
                if n >= 1:
                    pe.wait_ge(lvl_taken, n)
                for c in range(TC):
                    for hd in range(HG_H):
                        rows = slice(HD * (hd % 2), HD * (hd % 2) + HD)
                        span = slice((hd // 2) * T + c * P, (hd // 2) * T + (c + 1) * P)
                        if n < 7:
                            lhs, rhs = hg_d[rows, n % 2, span], hg_d[rows, n % 2, span]
                        else:
                            lhs, rhs = hg_k[rows, span], gqT[rows, hd // 2, c * P:(c + 1) * P]
                        j = c * 2 + hd // 2
                        last = pe.matmul(psum[:, 3 + hd % 2, j * P:(j + 1) * P], lhs, rhs, start=True, stop=True)
                last.then_inc(lvl_mm, 1)

            def cross():
                pe.wait_ge(lvl_dec, 8)
                pe.wait_ge(lvl_taken, 8)
                for hd in range(HG_H):
                    rows = slice(HD * (hd % 2), HD * (hd % 2) + HD)
                    o = (hd // 2) * T
                    last = pe.matmul(psum[:, 3 + hd % 2, (hd // 2) * P:(hd // 2 + 1) * P], hg_d[rows, 1, o:o + P],
                                     hg_d[rows, 1, o + P:o + T], start=True, stop=True)
                last.then_inc(lvl_mm, 1)

            for n in range(NB):
                project(n)
                if n >= 4:
                    level(n - 4)
            pe.wait_ge(proj_out, NB)
            level(7)
            pe.wait_ge(pooled_ready, 2)
            for g in range(4):
                rows = slice(HD * (g % 2), HD * (g % 2) + HD)
                last = pe.matmul(psum[rows, 7 - g % 2, (g // 2) * T:(g // 2 + 1) * T], poolw_sb[rows, g // 2, :],
                                 win_b[rows, g // 2, :], start=True, stop=True)
            last.then_inc(pool_mm, 1)

            pe.wait_ge(fox_lr, 5)

            def scores(hd):
                rows = slice(HD * (hd % 2), HD * (hd % 2) + HD)
                if hd >= 2:
                    pe.wait_ge(score_max, hd - 1)
                for c in range(TC):
                    o = psum[:, hd % 2, P * c:P * c + P * (c + 1)]
                    pe.matmul(o, qT[rows, hd // 2, c * P:(c + 1) * P], kT[rows, hd // 2, 0:P * (c + 1)], start=True, stop=False)
                    last = pe.matmul(o, fox_l[rows, c * P:(c + 1) * P], fox_r[rows, hd // 2, 0:P * (c + 1)], start=False,
                                     stop=True)
                last.then_inc(score_mm, 1)

            def probT(hd):
                pe.wait_ge(prob_ready, TC * (hd + 1))
                if hd >= 1:
                    pe.wait_ge(probT_ready, hd)
                for j in range(3):
                    last = pe.transpose(psum[:, 2, j * P:(j + 1) * P], fox_p[:, hd % 4, j * P:(j + 1) * P], ident[:, :])
                last.then_inc(probT_mm, 1)

            def weigh(hd):
                pe.wait_ge(probT_ready, hd + 1)
                span = slice(hd * HD, (hd + 1) * HD)
                pe.matmul(psum[:, 5, span], fox_pt[:, hd % 2, 0:P], v_sb[:, 0, span], start=True, stop=True)
                pe.matmul(psum[:, 6, span], fox_pt[:, hd % 2, P:2 * P], v_sb[:, 0, span], start=True, stop=False)
                pe.matmul(psum[:, 6, span], fox_pt[:, hd % 2, 2 * P:3 * P], v_sb[:, 1, span], start=False, stop=True
                          ).then_inc(pv_mm, 1)

            for hd in range(FOX_H + 2):
                if hd < FOX_H:
                    scores(hd)
                if 1 <= hd <= FOX_H:
                    probT(hd - 1)
                if hd == 0:
                    cross()
                if hd == 2:
                    pe.wait_ge(pool_out, 4)
                if hd >= 2:
                    weigh(hd - 2)
                if hd == 3:
                    pe.wait_ge(lvl_taken, 9)
                    for c in range(TC):
                        for g in range(HG_H):
                            o = psum[:, 7, c * T + g * HD:c * T + (g + 1) * HD]
                            pe_last = pe.matmul(o, hg_s[:, (g % 2) * 4 + c * 2 + g // 2, :], gi[:, c, g * HD:(g + 1) * HD],
                                                start=True, stop=c == 0)
                            if c == 1:
                                pe_last = pe.matmul(o, hg_x[:, (g % 2) * 2 + g // 2, :], gi[:, 0, g * HD:(g + 1) * HD],
                                                    start=False, stop=True)
                    pe_last.then_inc(hg_mm, 1)
            pe.wait_ge(hg_ready, 1)
            for a in range(2):
                for c in range(TC):
                    last = pe.transpose(psum[:, 3, a * T + c * P:a * T + (c + 1) * P],
                                        hg_o[:, c * T + a * P:c * T + (a + 1) * P], ident[:, :])
            last.then_inc(hgT_mm, 1)
            pe.wait_ge(fox_ready, 1)
            for a in range(4):
                for c in range(TC):
                    last = pe.transpose(psum[:, a // 2, (a % 2) * T + c * P:(a % 2) * T + (c + 1) * P],
                                        fox_o[:, c, a * P:(a + 1) * P], ident[:, :])
                if a % 2:
                    last.then_inc(foxT_mm, 1)
            for n in range(4):
                pe.wait_ge(wout_in[n], 16)
            pe.wait_ge(hgT_out, 2)
            for c in range(TC):
                for j, k in enumerate((6, 7, 4, 5, 0, 1, 2, 3)):
                    if c == 0 and j == 4:
                        pe.wait_ge(foxT_out, 4)
                    for half in range(2):
                        last = pe.matmul(psum[:, (5, 3)[c] + half, :], oT[:, k, c * P:(c + 1) * P],
                                         w2_ring[:, 0, k, half * 512:(half + 1) * 512], start=j == 0, stop=j == 7)
                last.then_inc(mix_mm, 1)
            for c in range(TC):
                pe.wait_ge(xn2_ready, c + 1)
                for k in range(KC):
                    last = pe.transpose(psum[:, ((0, 1), (2, 7))[c][k // 4], (k % 4) * P:(k % 4 + 1) * P],
                                        xn[:, c, k * P:(k + 1) * P], ident[:, :])
                last.then_inc(x2T_mm, 1)
            pe.wait_ge(h2T_out, 4)
            for c in range(TC):
                for k in range(KC):
                    last = pe.matmul(psum[:, 5, c * E:(c + 1) * E], h2T[:, k, c * P:(c + 1) * P], wr_sb[:, k, :],
                                     start=k == 0, stop=k == KC - 1)
                last.then_inc(logit_mm, 1)
            pe.wait_ge(chosen_ready, 2)
            pe.matmul(psum[:, 5, 2 * E:3 * E], before[:, :], chosen_b[:, 0, :], start=True, stop=True)
            pe.matmul(psum[:, 5, 3 * E:4 * E], ones_bf[:, :], chosen_b[:, 0, :], start=True, stop=False)
            pe.matmul(psum[:, 5, 3 * E:4 * E], before[:, :], chosen_b[:, 1, :], start=False, stop=True)
            pe.matmul(psum[:, 5, 4 * E:5 * E], ones_bf[:, :], chosen_b[:, 0, :], start=True, stop=False)
            pe.matmul(psum[:, 5, 4 * E:5 * E], ones_bf[:, :], chosen_b[:, 1, :], start=False, stop=True
                      ).then_inc(rank_mm, 1)
            pe.wait_ge(gate_ready, 2)
            for c in range(TC):
                last = pe.transpose(psum[:, 3, c * P:(c + 1) * P], gate_t[:, c, :], ident[:, :])
            last.then_inc(gateT_mm, 1)
            pe.wait_ge(gateT_out, 1)
            for c in range(TC):
                for half in range(2):
                    last = pe.matmul(psum[:, (6, 1)[c] + half, :], gateT[:, c * P:(c + 1) * P],
                                     b2_sb[:, half * 512:(half + 1) * 512], start=True, stop=True)
                last.then_inc(bias2_mm, 1)

            def gather(i, b):
                pe.wait_ge(sel_ready, i + 1)
                for k in range(KC):
                    for c in range(TC):
                        last = pe.matmul(psum[:, 0, k * SLOTS:(k + 1) * SLOTS], xn[:, c, k * P:(k + 1) * P],
                                         pick[:, b, c, :], start=c == 0, stop=c == TC - 1)
                last.then_inc(gather_mm, 1)

            def transpose_act(i, b, reuse=True):
                pe.wait_ge(act_ready, i + 1)
                if reuse:
                    pe.wait_ge(put_added, TC * i)
                for j in range(4):
                    last = pe.transpose(psum[:, 1, j * P:(j + 1) * P], act_r[:, j * P:(j + 1) * P], ident[:, :])
                last.then_inc(actT_mm, 1)
                for c in range(TC):
                    last = pe.transpose(psum[:, 2, c * P:(c + 1) * P], put[:, b, c, :], ident[:, :])
                last.then_inc(comb_mm, 1)

            def up(i, b, reuse=True):
                if reuse:
                    pe.wait_ge(lin_ready, i)
                for q in range(2):
                    for g in range(2):
                        pe.matmul(psum[g * SLOTS:(g + 1) * SLOTS, 3 + q, :], which[:, b, :],
                                  b1_parts[:, g * F + q * 512:g * F + (q + 1) * 512], start=True, stop=False)
                pe.wait_ge(xe_ready, i + 1)
                for k in range(KC):
                    pe.wait_ge(w1_in[k], 16 * i + 16)
                    for q in range(2):
                        for g in range(2):
                            last = pe.matmul(psum[g * SLOTS:(g + 1) * SLOTS, 3 + q, :], xe[:, k, :],
                                             w1_ring[:, k, g * F + q * 512:g * F + (q + 1) * 512], start=False,
                                             stop=k == KC - 1)
                    last.then_inc(w1_used, 1)

            def down(i, b, loaded, reuse=True):
                pe.wait_ge(actT_ready, i + 1)
                if reuse:
                    pe.wait_ge(y_ready, i)
                for k in range(KC):
                    if k % 2 == 0:
                        pe.wait_ge(w2_in[b][k // 2], loaded)
                    for g in range(2):
                        last = pe.matmul(psum[g * SLOTS:(g + 1) * SLOTS, 5, :],
                                         actT[:, k % 4, (k // 4) * SLOTS:(k // 4 + 1) * SLOTS],
                                         w2_ring[:, b, k, g * 512:(g + 1) * 512], start=k == 0, stop=k == KC - 1)
                    if k % 2:
                        last.then_inc(w2_used, 1)

            def combine(i, reuse=True):
                pe.wait_ge(y_ready, i + 1)
                pe.wait_ge(comb_ready, i + 1)
                for c in range(TC):
                    if c == 0 and reuse:
                        pe.wait_ge(put_added, TC * i - 1)
                    for g in range(2):
                        last = pe.matmul(psum[:, (6, 1)[c] + g, :], comb[g * SLOTS:(g + 1) * SLOTS, c, :],
                                         y_sb[g * SLOTS:(g + 1) * SLOTS, :], start=True, stop=True)
                    last.then_inc(put_mm, 1)

            def item(i, b, loaded):
                gather(i, b)
                transpose_act(i - 1, 1 - b)
                up(i, b)
                down(i - 1, 1 - b, loaded)
                combine(i - 1)

            pe.wait_ge(count_ready, 1)
            extra = pe.value_load(extra_pairs[0:1, 0:1], min_val=0, max_val=(PASSES - 1) * E // 2)
            pairs = extra + E // 2
            n = extra * 2 + E
            gather(0, 0)
            up(0, 0, reuse=False)
            gather(1, 1)
            pe.wait_ge(bias2_added, 2)
            transpose_act(0, 0, reuse=False)
            up(1, 1)
            down(0, 0, 16, reuse=False)
            combine(0, reuse=False)
            with pe.Fori(1, pairs) as j:
                i = j * 2
                item(i, 0, 8 * i)
                item(i + 1, 1, 8 * i + 16)
            transpose_act(n - 1, 1)
            down(n - 1, 1, 8 * n)
            combine(n - 1)


_INS = ["x", "norm_mix", "w_in", "b_fox_f", "fox_gain", "hgrn_lb", "hgrn_gain", "pool_w", "pool_scale", "w_out",
        "norm_moe", "w_router", "b_router", "w1", "b1", "w2", "b2", "norm_final"]


def kernel(**inputs):
    import numpy as _np
    import concourse.bacc as _bacc
    from concourse import mybir as _mybir
    from concourse.bass_utils import run_bass_kernel_spmd as _run

    nc = _bacc.Bacc("TRN2", target_bir_lowering=False, num_devices=1)
    arrays, args = {}, []
    for name in _INS:
        a = _np.ascontiguousarray(inputs[name])
        arrays[f"in_{name}_dram"] = a
        args.append(nc.dram_tensor(f"in_{name}_dram", a.shape, _mybir.dt.from_np(a.dtype), kind="ExternalInput").ap())
    args.append(nc.dram_tensor("out_0_dram", (1, T, D), _mybir.dt.float32, kind="ExternalOutput").ap())
    build(nc, *args)
    r = _run(nc, [arrays], core_ids=[0])
    return r.results[0]["out_0_dram"]
```

```python
from contextlib import ExitStack

import concourse.bass as bass
from concourse import mybir

F32 = mybir.dt.float32
BF16 = mybir.dt.bfloat16
I16 = mybir.dt.int16
I32 = mybir.dt.int32
ALU = mybir.AluOpType
ACT = mybir.ActivationFunctionType
AX = mybir.AxisListType.X

P = 128
D = 1024
T = 256
TC = T // P
KC = D // P
FOX_H, HG_H, HD = 8, 4, 64
CHUNK = 64
WINDOWS = (2, 4, 8, 16)
E, TOPK, F = 32, 4, 1024
LIMIT, ALPHA = 7.0, 1.702
EPS = 1e-5
SLOTS = 64
PASSES = T // SLOTS
NEG = -1e30

BLOCKS = [("gf", 1800, True), ("gq", 1544, True), ("fk0", 512, True), ("fq0", 0, True), ("fv0", 1024, False),
          ("pu", 2568, True), ("fk1", 768, True), ("fq1", 256, True), ("fv1", 1280, False), ("gi", 2056, False),
          ("gg", 2312, False)]
FF_COL = 1536
BN = 256
NB = len(BLOCKS)
SLOT_LEVEL = {6: 0, 7: 1, 9: 2, 11: 3, 12: 4, 13: 5, 14: 6, 15: 7, 16: 8}
SLOT_HEAD = {8: 0, 9: 1, 10: 2, 11: 3, 16: 4, 17: 5, 18: 6, 19: 7}
NSLOT = 2 * NB
SLOT_DIV0 = 14
SLOT_VAR0 = 15
SLOT_NORM0 = 17
SLOT_POOL = 18
SLOT_HG_OUT = 20
LEVELS = (64, 32, 16, 8, 4, 2, 1, 0)
NL = len(LEVELS)


def build(nc, x, norm_mix, w_in, b_fox_f, fox_gain, hgrn_lb, hgrn_gain, pool_w, pool_scale, w_out,
          norm_moe, w_router, b_router, w1, b1, w2, b2, norm_final, out):
    with ExitStack() as ctx:
        def sb(name, shape, dt=F32):
            return ctx.enter_context(nc.sbuf_tensor(name, shape, dt))

        def sem(name):
            return ctx.enter_context(nc.semaphore(name))

        w1_ring = sb("w1_ring", [P, KC, 2 * F])
        w2_ring = sb("w2_ring", [P, 2, KC, D])
        h = sb("h", [P, TC, D])
        xn = sb("xn", [P, TC, D])
        gain_a = sb("gain_a", [P, D])
        gain_b = sb("gain_b", [P, D])
        arena = sb("arena", [P, 8960])
        ident = sb("ident", [P, P])
        iota2 = sb("iota2", [P, 2, SLOTS])
        b1_parts = sb("b1_parts", [3 * E, 2 * F], BF16)
        b2_sb = sb("b2_sb", [E, D])
        wr_sb = sb("wr_sb", [P, KC, E])
        wff = sb("wff", [P, KC, P])
        before = sb("before", [P, P], BF16)
        ones_bf = sb("ones_bf", [P, P], BF16)
        lvl_mask = sb("lvl_mask", [P, NL, P], BF16)
        causal = sb("causal", [P, 2 * P])
        restart = sb("restart", [P, 2 * T], BF16)
        poolw_sb = sb("poolw_sb", [P, 2, HD])
        mix_gain = sb("mix_gain", [P, KC])
        br_sb = sb("br_sb", [P, E])
        small = sb("small", [P, 256])
        expert_id = sb("expert_id", [3 * E, PASSES * E], BF16)
        extra_pairs = sb("extra_pairs", [1, 1], I32)
        psum = ctx.enter_context(nc.psum_tensor("psum", [P, 8, 512], F32))

        at = [0]

        def take(*shape, start=None):
            if start is not None:
                at[0] = start
            n = 1
            for s in shape:
                n *= s
            v = arena[:, at[0]:at[0] + n]
            at[0] += n
            assert at[0] <= 8960
            if len(shape) == 2:
                v = v.rearrange("p (a b) -> p a b", a=shape[0])
            if len(shape) == 3:
                v = v.rearrange("p (a b c) -> p a b c", a=shape[0], b=shape[1])
            return v

        hT = take(KC, T)
        qT = take(4, T)
        kT = take(4, T)
        v_sb = take(TC, 512)
        gfT = take(2, T)
        gqT = take(2, T)
        gi = take(TC, T)
        gg = take(TC, T)
        puT = take(2, T)
        fox_r = take(4, T)
        fox_l = take(1, T)[:, 0, :]
        scratch = w2_ring[:, 0, :, :].rearrange("p k n -> p (k n)")
        hg_a = scratch[:, 0:512]
        hg_k = scratch[:, 512:1024]
        hg_e = scratch[:, 1024:2048].rearrange("p (a b) -> p a b", a=2)
        hg_d = scratch[:, 2048:3072].rearrange("p (a b) -> p a b", a=2)
        hg_s = scratch[:, 3072:4096].rearrange("p (a b) -> p a b", a=8)
        hg_x = scratch[:, 4096:4608].rearrange("p (a b) -> p a b", a=4)
        hg_x_rows = scratch[:, 4096:4608].rearrange("p (a b) -> p a b", a=2)
        fox_pt = scratch[:, 4608:5376].rearrange("p (a b) -> p a b", a=2)
        hg_t = scratch[:, 5376:5888]
        ff_t = scratch[:, 5888:6144]
        win_a = scratch[:, 6144:6656].rearrange("p (a b) -> p a b", a=2)
        win_b = scratch[:, 6656:7168].rearrange("p (a b) -> p a b", a=2)
        win_inv = scratch[:, 7168:7680].rearrange("p (a b) -> p a b", a=2)
        hg_o = scratch[:, 7680:8192]
        b1_tmp = scratch[0:3 * E, 6144:8192]
        ones_row = scratch[0:1, 1024:1280]
        ffb_row = scratch[0:1, 1280:1408]
        ffb_in_row = scratch[0:1, 1408:1416]
        wff_cols = scratch[:, 1536:1600].rearrange("p (k h) -> p k h", k=KC)
        xflat = xn[:, :, :].rearrange("p c n -> p (c n)")
        fox_p = xflat[:, 0:768].rearrange("p (a b) -> p a b", a=2)
        fox_o = xflat[:, 768:1792].rearrange("p (g n) -> p g n", g=2)
        fox_sq = (gfT.rearrange("p a t -> p (a t)"), hT[:, 0:2, :].rearrange("p a t -> p (a t)"))
        oT = {0: qT[:, 0:2, :], 2: puT, 4: kT[:, 0:2, :], 6: gfT}
        h2T = take(KC, T, start=0)
        xe = take(KC, SLOTS)
        put = take(2, TC, P)
        pick = take(2, TC, SLOTS)
        comb = take(TC, P)
        glu = take(512)
        lin = take(512)
        sig = take(512)
        act_r = take(512)
        actT = take(4, P)
        y_sb = take(512)
        rank_t = take(TC, PASSES * E)
        gate_t = take(TC, PASSES * E)
        which = take(SLOTS).bitcast(BF16).rearrange("p (a b) -> p a b", a=2)[0:3 * E]
        gateT = take(T)[0:E]
        logit = take(TC, E)
        strict = take(TC, E)
        tie = take(TC, E)
        tie_n = take(TC, E)
        chosen = take(TC, E)
        expo = take(TC, E)
        chosen_b = take(TC * E // 2).bitcast(BF16).rearrange("p (c e) -> p c e", c=TC)
        cnt = take(E)

        def row_of(hd, c):
            return (hd // 4) * 8 + c * 4 + hd % 4

        col = [0]

        def cols(n):
            col[0] += n
            return small[:, col[0] - n:col[0]]

        ss, ms, rstd = cols(TC), cols(TC), cols(TC)
        neg_half = cols(16)
        ffb = cols(1)
        l_scale, l_shift = cols(1), cols(1)
        r_neg, r_one = cols(4), cols(4)
        rowsum, rowinv = cols(16), cols(16)
        fox_ms, fox_r2 = cols(16), cols(16)
        hg_ms, hg_r2 = cols(8), cols(8)
        negmax = cols(16)
        lbraw, lbe, lbp, lb, one_lb = cols(2), cols(2), cols(2), cols(2), cols(2)
        ref2 = cols(2)
        top8 = cols(16).rearrange("p (c k) -> p c k", c=TC)
        nstrict, need, negtop, gsum, ginv = cols(2), cols(2), cols(2), cols(2), cols(2)
        nmax, over = cols(1), cols(3)

        x_in = [sem(f"x_in{c}") for c in range(TC)]
        mixgain_in, small_in = sem("mixgain_in"), sem("small_in")
        ff_in, b1_in, late_in = sem("ff_in"), sem("b1_in"), sem("late_in")
        block_in = [sem(f"block_in{n}") for n in range(NB)]
        wout_in = [sem(f"wout_in{n}") for n in range(4)]
        w1_in = [sem(f"w1_in{k}") for k in range(KC)]
        w2_in = [[sem(f"w2_in{b}_{k}") for k in range(4)] for b in range(2)]
        finalgain_in, out_done = sem("finalgain_in"), sem("out_done")
        pool_chain, dve_chain, act_chain = sem("pool_chain"), sem("dve_chain"), sem("act_chain")
        ident_ready, consts, wff_ready, b1_part, b1_rest = (sem("ident_ready"), sem("consts"), sem("wff_ready"),
                                                           sem("b1_part"), sem("b1_rest"))
        masks_ready = sem("masks_ready")
        sumsq, rstd_ready, xn_ready, xT_done, hT_ready = (sem("sumsq"), sem("rstd_ready"), sem("xn_ready"),
                                                          sem("xT_done"), sem("hT_ready"))
        ff_done, ff_z, ff_ln, fox_lr = sem("ff_done"), sem("ff_z"), sem("ff_ln"), sem("fox_lr")
        proj_done, proj_out = sem("proj_done"), sem("proj_out")
        hg_ln, hg_karg, hg_kexp, hg_targ, hg_tln = (sem("hg_ln"), sem("hg_karg"),
                                                          sem("hg_kexp"), sem("hg_targ"), sem("hg_tln"))
        lvl_arg, lvl_exp, lvl_dec, lvl_mm, lvl_taken = (sem("lvl_arg"), sem("lvl_exp"), sem("lvl_dec"),
                                                        sem("lvl_mm"), sem("lvl_taken"))
        pooled_ready, pool_mm, pool_out = sem("pooled_ready"), sem("pool_mm"), sem("pool_out")
        score_mm, score_max, prob_ready, probT_mm, probT_ready, pv_mm = (
            sem("score_mm"), sem("score_max"), sem("prob_ready"), sem("probT_mm"), sem("probT_ready"), sem("pv_mm"))
        hg_mm, hg_copied, hg_sq, hg_var, hg_rstd = (sem("hg_mm"), sem("hg_copied"), sem("hg_sq"),
                                                  sem("hg_var"), sem("hg_rstd"))
        silu_exp, hg_ready, hgT_mm, hgT_out = sem("silu_exp"), sem("hg_ready"), sem("hgT_mm"), sem("hgT_out")
        fox_div, fox_sqd, fox_var, fox_rstd, fox_ready, foxT_mm, foxT_out = (
            sem("fox_div"), sem("fox_sqd"), sem("fox_var"), sem("fox_rstd"), sem("fox_ready"), sem("foxT_mm"),
            sem("foxT_out"))
        mix_mm, h1_ready, sumsq2, rstd2, xn2_ready, x2T_mm, h2T_out = (
            sem("mix_mm"), sem("h1_ready"), sem("sumsq2"), sem("rstd2"), sem("xn2_ready"), sem("x2T_mm"),
            sem("h2T_out"))
        logit_mm, top_ready, gate_exp, chosen_ready, rank_mm, count_ready = (
            sem("logit_mm"), sem("top_ready"), sem("gate_exp"), sem("chosen_ready"), sem("rank_mm"),
            sem("count_ready"))
        gate_ready, gateT_mm, gateT_out, bias2_mm, bias2_added = (
            sem("gate_ready"), sem("gateT_mm"), sem("gateT_out"), sem("bias2_mm"), sem("bias2_added"))
        sel_ready, gather_mm, xe_ready, actT_mm, actT_ready, comb_mm, comb_ready = (
            sem("sel_ready"), sem("gather_mm"), sem("xe_ready"), sem("actT_mm"), sem("actT_ready"),
            sem("comb_mm"), sem("comb_ready"))
        glu_ready, lin_ready, sig_ready, gated, act_ready = (
            sem("glu_ready"), sem("lin_ready"), sem("sig_ready"), sem("gated"), sem("act_ready"))
        y_ready, put_mm, put_added = sem("y_ready"), sem("put_mm"), sem("put_added")
        w1_used, w2_used = sem("w1_used"), sem("w2_used")
        sumsq3, rstd3, final_ready = sem("sumsq3"), sem("rstd3"), sem("final_ready")

        x_v = x[0].rearrange("(c p) n -> p c n", p=P)
        out_v = out[0].rearrange("(c p) n -> p c n", p=P)
        w_in_v = w_in[0].rearrange("(k p) n -> p k n", p=P)
        w_out_v = w_out[0].rearrange("(k p) n -> p k n", p=P)
        w1_v = w1[0].rearrange("e (k p) n -> e p k n", p=P)
        w2_v = w2[0].rearrange("e (k p) n -> e p k n", p=P)

        def block_sb(n):
            if n < 3:
                return w2_ring[:, 1, 2 * n:2 * n + 2, :].rearrange("p a (b n) -> p (a b) n", n=BN)
            return w1_ring[:, n - 3, :].rearrange("p (k n) -> p k n", n=BN)

        block = ctx.enter_context(nc.Block())

        @block.sync
        def _(sp):
            for c in range(TC):
                sp.dma_start(h[:, c, :], x_v[:, c, :]).then_inc(x_in[c], 16)
            for n, (_, c0, _) in enumerate(BLOCKS):
                sp.dma_start(block_sb(n), w_in_v[:, :, c0:c0 + BN]).then_inc(block_in[n], 16)
                if n == 0:
                    for part in range(3):
                        sp.dma_start(b1_tmp[E * part:E * part + E, :], b1[0]).then_inc(b1_in, 16)
            sp.wait_ge(proj_done, 3)
            for n in range(4):
                sp.dma_start(w2_ring[:, 1, 2 * n:2 * n + 2, :], w_out_v[:, 2 * n:2 * n + 2, :]).then_inc(wout_in[n], 16)
            for k in range(KC):
                sp.wait_ge(proj_done, 4 + k)
                sp.dma_start(w1_ring[:, k, :], w1_v[0, :, k, :]).then_inc(w1_in[k], 16)
            sp.wait_ge(hgT_mm, 1)
            sp.wait_ge(pv_mm, FOX_H)
            for k in range(4):
                sp.dma_start(w2_ring[:, 0, 2 * k:2 * k + 2, :], w2_v[0, :, 2 * k:2 * k + 2, :]).then_inc(w2_in[0][k], 16)
            sp.wait_ge(mix_mm, TC)
            for k in range(4):
                sp.dma_start(w2_ring[:, 1, 2 * k:2 * k + 2, :], w2_v[1, :, 2 * k:2 * k + 2, :]).then_inc(w2_in[1][k], 16)

            def load_w1(i):
                e = i % E
                for k in range(KC):
                    sp.wait_ge(w1_used, KC * (i - 1) + k + 1)
                    sp.dma_start(w1_ring[:, k, :], w1_v[bass.ds(e, 1), :, k, :].rearrange("e p n -> (e p) n")
                                 ).then_inc(w1_in[k], 16)

            def load_w2(i, b):
                e = i % E
                for k in range(4):
                    sp.wait_ge(w2_used, 4 * (i - 2) + k + 1)
                    sp.dma_start(w2_ring[:, b, 2 * k:2 * k + 2, :],
                                 w2_v[bass.ds(e, 1), :, 2 * k:2 * k + 2, :].rearrange("e p k n -> (e p) k n")
                                 ).then_inc(w2_in[b][k], 16)

            load_w1(1)
            sp.wait_ge(count_ready, 1)
            extra = sp.value_load(extra_pairs[0:1, 0:1], min_val=0, max_val=(PASSES - 1) * E // 2)
            pairs = extra + E // 2
            n = extra * 2 + E
            with sp.Fori(1, pairs) as j:
                i = j * 2
                load_w1(i)
                load_w2(i, 0)
                load_w1(i + 1)
                load_w2(i + 1, 1)
            for c in range(TC):
                sp.wait_ge(final_ready, c + 1)
                sp.dma_start(out_v[:, c, :], xn[:, c, :]).then_inc(out_done, 16)
            sp.wait_ge(out_done, 16 * TC)

        @block.gpsimd
        def _(pool):
            done = [0]

            def link(ins):
                done[0] += 1
                ins.then_inc(pool_chain, 1)
                pool.wait_ge(pool_chain, done[0])

            def band(v, op_base, pattern, mult, op=ALU.is_ge):
                link(pool.affine_select(out=v, in_=v, pattern=pattern, compare_op=op, fill=0.0, base=op_base,
                                        channel_multiplier=mult))

            link(pool.memset(neg_half, -0.5))
            link(pool.memset(ident[:, :], 0.0))
            pool.affine_select(out=ident[:, :], in_=ident[:, :], compare_op=ALU.not_equal, fill=1.0, base=0,
                               pattern=[[-1, P]], channel_multiplier=1).then_inc(ident_ready, 1)
            pool.wait_ge(ident_ready, 1)
            for c in range(TC):
                pool.wait_ge(sumsq, c + 1)
                link(pool.tensor_scalar(ms[:, c:c + 1], ss[:, c:c + 1], 1.0 / D, EPS, ALU.mult, ALU.add))
                pool.tensor_tensor(rstd[:, c:c + 1], ms[:, c:c + 1], neg_half[:, 0:1], ALU.pow).then_inc(rstd_ready, 1)
                pool.wait_ge(rstd_ready, c + 1)
            link(pool.memset(l_scale, 0.0))
            link(pool.memset(l_shift, 0.0))
            link(pool.memset(r_neg, 0.0))
            link(pool.memset(r_one, 0.0))
            for q in range(4):
                rows = slice(32 * q, 32 * q + 32)
                link(pool.memset((l_scale if q % 2 == 0 else l_shift)[rows], 1.0))
                target = (r_one if q % 2 == 0 else r_neg)[rows]
                link(pool.memset(target, 1.0 if q % 2 == 0 else -1.0))
                band(target, -(q // 2), [[-2, 4]], 1, ALU.is_equal)
            link(pool.memset(restart[:, :], 1.0))
            link(pool.affine_select(out=restart[:, :].rearrange("p (a b) -> p a b", b=CHUNK),
                                    in_=restart[:, :].rearrange("p (a b) -> p a b", b=CHUNK),
                                    compare_op=ALU.not_equal, fill=0.0, base=0, pattern=[[0, 2 * T // CHUNK], [1, CHUNK]],
                                    channel_multiplier=0))
            pool.memset(lvl_mask[:, :, :], 0.0).then_inc(consts, 1)
            pool.wait_ge(consts, 1)
            for n, half in enumerate(LEVELS):
                if half == 0:
                    link(pool.memset(lvl_mask[:, n, :], 1.0))
                    band(lvl_mask[:, n, :], 0, [[-1, P]], 1, ALU.is_equal)
                    continue
                nb = P // (2 * half)
                v = lvl_mask[:, n, :].rearrange("p (a b) -> p a b", b=2 * half)[:, :, half:2 * half]
                link(pool.memset(v, 1.0))
                band(v, 0, [[-2 * half, nb], [0, half]], 1)
                band(v, half - 1, [[2 * half, nb], [0, half]], -1)
            link(pool.memset(causal[:, :], 0.0))
            link(pool.affine_select(out=causal[:, P:], in_=causal[:, P:], compare_op=ALU.is_ge, fill=NEG, base=0,
                                    pattern=[[-1, P]], channel_multiplier=1))
            pool.memset(hg_s, 0.0).then_inc(masks_ready, 1)
            link(pool.memset(ones_bf[:, :], 1.0))
            link(pool.memset(before[:, :], 1.0))
            band(before[:, :], -1, [[1, P]], -1)
            link(pool.iota(iota2[:, :, :], pattern=[[0, 2], [1, SLOTS]], base=0, channel_multiplier=0,
                           allow_small_or_imprecise_dtypes=True))
            link(pool.memset(expert_id[:, :], 1.0))
            for r in range(3):
                v = expert_id[E * r:E * r + E, :].rearrange("p (a e) -> p a e", e=E)
                band(v, 0, [[0, PASSES], [-1, E]], 1, ALU.is_equal)
            pool.wait_ge(b1_part, 4)
            link(pool.iota(win_inv, pattern=[[0, 2], [1, T]], base=1, channel_multiplier=0,
                           allow_small_or_imprecise_dtypes=True))
            for g, w in enumerate(WINDOWS):
                rows = slice(HD * (g % 2), HD * (g % 2) + HD)
                ins = pool.memset(win_inv[rows, g // 2, w:T], float(w))
                if g < 3:
                    link(ins)
            ins.then_inc(consts, 1)
            pool.wait_ge(consts, 2)
            pool.wait_ge(proj_out, 6)
            pool.wait_ge(pooled_ready, 1)
            src = puT
            for step, w in enumerate(WINDOWS):
                sh = w // 2
                dst = (win_a, win_b)[step % 2]
                if step >= 1:
                    link(pool.tensor_copy(dst[:, :, :], src[:, :, :]))
                for g in range(step, 4):
                    rows = slice(HD * (g % 2), HD * (g % 2) + HD)
                    link(pool.tensor_tensor(dst[rows, g // 2, sh:T], src[rows, g // 2, sh:T],
                                            src[rows, g // 2, 0:T - sh], ALU.add))
                    if step == 0:
                        link(pool.tensor_copy(dst[rows, g // 2, 0:sh], src[rows, g // 2, 0:sh]))
                src = dst
            link(pool.tensor_tensor(win_a, src, win_inv, ALU.mult))
            pool.tensor_tensor(win_b, win_a, puT, ALU.subtract).then_inc(pooled_ready, 1)
            pool.wait_ge(pooled_ready, 2)
            pool.wait_ge(fox_var, 1)
            pool.tensor_tensor(fox_r2[:, 0:8], fox_ms[:, 0:8], neg_half[:, 0:8], ALU.pow).then_inc(fox_rstd, 1)
            pool.wait_ge(fox_rstd, 1)
            pool.wait_ge(hg_var, 1)
            pool.tensor_tensor(hg_r2, hg_ms, neg_half[:, 0:8], ALU.pow).then_inc(hg_rstd, 1)
            pool.wait_ge(hg_rstd, 1)
            pool.wait_ge(fox_var, 2)
            pool.tensor_tensor(fox_r2[:, 8:16], fox_ms[:, 8:16], neg_half[:, 0:8], ALU.pow).then_inc(fox_rstd, 1)
            pool.wait_ge(fox_rstd, 2)
            for got, give in ((sumsq2, rstd2), (sumsq3, rstd3)):
                for c in range(TC):
                    pool.wait_ge(got, c + 1)
                    link(pool.tensor_scalar(ms[:, c:c + 1], ss[:, c:c + 1], 1.0 / D, EPS, ALU.mult, ALU.add))
                    pool.tensor_tensor(rstd[:, c:c + 1], ms[:, c:c + 1], neg_half[:, 0:1], ALU.pow).then_inc(give, 1)
                    pool.wait_ge(give, c + 1)

        @block.scalar
        def _(act):
            done = [0]

            def link(ins):
                done[0] += 1
                ins.then_inc(act_chain, 1)
                act.wait_ge(act_chain, done[0])

            act.dma_start(gain_a[:, :], norm_mix[0].partition_broadcast(P)).then_inc(mixgain_in, 16)
            act.dma_start(wff_cols, w_in_v[:, :, FF_COL:FF_COL + FOX_H]).then_inc(ff_in, 16)
            act.dma_start(ffb_in_row, b_fox_f).then_inc(ff_in, 16)
            for c in range(TC):
                act.wait_ge(x_in[c], 16)
                act.activation(xn[:, c, :], h[:, c, :], ACT.Square, accum_out=ss[:, c:c + 1]).then_inc(sumsq, 1)
            act.dma_start(lbraw, hgrn_lb[0].rearrange("(c p) -> p c", p=P), allow_slow_non_contiguous=True).then_inc(small_in, 16)
            act.wait_ge(xT_done, TC)
            for b in range(2):
                act.activation(hT[:, 2 * b:2 * b + 2, :], psum[:, 2 + b, :].rearrange("p (a t) -> p a t", a=2),
                               ACT.Copy).then_inc(hT_ready, 1)
            act.wait_ge(b1_in, 48)
            act.activation(b1_parts[:, :], b1_tmp, ACT.Copy).then_inc(b1_part, 1)
            act.wait_ge(ff_z, 1)
            link(act.activation(ff_t, fox_l, ACT.Abs))
            link(act.activation(ff_t, ff_t, ACT.Exp, scale=-1.0))
            act.activation(ff_t, ff_t, ACT.Ln, bias=1.0).then_inc(ff_ln, 1)
            act.wait_ge(b1_rest, 1)
            for part in (1, 2):
                act.activation(b1_parts[E * part:E * part + E, :], b1_tmp[E * part:E * part + E, :], ACT.Copy
                               ).then_inc(b1_part, 1)
            act.dma_start(gain_a[:, :], norm_final.partition_broadcast(P)).then_inc(finalgain_in, 16)
            act.dma_start(mix_gain[:, 0:4], fox_gain[0].rearrange("(c p) -> p c", p=P), allow_slow_non_contiguous=True).then_inc(small_in, 16)
            act.dma_start(mix_gain[:, 4:6], hgrn_gain[0].rearrange("(c p) -> p c", p=P), allow_slow_non_contiguous=True).then_inc(small_in, 16)
            act.dma_start(mix_gain[:, 6:8], pool_scale[0].rearrange("(c p) -> p c", p=P), allow_slow_non_contiguous=True).then_inc(small_in, 16)
            for a in range(2):
                act.dma_start(poolw_sb[:, a, :], pool_w[0, 2 * a:2 * a + 2].rearrange("g c d -> (g c) d")).then_inc(small_in, 16)

            where = {"gf": gfT, "gq": gqT, "gi": gi, "pu": puT, "gg": gg, "fk0": kT[:, 0:2, :], "fk1": kT[:, 2:4, :],
                     "fq0": qT[:, 0:2, :], "fq1": qT[:, 2:4, :], "fv0": v_sb[:, :, 0:BN], "fv1": v_sb[:, :, BN:2 * BN]}

            def take_block(n):
                name = BLOCKS[n][0]
                act.wait_ge(proj_done, n + 1)
                act.activation(where[name], psum[:, n % 2, :].rearrange("p (a t) -> p a t", a=2), ACT.Copy,
                               scale=HD ** -0.5 if name in ("fq0", "fq1") else 1.0).then_inc(proj_out, 1)

            def level_exp(n):
                act.wait_ge(lvl_arg, n + 1)
                act.activation(hg_e[:, n % 2, :], hg_e[:, n % 2, :], ACT.Exp).then_inc(lvl_exp, 1)

            def head_exp(hd):
                act.wait_ge(score_max, hd + 1)
                for c in range(TC):
                    v = fox_p[:, hd % 2, P * c:P * c + P * (c + 1)]
                    g = row_of(hd, c)
                    act.activation(v, v, ACT.Exp, bias=negmax[:, g:g + 1],
                                   accum_out=rowsum[:, g:g + 1]).then_inc(prob_ready, 1)

            def scaled_out(first, bank, signal):
                for a in range(2):
                    act.activation(oT[first][:, a, :], psum[:, bank, a * T:(a + 1) * T], ACT.Copy,
                                   scale=mix_gain[:, first + a:first + a + 1]).then_inc(signal, 1)

            for s in range(NSLOT):
                nxt = SLOT_LEVEL.get(s + 1)
                if nxt is not None and nxt != 7:
                    level_exp(min(nxt, 7))
                if s % 2 == 1:
                    take_block(s // 2)
                if s == 1:
                    act.wait_ge(proj_out, 1)
                    link(act.activation(hg_t, gfT.rearrange("p a t -> p (a t)"), ACT.Abs))
                    link(act.activation(hg_t, hg_t, ACT.Exp, scale=-1.0))
                    act.activation(hg_t, hg_t, ACT.Ln, bias=1.0).then_inc(hg_ln, 1)
                    act.wait_ge(hg_karg, 1)
                    act.activation(hg_k, hg_k, ACT.Exp).then_inc(hg_kexp, 1)
                    act.wait_ge(hg_targ, 1)
                    act.activation(hg_t, hg_t, ACT.Exp).then_inc(hg_tln, 1)
                    act.wait_ge(hg_targ, 2)
                    act.activation(hg_t, hg_t, ACT.Ln).then_inc(hg_tln, 1)
                if s in SLOT_HEAD:
                    head_exp(SLOT_HEAD[s])
                if s == 5:
                    act.dma_start(gain_b[:, :], norm_moe[0].partition_broadcast(P)).then_inc(late_in, 16)
                    act.dma_start(wr_sb[:, :, :], w_router[0].rearrange("(k p) e -> p k e", p=P)).then_inc(late_in, 16)
                    act.dma_start(br_sb[:, :], b_router[0].partition_broadcast(P)).then_inc(late_in, 16)
                    act.dma_start(b2_sb[:, :], b2[0]).then_inc(late_in, 16)
                if s == SLOT_DIV0:
                    act.wait_ge(fox_div, 1)
                    act.activation(fox_sq[0], fox_o[:, 0, :], ACT.Square).then_inc(fox_sqd, 1)
                if s == SLOT_POOL:
                    act.wait_ge(pool_mm, 1)
                    act.wait_ge(small_in, 96)
                    for g in range(2):
                        for a in range(2):
                            rows = slice(HD * g, HD * g + HD)
                            act.activation(oT[6][rows, a, :], psum[rows, 4 - g, a * T:(a + 1) * T], ACT.Copy,
                                           scale=mix_gain[rows, 6 + a:7 + a]).then_inc(pool_out, 1)
                if s == SLOT_HG_OUT:
                    act.wait_ge(hg_copied, 1)
                    act.activation(hg_e[:, 0, :], hg_o, ACT.Square).then_inc(hg_sq, 1)
                    act.wait_ge(foxT_mm, 1)
                    scaled_out(0, 4, foxT_out)
            act.wait_ge(proj_out, NB)
            act.activation(hg_t, gg.rearrange("p c n -> p (c n)"), ACT.Exp, scale=-1.0).then_inc(silu_exp, 1)
            act.wait_ge(fox_div, 2)
            act.activation(fox_sq[1], fox_o[:, 1, :], ACT.Square).then_inc(fox_sqd, 1)
            act.wait_ge(hgT_mm, 1)
            scaled_out(4, 2, hgT_out)
            act.wait_ge(foxT_mm, 2)
            scaled_out(2, 7, foxT_out)
            for c in range(TC):
                act.wait_ge(h1_ready, c + 1)
                act.activation(xn[:, c, :], h[:, c, :], ACT.Square, accum_out=ss[:, c:c + 1]).then_inc(sumsq2, 1)
            for c in range(TC):
                act.wait_ge(x2T_mm, c + 1)
                act.activation(h2T[:, 0:4, P * c:P * c + P], psum[:, (5, 2)[c], :].rearrange("p (a t) -> p a t", a=4),
                               ACT.Copy).then_inc(h2T_out, 1)
            for c in range(TC):
                act.wait_ge(top_ready, c + 1)
                act.activation(expo[:, c, :], logit[:, c, :], ACT.Exp, bias=negtop[:, c:c + 1]).then_inc(gate_exp, 1)

            def before_down(i, first=False):
                act.wait_ge(gather_mm, i + 1)
                act.activation(xe, psum[:, 0, :].rearrange("p (k s) -> p k s", k=KC), ACT.Copy).then_inc(xe_ready, 1)
                if not first:
                    transposed(i - 1)

            def transposed(i):
                act.wait_ge(actT_mm, i + 1)
                act.activation(actT, psum[:, 1, :].rearrange("p (j s) -> p j s", j=4), ACT.Copy).then_inc(actT_ready, 1)
                act.wait_ge(comb_mm, i + 1)
                act.activation(comb, psum[:, 2, 0:T].rearrange("p (c t) -> p c t", c=TC), ACT.Copy).then_inc(comb_ready, 1)

            def sigmoid(i):
                act.wait_ge(glu_ready, i + 1)
                act.activation(sig, glu, ACT.Sigmoid, scale=ALPHA).then_inc(sig_ready, 1)

            def y_copy(i):
                act.wait_ge(w2_used, 4 * i + 4)
                act.activation(y_sb, psum[:, 5, :], ACT.Copy).then_inc(y_ready, 1)

            before_down(0, first=True)
            act.wait_ge(gateT_mm, 1)
            act.activation(gateT, psum[0:E, 1, 0:T], ACT.Copy).then_inc(gateT_out, 1)
            act.wait_ge(count_ready, 1)
            extra = act.value_load(extra_pairs[0:1, 0:1], min_val=0, max_val=(PASSES - 1) * E // 2)
            pairs = extra + E // 2
            n = extra * 2 + E
            sigmoid(0)
            before_down(1)
            sigmoid(1)
            y_copy(0)
            with act.Fori(2, n) as i:
                before_down(i)
                sigmoid(i)
                y_copy(i - 1)
            transposed(n - 1)
            y_copy(n - 1)
            for c in range(TC):
                act.wait_ge(put_added, TC * n - 1 + c)
                act.activation(xn[:, c, :], h[:, c, :], ACT.Square, accum_out=ss[:, c:c + 1]).then_inc(sumsq3, 1)

        @block.vector
        def _(dve):
            done = [0]

            def link(ins):
                done[0] += 1
                ins.then_inc(dve_chain, 1)
                dve.wait_ge(dve_chain, done[0])

            link(dve.memset(wff[:, :, :], 0.0))
            link(dve.memset(ffb_row, 0.0))
            dve.memset(ones_row, 1.0)
            dve.wait_ge(ff_in, 32)
            for q in range(4):
                dve.tensor_copy(wff[:, :, 32 * q:32 * q + FOX_H], wff_cols)
                ins = dve.tensor_copy(ffb_row[:, 32 * q:32 * q + FOX_H], ffb_in_row)
            ins.then_inc(wff_ready, 1)
            dve.wait_ge(mixgain_in, 16)
            for c in range(TC):
                dve.wait_ge(rstd_ready, c + 1)
                dve.scalar_tensor_tensor(out=xn[:, c, :], in0=h[:, c, :], scalar=rstd[:, c:c + 1], in1=gain_a[:, :],
                                         op0=ALU.mult, op1=ALU.mult).then_inc(xn_ready, 1)
            dve.wait_ge(small_in, 16)
            link(dve.tensor_tensor(lbe, lbraw, lbraw, ALU.subtract))
            link(dve.tensor_scalar(lbe, lbe, 1.0, None, ALU.add))
            link(dve.reciprocal(lbp, lbe))
            link(dve.tensor_tensor(lbp, lbe, lbp, ALU.mult))
            link(dve.tensor_tensor(lb, lbp, lbp, ALU.subtract))
            link(dve.tensor_scalar(one_lb, lb, -1.0, 1.0, ALU.mult, ALU.add))
            dve.wait_ge(xT_done, TC)
            for b in range(2, 4):
                dve.tensor_copy(hT[:, 2 * b:2 * b + 2, :],
                                psum[:, 2 + b, :].rearrange("p (a t) -> p a t", a=2)).then_inc(hT_ready, 1)
            dve.wait_ge(b1_part, 1)
            dve.tensor_tensor(b1_tmp, b1_tmp, b1_parts[:, :], ALU.subtract).then_inc(b1_rest, 1)
            dve.wait_ge(ff_done, 1)
            dve.tensor_copy(fox_l, psum[:, 6, 0:T]).then_inc(ff_z, 1)
            dve.wait_ge(ff_ln, 1)
            dve.wait_ge(consts, 1)
            link(dve.scalar_tensor_tensor(out=ff_t, in0=fox_l, scalar=0.0, in1=ff_t, op0=ALU.min, op1=ALU.subtract))
            link(dve.memset(hg_a[:, 0:T], 1.0))
            link(dve.tensor_tensor_scan(fox_l, hg_a[:, 0:T], ff_t, 0.0, ALU.mult, ALU.add))
            for j in range(4):
                dve.tensor_scalar(fox_r[:, j, :], fox_l, r_neg[:, j:j + 1], r_one[:, j:j + 1], ALU.mult, ALU.add
                                  ).then_inc(fox_lr, 1)
            dve.wait_ge(fox_lr, 4)
            dve.tensor_scalar(fox_l, fox_l, l_scale, l_shift, ALU.mult, ALU.add).then_inc(fox_lr, 1)
            dve.wait_ge(b1_part, 3)
            last_part = slice(2 * E, 3 * E)
            dve.tensor_tensor(b1_tmp[last_part], b1_tmp[last_part], b1_parts[last_part, :], ALU.subtract
                              ).then_inc(b1_rest, 1)
            dve.wait_ge(b1_rest, 2)
            dve.tensor_copy(b1_parts[last_part, :], b1_tmp[last_part]).then_inc(b1_part, 1)
            gf = gfT.rearrange("p a t -> p (a t)")
            dve.wait_ge(hg_ln, 1)
            link(dve.scalar_tensor_tensor(out=hg_a, in0=gf, scalar=0.0, in1=hg_t, op0=ALU.min, op1=ALU.subtract))
            dve.tensor_tensor(hg_k, hg_a, gf, ALU.subtract).then_inc(hg_karg, 1)
            dve.tensor_scalar(hg_t, hg_a, -1.0, 40.0, ALU.mult, ALU.min).then_inc(hg_targ, 1)
            dve.wait_ge(hg_tln, 1)
            for a in range(2):
                v = hg_t[:, a * T:(a + 1) * T]
                ins = dve.tensor_scalar(v, v, lb[:, a:a + 1], one_lb[:, a:a + 1], ALU.mult, ALU.add)
            ins.then_inc(hg_targ, 1)
            dve.wait_ge(hg_kexp, 1)
            for a in range(2):
                v = hg_k[:, a * T:(a + 1) * T]
                link(dve.tensor_scalar(v, v, one_lb[:, a:a + 1], None, ALU.mult))
            dve.wait_ge(hg_tln, 2)
            link(dve.tensor_tensor(gf, hg_a, hg_t, ALU.add))
            link(dve.tensor_tensor_scan(hg_a, restart[:, :], gf, 0.0, ALU.mult, ALU.add))

            gq = gqT.rearrange("p a t -> p (a t)")

            def halves(v, half):
                w = v.rearrange("p (n b) -> p n b", b=2 * half)
                return w[:, :, 0:half], w[:, :, half:2 * half]

            def level_args(n):
                half = LEVELS[n]
                if n >= 2:
                    dve.wait_ge(lvl_dec, n - 1)
                lo_a, hi_a = halves(hg_a, half)
                lo_e, hi_e = halves(hg_e[:, n % 2, :], half)
                end = lo_a[:, :, half - 1:half].to_broadcast([P, 2 * T // (2 * half), half])
                dve.tensor_tensor(lo_e, end, lo_a, ALU.subtract)
                if half == CHUNK:
                    dve.tensor_copy(hi_e, hi_a).then_inc(lvl_arg, 1)
                else:
                    dve.tensor_tensor(hi_e, hi_a, end, ALU.subtract).then_inc(lvl_arg, 1)

            def level_decayed(n):
                half = LEVELS[n]
                dve.wait_ge(lvl_exp, n + 1)
                if n >= 2:
                    dve.wait_ge(lvl_mm, n - 1)
                lo_e, hi_e = halves(hg_e[:, n % 2, :], half)
                lo_d, hi_d = halves(hg_d[:, n % 2, :], half)
                dve.tensor_tensor(lo_d, halves(hg_k, half)[0], lo_e, ALU.mult)
                dve.tensor_tensor(hi_d, halves(gq, half)[1], hi_e, ALU.mult).then_inc(lvl_dec, 1)

            def level_take(n):
                dve.wait_ge(lvl_mm, n + 1)
                mask = lvl_mask[:, n, :].bitcast(I16).unsqueeze(1).to_broadcast([P, 8, P])
                dve.copy_predicated(hg_s, mask, psum[:, 3:5, :].rearrange("p a (b t) -> p (a b) t", t=P)
                                    ).then_inc(lvl_taken, 1)

            def cross_args(n):
                a2 = hg_a.rearrange("p (a t) -> p a t", a=2)
                e2 = hg_e[:, n % 2, :].rearrange("p (a t) -> p a t", a=2)
                end0 = a2[:, :, 63:64]
                end1 = a2[:, :, 127:128]
                link(dve.tensor_tensor(ref2.unsqueeze(2), end0, end1, ALU.add))
                dve.tensor_tensor(e2[:, :, 0:64], ref2.unsqueeze(2).to_broadcast([P, 2, 64]), a2[:, :, 0:64], ALU.subtract)
                dve.tensor_tensor(e2[:, :, 64:128], end1.to_broadcast([P, 2, 64]), a2[:, :, 64:128], ALU.subtract)
                dve.tensor_copy(e2[:, :, 128:192], a2[:, :, 128:192])
                dve.tensor_tensor(e2[:, :, 192:256], a2[:, :, 192:256], a2[:, :, 191:192].to_broadcast([P, 2, 64]),
                                  ALU.add).then_inc(lvl_arg, 1)

            def cross_decayed(n):
                dve.wait_ge(lvl_exp, n + 1)
                dve.wait_ge(lvl_mm, n - 1)
                e2 = hg_e[:, n % 2, :].rearrange("p (a t) -> p a t", a=2)
                d2 = hg_d[:, n % 2, :].rearrange("p (a t) -> p a t", a=2)
                dve.tensor_tensor(d2[:, :, 0:P], hg_k.rearrange("p (a t) -> p a t", a=2)[:, :, 0:P], e2[:, :, 0:P], ALU.mult)
                dve.tensor_tensor(d2[:, :, P:T], gqT[:, :, P:T], e2[:, :, P:T], ALU.mult).then_inc(lvl_dec, 1)

            def masked_max(hd):
                dve.wait_ge(score_mm, hd + 1)
                for c in range(TC):
                    g = row_of(hd, c)
                    v = fox_p[:, hd % 2, P * c:P * c + P * (c + 1)]
                    ins = dve.tensor_tensor_reduce(out=v, in0=psum[:, 7, P * c:P * c + P * (c + 1)],
                                                   in1=causal[:, P * (1 - c):], scale=1.0, scalar=-3e38,
                                                   op0=ALU.add, op1=ALU.max, accum_out=negmax[:, g:g + 1])
                    link(ins)
                    ins = dve.tensor_scalar(negmax[:, g:g + 1], negmax[:, g:g + 1], -1.0, None, ALU.mult)
                ins.then_inc(score_max, 1)

            def probT_copy(hd):
                dve.wait_ge(probT_mm, hd + 1)
                if hd >= 2:
                    dve.wait_ge(pv_mm, hd - 1)
                dve.tensor_copy(fox_pt[:, hd % 2, :], psum[:, 2, 0:3 * P]).then_inc(probT_ready, 1)

            def fox_divide(g):
                dve.wait_ge(pv_mm, 4 * g + 4)
                link(dve.reciprocal(rowinv[:, 8 * g:8 * g + 8], rowsum[:, 8 * g:8 * g + 8]))
                inv = rowinv[:, 8 * g:8 * g + 8].rearrange("p (c j) -> p c j", c=TC).unsqueeze(3)
                dve.tensor_tensor(fox_o[:, g, :].rearrange("p (c j d) -> p c j d", c=TC, j=4),
                                  psum[:, 5:7, g * T:(g + 1) * T].rearrange("p c (j d) -> p c j d", d=HD),
                                  inv.to_broadcast([P, TC, 4, HD]), ALU.mult).then_inc(fox_div, 1)

            def fox_variance(g):
                dve.wait_ge(fox_sqd, g + 1)
                m = fox_ms[:, 8 * g:8 * g + 8]
                link(dve.tensor_reduce(m, fox_sq[g].rearrange("p (g d) -> p g d", d=HD), AX, ALU.add))
                dve.tensor_scalar(m, m, 1.0 / HD, EPS, ALU.mult, ALU.add).then_inc(fox_var, 1)

            def fox_normalise(g):
                dve.wait_ge(fox_rstd, g + 1)
                v = fox_o[:, g, :].rearrange("p (g d) -> p g d", d=HD)
                dve.tensor_tensor(v, v, fox_r2[:, 8 * g:8 * g + 8].unsqueeze(2).to_broadcast([P, 8, HD]), ALU.mult
                                  ).then_inc(fox_ready, 1)

            dve.wait_ge(masks_ready, 1)
            for s in range(NSLOT):
                ahead, after, now = SLOT_LEVEL.get(s + 1), SLOT_LEVEL.get(s + 2), SLOT_LEVEL.get(s)
                if s == 4:
                    dve.wait_ge(proj_out, 2)
                if ahead == 8:
                    cross_decayed(7)
                elif ahead is not None and ahead < 7:
                    level_decayed(ahead)
                if s - 1 in SLOT_HEAD:
                    probT_copy(SLOT_HEAD[s - 1])
                if s in SLOT_HEAD:
                    masked_max(SLOT_HEAD[s])
                if now == 8:
                    dve.wait_ge(lvl_mm, 9)
                    dve.tensor_copy(hg_x_rows, psum[:, 3:5, 0:T]).then_inc(lvl_taken, 1)
                elif now is not None:
                    level_take(now)
                if after == 8:
                    dve.wait_ge(lvl_dec, 6)
                    cross_args(7)
                elif after is not None and after < 7:
                    level_args(after)
                if s == 8:
                    dve.wait_ge(consts, 2)
                    dve.reciprocal(win_inv, win_inv).then_inc(pooled_ready, 1)
                if s == SLOT_DIV0:
                    fox_divide(0)
                if s == SLOT_VAR0:
                    fox_variance(0)
                if s == SLOT_NORM0:
                    fox_normalise(0)
                if s == SLOT_HG_OUT:
                    dve.wait_ge(hg_mm, 1)
                    dve.tensor_copy(hg_o, psum[:, 3, :]).then_inc(hg_copied, 1)
                    dve.wait_ge(hg_sq, 1)
                    link(dve.tensor_reduce(hg_ms, hg_e[:, 0, :].rearrange("p (g d) -> p g d", d=HD), AX, ALU.add))
                    dve.tensor_scalar(hg_ms, hg_ms, 1.0 / HD, EPS, ALU.mult, ALU.add).then_inc(hg_var, 1)
            fox_divide(1)
            dve.wait_ge(silu_exp, 1)
            link(dve.tensor_scalar(hg_t, hg_t, 1.0, None, ALU.add))
            link(dve.reciprocal(hg_t, hg_t))
            fox_variance(1)
            link(dve.tensor_tensor(hg_t, hg_t, gg.rearrange("p c n -> p (c n)"), ALU.mult))
            link(dve.tensor_tensor(hg_t, hg_o, hg_t, ALU.mult))
            dve.wait_ge(hg_rstd, 1)
            dve.tensor_tensor(hg_o.rearrange("p (g d) -> p g d", d=HD), hg_t.rearrange("p (g d) -> p g d", d=HD),
                              hg_r2.unsqueeze(2).to_broadcast([P, 8, HD]), ALU.mult).then_inc(hg_ready, 1)
            fox_normalise(1)
            def residual(c):
                dve.wait_ge(mix_mm, c + 1)
                dve.tensor_tensor(h[:, c, :], h[:, c, :], psum[:, (0, 3)[c]:(2, 5)[c], :].rearrange("p a n -> p (a n)"),
                                  ALU.add).then_inc(h1_ready, 1)

            def norm2(c):
                dve.wait_ge(rstd2, c + 1)
                dve.scalar_tensor_tensor(out=xn[:, c, :], in0=h[:, c, :], scalar=rstd[:, c:c + 1], in1=gain_b[:, :],
                                         op0=ALU.mult, op1=ALU.mult).then_inc(xn2_ready, 1)

            def norm2T(c):
                dve.wait_ge(x2T_mm, c + 1)
                dve.tensor_copy(h2T[:, 4:8, P * c:P * c + P], psum[:, (6, 7)[c], :].rearrange("p (a t) -> p a t", a=4)
                                ).then_inc(h2T_out, 1)

            def route(c):
                dve.wait_ge(logit_mm, c + 1)
                link(dve.tensor_tensor(logit[:, c, :], psum[:, c, 0:E], br_sb[:, :], ALU.add))
                link(dve.max(out=top8[:, c, :], in_=logit[:, c, :]))
                dve.tensor_scalar(negtop[:, c:c + 1], top8[:, c, 0:1], -1.0, None, ALU.mult).then_inc(top_ready, 1)
                fourth = top8[:, c, TOPK - 1:TOPK]
                dve.tensor_scalar(strict[:, c, :], logit[:, c, :], fourth, None, ALU.is_gt)
                link(dve.tensor_scalar(tie[:, c, :], logit[:, c, :], fourth, None, ALU.is_equal))
                dve.tensor_reduce(nstrict[:, c:c + 1], strict[:, c, :], AX, ALU.add)
                link(dve.tensor_tensor_scan(tie_n[:, c, :], restart[:, 1:1 + E], tie[:, c, :], 0.0, ALU.mult, ALU.add))
                link(dve.tensor_scalar(need[:, c:c + 1], nstrict[:, c:c + 1], -1.0, float(TOPK), ALU.mult, ALU.add))
                link(dve.scalar_tensor_tensor(out=tie[:, c, :], in0=tie_n[:, c, :], scalar=need[:, c:c + 1],
                                              in1=tie[:, c, :], op0=ALU.is_le, op1=ALU.mult))
                dve.tensor_tensor(chosen_b[:, c, :], strict[:, c, :], tie[:, c, :], ALU.add).then_inc(chosen_ready, 1)
                link(dve.tensor_tensor(chosen[:, c, :], strict[:, c, :], tie[:, c, :], ALU.add))

            residual(0)
            dve.wait_ge(late_in, 64)
            norm2(0)
            residual(1)
            norm2T(0)
            norm2(1)
            route(0)
            norm2T(1)
            route(1)
            dve.wait_ge(rank_mm, 1)
            for c in range(TC):
                link(dve.scalar_tensor_tensor(out=tie[:, c, :], in0=psum[:, 3, c * E:(c + 1) * E], scalar=1.0,
                                              in1=chosen[:, c, :], op0=ALU.add, op1=ALU.mult))

            def pass_ranks(first, last):
                for c in range(TC):
                    for b in range(first, last):
                        link(dve.tensor_scalar(rank_t[:, c, b * E:(b + 1) * E], tie[:, c, :], float(-1 - SLOTS * b),
                                               None, ALU.add))

            link(dve.tensor_reduce(nmax, psum[:, 3, 2 * E:3 * E], AX, ALU.max))
            pass_ranks(0, 1)

            def select(i, b, reuse=True):
                if reuse:
                    dve.wait_ge(comb_mm, i - 1)
                for c in range(TC):
                    dve.tensor_scalar(pick[:, b, c, :], iota2[:, 0, :], rank_t[:, c, bass.ds(i, 1)], None, ALU.is_equal)
                dve.tensor_scalar(which[:, b, :], ones_bf[0:3 * E, 0:SLOTS], expert_id[:, bass.ds(i, 1)], None,
                                  ALU.mult).then_inc(sel_ready, 1)

            def weight(i, b):
                for c in range(TC):
                    dve.tensor_scalar(put[:, b, c, :].rearrange("p (a s) -> p a s", a=2), iota2[:, :, :],
                                      rank_t[:, c, bass.ds(i, 1)], gate_t[:, c, bass.ds(i, 1)], ALU.is_equal, ALU.mult)

            def activate(i, reuse=True):
                pairs = psum[:, 3:5, :].rearrange("p a (f two) -> p (a f) two", two=2)
                dve.wait_ge(w1_used, KC * i + KC)
                if reuse:
                    dve.wait_ge(act_ready, i)
                dve.tensor_scalar(glu, pairs[:, :, 0], LIMIT, None, ALU.min).then_inc(glu_ready, 1)
                dve.tensor_scalar(lin, pairs[:, :, 1], -LIMIT, LIMIT, ALU.max, ALU.min).then_inc(lin_ready, 1)
                dve.wait_ge(lin_ready, i + 1)
                dve.wait_ge(glu_ready, i + 1)
                dve.scalar_tensor_tensor(out=lin, in0=lin, scalar=1.0, in1=glu, op0=ALU.add, op1=ALU.mult
                                         ).then_inc(gated, 1)
                dve.wait_ge(gated, i + 1)
                dve.wait_ge(sig_ready, i + 1)
                if reuse:
                    dve.wait_ge(actT_mm, i)
                dve.tensor_tensor(act_r, lin, sig, ALU.mult).then_inc(act_ready, 1)

            def add_up(i, reuse=True):
                for c in range(TC):
                    dve.wait_ge(put_mm, TC * i + c + 1)
                    dve.tensor_tensor(h[:, c, :], h[:, c, :],
                                      psum[:, (6, 1)[c]:(8, 3)[c], :].rearrange("p a n -> p (a n)"), ALU.add
                                      ).then_inc(put_added, 1)
                dve.wait_ge(put_added, TC * i + TC)

            select(0, 0, reuse=False)
            for c in range(TC):
                dve.wait_ge(gate_exp, c + 1)
                link(dve.tensor_tensor(expo[:, c, :], expo[:, c, :], chosen[:, c, :], ALU.mult))
                link(dve.tensor_reduce(gsum[:, c:c + 1], expo[:, c, :], AX, ALU.add))
                link(dve.reciprocal(ginv[:, c:c + 1], gsum[:, c:c + 1]))
                dve.tensor_scalar(gate_t[:, c, :].rearrange("p (a e) -> p a e", e=E),
                                  expo[:, c, :].unsqueeze(1).to_broadcast([P, PASSES, E]), ginv[:, c:c + 1], None,
                                  ALU.mult).then_inc(gate_ready, 1)
            for b in range(1, PASSES):
                ins = dve.tensor_scalar(over[:, b - 1:b], nmax, float(SLOTS * b), float(E // 2), ALU.is_gt, ALU.mult)
            link(ins)
            link(dve.tensor_reduce(nmax, over, AX, ALU.add))
            dve.tensor_copy(extra_pairs[0:1, :], nmax[0:1, :]).then_inc(count_ready, 1)
            pass_ranks(1, PASSES)
            dve.wait_ge(gate_ready, 2)
            dve.wait_ge(count_ready, 1)
            extra = dve.value_load(extra_pairs[0:1, 0:1], min_val=0, max_val=(PASSES - 1) * E // 2)
            pairs = extra + E // 2
            n = extra * 2 + E
            select(1, 1, reuse=False)
            weight(0, 0)
            activate(0, reuse=False)
            for c in range(TC):
                dve.wait_ge(bias2_mm, c + 1)
                dve.tensor_tensor(h[:, c, :], h[:, c, :], psum[:, (6, 1)[c]:(8, 3)[c], :].rearrange("p a n -> p (a n)"),
                                  ALU.add).then_inc(bias2_added, 1)
            dve.wait_ge(bias2_added, 2)
            weight(1, 1)
            activate(1)
            with dve.Fori(1, pairs) as j:
                i = j * 2
                for b in range(2):
                    select(i + b, b)
                    weight(i + b, b)
                    add_up(i + b - 2)
                    activate(i + b)
            add_up(n - 2)
            add_up(n - 1)
            dve.wait_ge(finalgain_in, 16)
            for c in range(TC):
                dve.wait_ge(rstd3, c + 1)
                dve.scalar_tensor_tensor(out=xn[:, c, :], in0=h[:, c, :], scalar=rstd[:, c:c + 1], in1=gain_a[:, :],
                                         op0=ALU.mult, op1=ALU.mult).then_inc(final_ready, 1)

        @block.tensor
        def _(pe):
            pe.wait_ge(ident_ready, 1)
            for c in range(TC):
                pe.wait_ge(xn_ready, c + 1)
                for k in range(KC):
                    last = pe.transpose(psum[:, 2 + k // 2, (k % 2) * T + c * P:(k % 2) * T + (c + 1) * P],
                                        xn[:, c, k * P:(k + 1) * P], ident[:, :])
                last.then_inc(xT_done, 1)
            pe.wait_ge(hT_ready, 4)
            pe.wait_ge(wff_ready, 1)
            pe.matmul(psum[:, 6, 0:T], ffb_row, ones_row, start=True, stop=False)
            for k in range(KC):
                last = pe.matmul(psum[:, 6, 0:T], wff[:, k, :], hT[:, k, :], start=False, stop=k == KC - 1)
            last.then_inc(ff_done, 1)

            def project(n, half):
                _, _, transposed = BLOCKS[n]
                w = block_sb(n)
                if half == 0:
                    pe.wait_ge(block_in[n], 16)
                    if n >= 2:
                        pe.wait_ge(proj_out, n - 1)
                for k in range(KC):
                    if transposed:
                        lhs, rhs = w[:, k, half * P:(half + 1) * P], hT[:, k, :]
                    else:
                        lhs, rhs = hT[:, k, half * P:(half + 1) * P], w[:, k, :]
                    last = pe.matmul(psum[:, n % 2, half * T:(half + 1) * T], lhs, rhs, start=k == 0,
                                     stop=k == KC - 1)
                if half == 1:
                    last.then_inc(proj_done, 1)

            def level(n):
                if n < 7:
                    pe.wait_ge(lvl_dec, n + 1)
                if n == 0:
                    pe.wait_ge(hT_ready, 4)
                if n >= 1:
                    pe.wait_ge(lvl_taken, n)
                for c in range(TC):
                    for hd in range(HG_H):
                        rows = slice(HD * (hd % 2), HD * (hd % 2) + HD)
                        span = slice((hd // 2) * T + c * P, (hd // 2) * T + (c + 1) * P)
                        if n < 7:
                            lhs, rhs = hg_d[rows, n % 2, span], hg_d[rows, n % 2, span]
                        else:
                            lhs, rhs = hg_k[rows, span], gqT[rows, hd // 2, c * P:(c + 1) * P]
                        j = c * 2 + hd // 2
                        last = pe.matmul(psum[:, 3 + hd % 2, j * P:(j + 1) * P], lhs, rhs, start=True, stop=True)
                last.then_inc(lvl_mm, 1)

            def cross():
                pe.wait_ge(lvl_dec, 8)
                pe.wait_ge(lvl_taken, 8)
                for hd in range(HG_H):
                    rows = slice(HD * (hd % 2), HD * (hd % 2) + HD)
                    o = (hd // 2) * T
                    last = pe.matmul(psum[:, 3 + hd % 2, (hd // 2) * P:(hd // 2 + 1) * P], hg_d[rows, 1, o:o + P],
                                     hg_d[rows, 1, o + P:o + T], start=True, stop=True)
                last.then_inc(lvl_mm, 1)

            def scores(hd):
                rows = slice(HD * (hd % 2), HD * (hd % 2) + HD)
                if hd == 0:
                    pe.wait_ge(fox_lr, 5)
                pe.wait_ge(proj_out, 4 if hd < 4 else 8)
                if hd >= 1:
                    pe.wait_ge(score_max, hd)
                for c in range(TC):
                    o = psum[:, 7, P * c:P * c + P * (c + 1)]
                    pe.matmul(o, qT[rows, hd // 2, c * P:(c + 1) * P], kT[rows, hd // 2, 0:P * (c + 1)], start=True, stop=False)
                    last = pe.matmul(o, fox_l[rows, c * P:(c + 1) * P], fox_r[rows, hd // 2, 0:P * (c + 1)], start=False,
                                     stop=True)
                last.then_inc(score_mm, 1)

            def probT(hd):
                pe.wait_ge(prob_ready, TC * (hd + 1))
                if hd >= 1:
                    pe.wait_ge(probT_ready, hd)
                for j in range(3):
                    last = pe.transpose(psum[:, 2, j * P:(j + 1) * P], fox_p[:, hd % 2, j * P:(j + 1) * P], ident[:, :])
                last.then_inc(probT_mm, 1)

            def weigh(hd):
                pe.wait_ge(probT_ready, hd + 1)
                pe.wait_ge(proj_out, 5 if hd < 4 else 9)
                if hd == 4:
                    pe.wait_ge(fox_div, 1)
                span = slice(hd * HD, (hd + 1) * HD)
                pe.matmul(psum[:, 5, span], fox_pt[:, hd % 2, 0:P], v_sb[:, 0, span], start=True, stop=True)
                pe.matmul(psum[:, 6, span], fox_pt[:, hd % 2, P:2 * P], v_sb[:, 0, span], start=True, stop=False)
                pe.matmul(psum[:, 6, span], fox_pt[:, hd % 2, 2 * P:3 * P], v_sb[:, 1, span], start=False, stop=True
                          ).then_inc(pv_mm, 1)

            def pooled():
                pe.wait_ge(pooled_ready, 2)
                pe.wait_ge(small_in, 96)
                pe.wait_ge(lvl_taken, 9)
                for g in range(4):
                    rows = slice(HD * (g % 2), HD * (g % 2) + HD)
                    last = pe.matmul(psum[rows, 4 - g % 2, (g // 2) * T:(g // 2 + 1) * T], poolw_sb[rows, g // 2, :],
                                     win_b[rows, g // 2, :], start=True, stop=True)
                last.then_inc(pool_mm, 1)

            def hgrn_out():
                pe.wait_ge(proj_out, 10)
                pe.wait_ge(pool_out, 4)
                for c in range(TC):
                    for g in range(HG_H):
                        o = psum[:, 3, c * T + g * HD:c * T + (g + 1) * HD]
                        last = pe.matmul(o, hg_s[:, (g % 2) * 4 + c * 2 + g // 2, :], gi[:, c, g * HD:(g + 1) * HD],
                                         start=True, stop=c == 0)
                        if c == 1:
                            last = pe.matmul(o, hg_x[:, (g % 2) * 2 + g // 2, :], gi[:, 0, g * HD:(g + 1) * HD],
                                             start=False, stop=True)
                last.then_inc(hg_mm, 1)

            def fox_transpose(g, bank):
                pe.wait_ge(fox_ready, g + 1)
                for a in range(2):
                    for c in range(TC):
                        last = pe.transpose(psum[:, bank, a * T + c * P:a * T + (c + 1) * P],
                                            fox_o[:, g, c * T + a * P:c * T + (a + 1) * P], ident[:, :])
                last.then_inc(foxT_mm, 1)

            for s in range(NSLOT):
                project(s // 2, s % 2)
                if s - 1 in SLOT_HEAD:
                    probT(SLOT_HEAD[s - 1])
                if s - 2 in SLOT_HEAD:
                    weigh(SLOT_HEAD[s - 2])
                if s in SLOT_HEAD:
                    scores(SLOT_HEAD[s])
                if SLOT_LEVEL.get(s) == 8:
                    cross()
                elif s in SLOT_LEVEL:
                    level(SLOT_LEVEL[s])
                if s == SLOT_POOL:
                    pooled()
                if s == SLOT_HG_OUT:
                    hgrn_out()
                    fox_transpose(0, 4)

            def mix(c, chunks):
                for k in chunks:
                    for half in range(2):
                        last = pe.matmul(psum[:, (0, 3)[c] + half, :], oT[k - k % 2][:, k % 2, c * P:(c + 1) * P],
                                         w2_ring[:, 1, k, half * 512:(half + 1) * 512], start=k == 6, stop=k == 3)
                return last

            for n in range(4):
                pe.wait_ge(wout_in[n], 16)
            pe.wait_ge(foxT_out, 2)
            pe.wait_ge(hg_copied, 1)
            mix(1, (6, 7, 0, 1))
            pe.wait_ge(proj_out, NB)
            pe.wait_ge(hg_ready, 1)
            for a in range(2):
                for c in range(TC):
                    last = pe.transpose(psum[:, 2, a * T + c * P:a * T + (c + 1) * P],
                                        hg_o[:, c * T + a * P:c * T + (a + 1) * P], ident[:, :])
            last.then_inc(hgT_mm, 1)
            mix(0, (6, 7, 0, 1))
            fox_transpose(1, 7)
            pe.wait_ge(hgT_out, 2)
            mix(0, (4, 5))
            pe.wait_ge(foxT_out, 4)
            mix(0, (2, 3)).then_inc(mix_mm, 1)
            mix(1, (4, 5, 2, 3)).then_inc(mix_mm, 1)
            for c in range(TC):
                pe.wait_ge(xn2_ready, c + 1)
                for k in range(KC):
                    last = pe.transpose(psum[:, ((5, 6), (2, 7))[c][k // 4], (k % 4) * P:(k % 4 + 1) * P],
                                        xn[:, c, k * P:(k + 1) * P], ident[:, :])
                last.then_inc(x2T_mm, 1)
                pe.wait_ge(h2T_out, 2 * c + 2)
                for k in range(KC):
                    last = pe.matmul(psum[:, c, 0:E], h2T[:, k, c * P:(c + 1) * P], wr_sb[:, k, :],
                                     start=k == 0, stop=k == KC - 1)
                last.then_inc(logit_mm, 1)
            pe.wait_ge(chosen_ready, 2)
            pe.matmul(psum[:, 3, 0:E], before[:, :], chosen_b[:, 0, :], start=True, stop=True)
            pe.matmul(psum[:, 3, E:2 * E], ones_bf[:, :], chosen_b[:, 0, :], start=True, stop=False)
            pe.matmul(psum[:, 3, E:2 * E], before[:, :], chosen_b[:, 1, :], start=False, stop=True)
            pe.matmul(psum[:, 3, 2 * E:3 * E], ones_bf[:, :], chosen_b[:, 0, :], start=True, stop=False)
            pe.matmul(psum[:, 3, 2 * E:3 * E], ones_bf[:, :], chosen_b[:, 1, :], start=False, stop=True
                      ).then_inc(rank_mm, 1)
            def gather(i, b):
                pe.wait_ge(sel_ready, i + 1)
                for k in range(KC):
                    for c in range(TC):
                        last = pe.matmul(psum[:, 0, k * SLOTS:(k + 1) * SLOTS], xn[:, c, k * P:(k + 1) * P],
                                         pick[:, b, c, :], start=c == 0, stop=c == TC - 1)
                last.then_inc(gather_mm, 1)

            def transpose_act(i, b, reuse=True):
                pe.wait_ge(act_ready, i + 1)
                if reuse:
                    pe.wait_ge(put_added, TC * i)
                for j in range(4):
                    last = pe.transpose(psum[:, 1, j * P:(j + 1) * P], act_r[:, j * P:(j + 1) * P], ident[:, :])
                last.then_inc(actT_mm, 1)
                for c in range(TC):
                    last = pe.transpose(psum[:, 2, c * P:(c + 1) * P], put[:, b, c, :], ident[:, :])
                last.then_inc(comb_mm, 1)

            def up(i, b, reuse=True):
                if reuse:
                    pe.wait_ge(lin_ready, i)
                for q in range(2):
                    for g in range(2):
                        pe.matmul(psum[g * SLOTS:(g + 1) * SLOTS, 3 + q, :], which[:, b, :],
                                  b1_parts[:, g * F + q * 512:g * F + (q + 1) * 512], start=True, stop=False)
                pe.wait_ge(xe_ready, i + 1)
                for k in range(KC):
                    pe.wait_ge(w1_in[k], 16 * i + 16)
                    for q in range(2):
                        for g in range(2):
                            last = pe.matmul(psum[g * SLOTS:(g + 1) * SLOTS, 3 + q, :], xe[:, k, :],
                                             w1_ring[:, k, g * F + q * 512:g * F + (q + 1) * 512], start=False,
                                             stop=k == KC - 1)
                    last.then_inc(w1_used, 1)

            def down(i, b, loaded, reuse=True):
                pe.wait_ge(actT_ready, i + 1)
                if reuse:
                    pe.wait_ge(y_ready, i)
                for k in range(KC):
                    if k % 2 == 0:
                        pe.wait_ge(w2_in[b][k // 2], loaded)
                    for g in range(2):
                        last = pe.matmul(psum[g * SLOTS:(g + 1) * SLOTS, 5, :],
                                         actT[:, k % 4, (k // 4) * SLOTS:(k // 4 + 1) * SLOTS],
                                         w2_ring[:, b, k, g * 512:(g + 1) * 512], start=k == 0, stop=k == KC - 1)
                    if k % 2:
                        last.then_inc(w2_used, 1)

            def combine(i, reuse=True):
                pe.wait_ge(y_ready, i + 1)
                pe.wait_ge(comb_ready, i + 1)
                for c in range(TC):
                    if c == 0 and reuse:
                        pe.wait_ge(put_added, TC * i - 1)
                    for g in range(2):
                        last = pe.matmul(psum[:, (6, 1)[c] + g, :], comb[g * SLOTS:(g + 1) * SLOTS, c, :],
                                         y_sb[g * SLOTS:(g + 1) * SLOTS, :], start=True, stop=True)
                    last.then_inc(put_mm, 1)

            def item(i, b, loaded):
                gather(i, b)
                transpose_act(i - 1, 1 - b)
                up(i, b)
                down(i - 1, 1 - b, loaded)
                combine(i - 1)

            gather(0, 0)
            up(0, 0, reuse=False)
            pe.wait_ge(gate_ready, 2)
            for c in range(TC):
                last = pe.transpose(psum[:, 1, c * P:(c + 1) * P], gate_t[:, c, :], ident[:, :])
            last.then_inc(gateT_mm, 1)
            gather(1, 1)
            pe.wait_ge(gateT_out, 1)
            for c in range(TC):
                for half in range(2):
                    last = pe.matmul(psum[:, (6, 1)[c] + half, :], gateT[:, c * P:(c + 1) * P],
                                     b2_sb[:, half * 512:(half + 1) * 512], start=True, stop=True)
                last.then_inc(bias2_mm, 1)
            pe.wait_ge(count_ready, 1)
            extra = pe.value_load(extra_pairs[0:1, 0:1], min_val=0, max_val=(PASSES - 1) * E // 2)
            pairs = extra + E // 2
            n = extra * 2 + E
            pe.wait_ge(bias2_added, 2)
            transpose_act(0, 0, reuse=False)
            up(1, 1)
            down(0, 0, 16, reuse=False)
            combine(0, reuse=False)
            with pe.Fori(1, pairs) as j:
                i = j * 2
                item(i, 0, 8 * i)
                item(i + 1, 1, 8 * i + 16)
            transpose_act(n - 1, 1)
            down(n - 1, 1, 8 * n)
            combine(n - 1)


_INS = ["x", "norm_mix", "w_in", "b_fox_f", "fox_gain", "hgrn_lb", "hgrn_gain", "pool_w", "pool_scale", "w_out",
        "norm_moe", "w_router", "b_router", "w1", "b1", "w2", "b2", "norm_final"]


def kernel(**inputs):
    import numpy as _np
    import concourse.bacc as _bacc
    from concourse import mybir as _mybir
    from concourse.bass_utils import run_bass_kernel_spmd as _run

    nc = _bacc.Bacc("TRN2", target_bir_lowering=False, num_devices=1)
    arrays, args = {}, []
    for name in _INS:
        a = _np.ascontiguousarray(inputs[name])
        arrays[f"in_{name}_dram"] = a
        args.append(nc.dram_tensor(f"in_{name}_dram", a.shape, _mybir.dt.from_np(a.dtype), kind="ExternalInput").ap())
    args.append(nc.dram_tensor("out_0_dram", (1, T, D), _mybir.dt.float32, kind="ExternalOutput").ap())
    build(nc, *args)
    r = _run(nc, [arrays], core_ids=[0])
    return r.results[0]["out_0_dram"]
```

```python
from contextlib import ExitStack

import concourse.bass as bass
from concourse import mybir

F32 = mybir.dt.float32
BF16 = mybir.dt.bfloat16
I16 = mybir.dt.int16
I32 = mybir.dt.int32
ALU = mybir.AluOpType
ACT = mybir.ActivationFunctionType
AX = mybir.AxisListType.X

P = 128
D = 1024
T = 256
TC = T // P
KC = D // P
FOX_H, HG_H, HD = 8, 4, 64
CHUNK = 64
WINDOWS = (2, 4, 8, 16)
E, TOPK, F = 32, 4, 1024
LIMIT, ALPHA = 7.0, 1.702
EPS = 1e-5
SLOTS = 64
PASSES = T // SLOTS
NEG = -1e30

BLOCKS = [("gf", 1800, True), ("gq", 1544, True), ("fk0", 512, True), ("fq0", 0, True), ("fv0", 1024, False),
          ("pu", 2568, True), ("fk1", 768, True), ("fq1", 256, True), ("fv1", 1280, False), ("gi", 2056, False),
          ("gg", 2312, False)]
FF_COL = 1536
BN = 256
NB = len(BLOCKS)
SLOT_LEVEL = {6: 0, 7: 1, 9: 2, 11: 3, 12: 4, 13: 5, 14: 6, 15: 7, 16: 8}
SLOT_HEAD = {8: 0, 9: 1, 10: 2, 11: 3, 16: 4, 17: 5, 18: 6, 19: 7}
NSLOT = 2 * NB
SLOT_DIV0 = 14
SLOT_VAR0 = 15
SLOT_NORM0 = 17
SLOT_POOL = 18
SLOT_HG_OUT = 20
LEVELS = (64, 32, 16, 8, 4, 2, 1, 0)
NL = len(LEVELS)
ARENA = 9984
WARM = 5
EARLY = 4


def build(nc, x, norm_mix, w_in, b_fox_f, fox_gain, hgrn_lb, hgrn_gain, pool_w, pool_scale, w_out,
          norm_moe, w_router, b_router, w1, b1, w2, b2, norm_final, out):
    with ExitStack() as ctx:
        def sb(name, shape, dt=F32):
            return ctx.enter_context(nc.sbuf_tensor(name, shape, dt))

        def sem(name):
            return ctx.enter_context(nc.semaphore(name))

        w1_ring = sb("w1_ring", [P, KC, 2 * F])
        w2_ring = sb("w2_ring", [P, 2, KC, D])
        h = sb("h", [P, TC, D])
        xn = sb("xn", [P, TC, D])
        gain_b = sb("gain_b", [P, D])
        arena = sb("arena", [P, ARENA])
        spare = sb("spare", [P, 2 * F])
        ident = sb("ident", [P, P])
        iota2 = sb("iota2", [P, 2, SLOTS])
        b1_parts = sb("b1_parts", [3 * E, 2 * F], BF16)
        b2_sb = sb("b2_sb", [E, D])
        wr_sb = sb("wr_sb", [P, KC, E])
        before = sb("before", [P, P], BF16)
        ones_bf = sb("ones_bf", [P, P], BF16)
        poolw_sb = sb("poolw_sb", [P, 2, HD])
        mix_gain = sb("mix_gain", [P, KC])
        br_sb = sb("br_sb", [P, E])
        small = sb("small", [P, 256])
        expert_id = sb("expert_id", [3 * E, PASSES * E], BF16)
        extra_pairs = sb("extra_pairs", [1, 1], I32)
        psum = ctx.enter_context(nc.psum_tensor("psum", [P, 8, 512], F32))

        at = [0]

        def take(*shape, start=None):
            if start is not None:
                at[0] = start
            n = 1
            for s in shape:
                n *= s
            v = arena[:, at[0]:at[0] + n]
            at[0] += n
            assert at[0] <= ARENA
            if len(shape) == 2:
                v = v.rearrange("p (a b) -> p a b", a=shape[0])
            if len(shape) == 3:
                v = v.rearrange("p (a b c) -> p a b c", a=shape[0], b=shape[1])
            return v

        wff = spare[:, 0:KC * P].rearrange("p (k n) -> p k n", n=P)
        lvl_mask = spare[:, 1024:1536].bitcast(BF16).rearrange("p (l n) -> p l n", n=P)
        causal = spare[:, 1536:1792]
        restart = spare[:, 1792:2048].bitcast(BF16)

        hT = take(KC, T)
        q_even = take(4, T)
        k_even = take(4, T)
        v_sb = take(TC, 512)
        gfT = take(2, T)
        gqT = take(2, T)
        puT = take(2, T)
        gg = take(TC, T)
        gi = take(TC, T)
        q_odd = take(4, T)
        k_odd = take(4, T)
        fox_l = take(1, T)[:, 0, :]
        scratch = w2_ring[:, 0, :, :].rearrange("p k n -> p (k n)")
        hg_a = scratch[:, 0:512]
        hg_k = scratch[:, 512:1024]
        hg_e = scratch[:, 1024:2048].rearrange("p (a b) -> p a b", a=2)
        hg_d = scratch[:, 2048:3072].rearrange("p (a b) -> p a b", a=2)
        hg_s = scratch[:, 3072:4096].rearrange("p (a b) -> p a b", a=8)
        hg_x = scratch[:, 4096:4608].rearrange("p (a b) -> p a b", a=4)
        hg_x_rows = scratch[:, 4096:4608].rearrange("p (a b) -> p a b", a=2)
        fox_pt = scratch[:, 4608:5376].rearrange("p (a b) -> p a b", a=2)
        hg_t = scratch[:, 5376:5888]
        ff_t = scratch[:, 5888:6144]
        win_a = scratch[:, 6144:6656].rearrange("p (a b) -> p a b", a=2)
        win_b = scratch[:, 6656:7168].rearrange("p (a b) -> p a b", a=2)
        win_inv = scratch[:, 7168:7680].rearrange("p (a b) -> p a b", a=2)
        hg_o = scratch[:, 7680:8192]
        b1_tmp = scratch[0:3 * E, 6144:8192]
        ones_row = scratch[0:1, 1024:1280]
        ffb_row = scratch[0:1, 1280:1408]
        ffb_in_row = scratch[0:1, 1408:1416]
        wff_cols = scratch[:, 1536:1600].rearrange("p (k h) -> p k h", k=KC)
        xflat = xn[:, :, :].rearrange("p c n -> p (c n)")
        fox_p = xflat[:, 0:768].rearrange("p (a b) -> p a b", a=2)
        fox_o = xflat[:, 768:1792].rearrange("p (g n) -> p g n", g=2)
        fox_sq = (gfT.rearrange("p a t -> p (a t)"), hT[:, 0:2, :].rearrange("p a t -> p (a t)"))
        oT = {0: q_even[:, 0:2, :], 2: puT, 4: k_even[:, 0:2, :], 6: gqT}
        h1T = take(KC, T, start=0)
        xe = take(KC, SLOTS)
        put = take(2, TC, P)
        pick = take(2, TC, SLOTS)
        comb = take(TC, P)
        glu = take(512)
        lin = take(512)
        sig = take(512)
        act_r = take(512)
        actT = take(4, P)
        y_sb = take(512)
        rank_t = take(TC, PASSES * E)
        gate_t = take(TC, PASSES * E)
        which = take(SLOTS).bitcast(BF16).rearrange("p (a b) -> p a b", a=2)[0:3 * E]
        gateT = take(T)[0:E]
        logit = take(TC, E)
        strict = take(TC, E)
        tie = take(TC, E)
        tie_n = take(TC, E)
        chosen = take(TC, E)
        expo = take(TC, E)
        chosen_b = take(TC * E // 2).bitcast(BF16).rearrange("p (c e) -> p c e", c=TC)
        assert at[0] <= ARENA - 2 * F
        w1_early = [arena[:, ARENA - 2 * F:ARENA], spare[:, :], arena[:, 3584:3584 + 2 * F], arena[:, 0:2 * F]]

        def row_of(hd, c):
            return (hd // 4) * 8 + c * 4 + hd % 4

        col = [0]

        def cols(n):
            col[0] += n
            return small[:, col[0] - n:col[0]]

        ss, ms, rstd = cols(TC), cols(TC), cols(TC)
        neg_half = cols(16)
        l_scale, l_shift = cols(1), cols(1)
        r_neg, r_one = cols(4), cols(4)
        rowsum, rowinv = cols(16), cols(16)
        fox_ms, fox_r2 = cols(16), cols(16)
        hg_ms, hg_r2 = cols(8), cols(8)
        negmax = cols(16)
        lbraw, lbe, lbp, lb, one_lb = cols(2), cols(2), cols(2), cols(2), cols(2)
        ref2 = cols(2)
        top8 = cols(16).rearrange("p (c k) -> p c k", c=TC)
        nstrict, need, negtop, gsum, ginv = cols(2), cols(2), cols(2), cols(2), cols(2)
        nmax, over = cols(1), cols(3)
        first_gain, moe_gain, ss_rest = cols(KC), cols(KC), cols(1)

        last_ss = cols(4)
        squares = arena[:, 0:2 * D].rearrange("p (c n) -> p c n", c=TC)
        row_half = [slice(0, D // 2), slice(D // 2, D)]

        x_in = [sem(f"x_in{c}") for c in range(TC)]
        mixgain_in, small_in, lb_in = sem("mixgain_in"), sem("small_in"), sem("lb_in")
        ff_in, b1_in, late_in = sem("ff_in"), sem("b1_in"), sem("late_in")
        block_in = [sem(f"block_in{n}") for n in range(NB)]
        wout_in = [sem(f"wout_in{n}") for n in range(4)]
        w1_in = [sem(f"w1_in{k}") for k in range(KC)]
        early_in = [sem(f"early_in{k}") for k in range(EARLY)]
        w2_in = [[sem(f"w2_in{b}_{k}") for k in range(4)] for b in range(2)]
        finalgain_in, out_done = sem("finalgain_in"), sem("out_done")
        pool_chain, dve_chain, act_chain = sem("pool_chain"), sem("dve_chain"), sem("act_chain")
        ident_ready, consts, wff_ready, b1_part, b1_rest = (sem("ident_ready"), sem("consts"), sem("wff_ready"),
                                                           sem("b1_part"), sem("b1_rest"))
        masks_ready = sem("masks_ready")
        sumsq, rstd_ready, xn_ready, xT_done, hT_ready = (sem("sumsq"), sem("rstd_ready"), sem("xn_ready"),
                                                          sem("xT_done"), sem("hT_ready"))
        ff_done, ff_z, ff_ln, fox_lr = sem("ff_done"), sem("ff_z"), sem("ff_ln"), sem("fox_lr")
        proj_done, proj_out = sem("proj_done"), sem("proj_out")
        hg_ln, hg_karg, hg_kexp, hg_targ, hg_tln = (sem("hg_ln"), sem("hg_karg"),
                                                          sem("hg_kexp"), sem("hg_targ"), sem("hg_tln"))
        lvl_arg, lvl_exp, lvl_dec, lvl_mm, lvl_taken = (sem("lvl_arg"), sem("lvl_exp"), sem("lvl_dec"),
                                                        sem("lvl_mm"), sem("lvl_taken"))
        pooled_ready, pool_mm, pool_out = sem("pooled_ready"), sem("pool_mm"), sem("pool_out")
        score_mm, score_max, prob_ready, probT_mm, probT_ready, pv_mm = (
            sem("score_mm"), sem("score_max"), sem("prob_ready"), sem("probT_mm"), sem("probT_ready"), sem("pv_mm"))
        hg_mm, hg_copied, hg_sq, hg_var, hg_rstd = (sem("hg_mm"), sem("hg_copied"), sem("hg_sq"),
                                                  sem("hg_var"), sem("hg_rstd"))
        silu_exp, hg_ready, hgT_mm, hgT_out = sem("silu_exp"), sem("hg_ready"), sem("hgT_mm"), sem("hgT_out")
        fox_div, fox_sqd, fox_var, fox_rstd, fox_ready, foxT_mm, foxT_out = (
            sem("fox_div"), sem("fox_sqd"), sem("fox_var"), sem("fox_rstd"), sem("fox_ready"), sem("foxT_mm"),
            sem("foxT_out"))
        mix_mm, h1_ready, sumsq2, rstd2, h1T_mm, h1T_act, h1T_dve, wr_ready = (
            sem("mix_mm"), sem("h1_ready"), sem("sumsq2"), sem("rstd2"), sem("h1T_mm"), sem("h1T_act"),
            sem("h1T_dve"), sem("wr_ready"))
        mix_part = sem("mix_part")
        xn2_scaled, xn2_ready, which_first, gather_first, xe_first = (
            sem("xn2_scaled"), sem("xn2_ready"), sem("which_first"), sem("gather_first"), sem("xe_first"))
        logit_mm, top_ready, gate_exp, chosen_ready, rank_mm, count_ready = (
            sem("logit_mm"), sem("top_ready"), sem("gate_exp"), sem("chosen_ready"), sem("rank_mm"),
            sem("count_ready"))
        gate_ready, gateT_mm, gateT_out = sem("gate_ready"), sem("gateT_mm"), sem("gateT_out")
        sel_ready, gather_mm, xe_ready, actT_mm, actT_ready, comb_mm, comb_ready = (
            sem("sel_ready"), sem("gather_mm"), sem("xe_ready"), sem("actT_mm"), sem("actT_ready"),
            sem("comb_mm"), sem("comb_ready"))
        glu_ready, lin_ready, sig_ready, gated, act_ready = (
            sem("glu_ready"), sem("lin_ready"), sem("sig_ready"), sem("gated"), sem("act_ready"))
        y_ready, put_mm, put_added = sem("y_ready"), sem("put_mm"), sem("put_added")
        w1_used, w2_used = sem("w1_used"), sem("w2_used")
        last_mm, last_added, sumsq3, rstd3, weighted, final_dve, final_act = (
            sem("last_mm"), sem("last_added"), sem("sumsq3"), sem("rstd3"), sem("weighted"), sem("final_dve"),
            sem("final_act"))

        x_v = x[0].rearrange("(c p) n -> p c n", p=P)
        out_v = out[0].rearrange("(c p) n -> p c n", p=P)
        w_in_v = w_in[0].rearrange("(k p) n -> p k n", p=P)
        w_out_v = w_out[0].rearrange("(k p) n -> p k n", p=P)
        w1_v = w1[0].rearrange("e (k p) n -> e p k n", p=P)
        w2_v = w2[0].rearrange("e (k p) n -> e p k n", p=P)

        def block_sb(n):
            if n < 3:
                return w2_ring[:, 1, 2 * n:2 * n + 2, :].rearrange("p a (b n) -> p (a b) n", n=BN)
            return w1_ring[:, n - 3, :].rearrange("p (k n) -> p k n", n=BN)

        block = ctx.enter_context(nc.Block())

        @block.sync
        def _(sp):
            for c in range(TC):
                sp.dma_start(h[:, c, :], x_v[:, c, :]).then_inc(x_in[c], 16)
            for n, (_, c0, _) in enumerate(BLOCKS):
                sp.dma_start(block_sb(n), w_in_v[:, :, c0:c0 + BN]).then_inc(block_in[n], 16)
                if n == 0:
                    for part in range(3):
                        sp.dma_start(b1_tmp[E * part:E * part + E, :], b1[0]).then_inc(b1_in, 16)
            sp.wait_ge(proj_done, 3)
            for n in range(4):
                sp.dma_start(w2_ring[:, 1, 2 * n:2 * n + 2, :], w_out_v[:, 2 * n:2 * n + 2, :]).then_inc(wout_in[n], 16)
            for k in range(KC):
                if k == KC - 1:
                    sp.wait_ge(score_mm, FOX_H)
                    sp.wait_ge(score_max, FOX_H)
                    sp.wait_ge(lvl_taken, NL + 1)
                    for n in (0, 1):
                        sp.dma_start(w1_early[n], w1_v[0, :, n, :]).then_inc(early_in[n], 16)
                sp.wait_ge(proj_done, 4 + k)
                sp.dma_start(w1_ring[:, k, :], w1_v[1 if k < EARLY else 0, :, k, :]).then_inc(w1_in[k], 16)
            sp.wait_ge(pv_mm, FOX_H)
            sp.dma_start(w1_early[2], w1_v[0, :, 2, :]).then_inc(early_in[2], 16)
            sp.wait_ge(hgT_mm, 1)
            for k in range(4):
                sp.dma_start(w2_ring[:, 0, 2 * k:2 * k + 2, :], w2_v[0, :, 2 * k:2 * k + 2, :]).then_inc(w2_in[0][k], 16)
            for k in (0, 3, 1, 2):
                if k == 0:
                    sp.wait_ge(mix_part, 1)
                if k == 1:
                    sp.wait_ge(mix_mm, 3)
                sp.dma_start(w2_ring[:, 1, 2 * k:2 * k + 2, :], w2_v[1, :, 2 * k:2 * k + 2, :]).then_inc(w2_in[1][k], 16)
            sp.wait_ge(logit_mm, TC)
            sp.dma_start(w1_early[3], w1_v[0, :, 3, :]).then_inc(early_in[3], 16)

            def load_w1(i):
                e = i % E
                for k in range(KC):
                    sp.wait_ge(w1_used, KC * (i - 1) + k + 1)
                    sp.dma_start(w1_ring[:, k, :], w1_v[bass.ds(e, 1), :, k, :].rearrange("e p n -> (e p) n")
                                 ).then_inc(w1_in[k], 16)

            def load_w2(i, b):
                e = i % E
                for k in range(4):
                    sp.wait_ge(w2_used, 4 * (i - 2) + k + 1)
                    sp.dma_start(w2_ring[:, b, 2 * k:2 * k + 2, :],
                                 w2_v[bass.ds(e, 1), :, 2 * k:2 * k + 2, :].rearrange("e p k n -> (e p) k n")
                                 ).then_inc(w2_in[b][k], 16)

            for k in range(EARLY, KC):
                sp.wait_ge(w1_used, k - EARLY + 1)
                sp.dma_start(w1_ring[:, k, :], w1_v[1, :, k, :]).then_inc(w1_in[k], 16)
            sp.wait_ge(count_ready, 1)
            extra = sp.value_load(extra_pairs[0:1, 0:1], min_val=0, max_val=(PASSES - 1) * E // 2)
            pairs = extra + E // 2
            n = extra * 2 + E
            with sp.Fori(1, pairs) as j:
                i = j * 2
                load_w1(i)
                load_w2(i, 0)
                load_w1(i + 1)
                load_w2(i + 1, 1)
            for c in range(TC):
                sp.wait_ge(final_dve, c + 1)
                sp.wait_ge(final_act, c + 1)
                sp.dma_start(out_v[:, c, :], xn[:, c, :]).then_inc(out_done, 16)
            sp.wait_ge(out_done, 16 * TC)

        @block.gpsimd
        def _(pool):
            done = [0]

            def link(ins):
                done[0] += 1
                ins.then_inc(pool_chain, 1)
                pool.wait_ge(pool_chain, done[0])

            def band(v, op_base, pattern, mult, op=ALU.is_ge):
                link(pool.affine_select(out=v, in_=v, pattern=pattern, compare_op=op, fill=0.0, base=op_base,
                                        channel_multiplier=mult))

            link(pool.memset(neg_half, -0.5))
            link(pool.memset(ident[:, :], 0.0))
            pool.affine_select(out=ident[:, :], in_=ident[:, :], compare_op=ALU.not_equal, fill=1.0, base=0,
                               pattern=[[-1, P]], channel_multiplier=1).then_inc(ident_ready, 1)
            pool.wait_ge(ident_ready, 1)
            for c in range(TC):
                pool.wait_ge(sumsq, c + 1)
                link(pool.tensor_scalar(ms[:, c:c + 1], ss[:, c:c + 1], 1.0 / D, EPS, ALU.mult, ALU.add))
                pool.tensor_tensor(rstd[:, c:c + 1], ms[:, c:c + 1], neg_half[:, 0:1], ALU.pow).then_inc(rstd_ready, 1)
                pool.wait_ge(rstd_ready, c + 1)
            link(pool.memset(l_scale, 0.0))
            link(pool.memset(l_shift, 0.0))
            link(pool.memset(r_neg, 0.0))
            link(pool.memset(r_one, 0.0))
            for q in range(4):
                rows = slice(32 * q, 32 * q + 32)
                link(pool.memset((l_scale if q % 2 == 0 else l_shift)[rows], 1.0))
                target = (r_one if q % 2 == 0 else r_neg)[rows]
                link(pool.memset(target, 1.0 if q % 2 == 0 else -1.0))
                band(target, q // 2 - 1, [[-2, 4]], 1, ALU.is_equal)
            link(pool.memset(restart[:, :], 1.0))
            link(pool.affine_select(out=restart[:, :].rearrange("p (a b) -> p a b", b=CHUNK),
                                    in_=restart[:, :].rearrange("p (a b) -> p a b", b=CHUNK),
                                    compare_op=ALU.not_equal, fill=0.0, base=0, pattern=[[0, 2 * T // CHUNK], [1, CHUNK]],
                                    channel_multiplier=0))
            pool.memset(lvl_mask[:, :, :], 0.0).then_inc(consts, 1)
            pool.wait_ge(consts, 1)
            for n, half in enumerate(LEVELS):
                if half == 0:
                    link(pool.memset(lvl_mask[:, n, :], 1.0))
                    band(lvl_mask[:, n, :], 0, [[-1, P]], 1, ALU.is_equal)
                    continue
                nb = P // (2 * half)
                v = lvl_mask[:, n, :].rearrange("p (a b) -> p a b", b=2 * half)[:, :, half:2 * half]
                link(pool.memset(v, 1.0))
                band(v, 0, [[-2 * half, nb], [0, half]], 1)
                band(v, half - 1, [[2 * half, nb], [0, half]], -1)
            link(pool.memset(causal[:, :], 0.0))
            link(pool.affine_select(out=causal[:, P:], in_=causal[:, P:], compare_op=ALU.is_ge, fill=NEG, base=0,
                                    pattern=[[-1, P]], channel_multiplier=1))
            pool.memset(hg_s, 0.0).then_inc(masks_ready, 1)
            link(pool.memset(ones_bf[:, :], 1.0))
            link(pool.memset(before[:, :], 1.0))
            band(before[:, :], -1, [[1, P]], -1)
            link(pool.iota(iota2[:, :, :], pattern=[[0, 2], [1, SLOTS]], base=1, channel_multiplier=0,
                           allow_small_or_imprecise_dtypes=True))
            link(pool.memset(expert_id[:, :], 1.0))
            for r in range(3):
                v = expert_id[E * r:E * r + E, :].rearrange("p (a e) -> p a e", e=E)
                band(v, 0, [[0, PASSES], [-1, E]], 1, ALU.is_equal)
            pool.wait_ge(b1_part, 4)
            link(pool.iota(win_inv, pattern=[[0, 2], [1, T]], base=1, channel_multiplier=0,
                           allow_small_or_imprecise_dtypes=True))
            for g, w in enumerate(WINDOWS):
                rows = slice(HD * (g % 2), HD * (g % 2) + HD)
                ins = pool.memset(win_inv[rows, g // 2, w:T], float(w))
                if g < 3:
                    link(ins)
            ins.then_inc(consts, 1)
            pool.wait_ge(consts, 2)
            pool.wait_ge(proj_out, 6)
            pool.wait_ge(pooled_ready, 1)
            src = puT
            for step, w in enumerate(WINDOWS):
                sh = w // 2
                dst = (win_a, win_b)[step % 2]
                if step >= 1:
                    link(pool.tensor_copy(dst[:, :, :], src[:, :, :]))
                for g in range(step, 4):
                    rows = slice(HD * (g % 2), HD * (g % 2) + HD)
                    link(pool.tensor_tensor(dst[rows, g // 2, sh:T], src[rows, g // 2, sh:T],
                                            src[rows, g // 2, 0:T - sh], ALU.add))
                    if step == 0:
                        link(pool.tensor_copy(dst[rows, g // 2, 0:sh], src[rows, g // 2, 0:sh]))
                src = dst
            link(pool.tensor_tensor(win_a, src, win_inv, ALU.mult))
            pool.tensor_tensor(win_b, win_a, puT, ALU.subtract).then_inc(pooled_ready, 1)
            pool.wait_ge(pooled_ready, 2)
            pool.wait_ge(fox_var, 1)
            pool.tensor_tensor(fox_r2[:, 0:8], fox_ms[:, 0:8], neg_half[:, 0:8], ALU.pow).then_inc(fox_rstd, 1)
            pool.wait_ge(fox_rstd, 1)
            pool.wait_ge(hg_var, 1)
            pool.tensor_tensor(hg_r2, hg_ms, neg_half[:, 0:8], ALU.pow).then_inc(hg_rstd, 1)
            pool.wait_ge(hg_rstd, 1)
            pool.wait_ge(fox_var, 2)
            pool.tensor_tensor(fox_r2[:, 8:16], fox_ms[:, 8:16], neg_half[:, 0:8], ALU.pow).then_inc(fox_rstd, 1)
            pool.wait_ge(fox_rstd, 2)

            def inverse_rms(c, give):
                link(pool.tensor_scalar(ms[:, c:c + 1], ss[:, c:c + 1], 1.0 / D, EPS, ALU.mult, ALU.add))
                pool.tensor_tensor(rstd[:, c:c + 1], ms[:, c:c + 1], neg_half[:, 0:1], ALU.pow).then_inc(give, 1)
                pool.wait_ge(give, c + 1)

            pool.wait_ge(late_in, 80)
            for c in range(TC):
                pool.wait_ge(sumsq2, (1, 3)[c])
                if c == 1:
                    link(pool.tensor_tensor(ss[:, 1:2], ss[:, 1:2], ss_rest, ALU.add))
                inverse_rms(c, rstd2)
                pool.wait_ge(xn2_scaled, c + 1)
                pool.tensor_tensor(xn[:, c, :], xn[:, c, :], gain_b[:, :], ALU.mult).then_inc(xn2_ready, 1)
            for c in range(TC):
                pool.wait_ge(sumsq3, 2 * c + 2)
                link(pool.tensor_tensor(ss[:, c:c + 1], last_ss[:, 2 * c:2 * c + 1], last_ss[:, 2 * c + 1:2 * c + 2],
                                        ALU.add))
                inverse_rms(c, rstd3)

        @block.scalar
        def _(act):
            done = [0]

            def link(ins):
                done[0] += 1
                ins.then_inc(act_chain, 1)
                act.wait_ge(act_chain, done[0])

            act.dma_start(first_gain, norm_mix[0].rearrange("(k p) -> p k", p=P), allow_slow_non_contiguous=True
                          ).then_inc(mixgain_in, 16)
            act.dma_start(wff_cols, w_in_v[:, :, FF_COL:FF_COL + FOX_H]).then_inc(ff_in, 16)
            act.dma_start(ffb_in_row, b_fox_f).then_inc(ff_in, 16)
            for c in range(TC):
                act.wait_ge(x_in[c], 16)
                act.activation(xn[:, c, :], h[:, c, :], ACT.Square, accum_out=ss[:, c:c + 1]).then_inc(sumsq, 1)
            act.dma_start(lbraw, hgrn_lb[0].rearrange("(c p) -> p c", p=P), allow_slow_non_contiguous=True).then_inc(lb_in, 16)
            act.wait_ge(xT_done, TC)
            act.wait_ge(mixgain_in, 16)
            for k in range(4):
                ins = act.activation(hT[:, k, :], psum[:, 2 + k // 2, (k % 2) * T:(k % 2 + 1) * T], ACT.Copy,
                                     scale=first_gain[:, k:k + 1])
                if k % 2:
                    ins.then_inc(hT_ready, 1)
            act.wait_ge(b1_in, 48)
            act.activation(b1_parts[:, :], b1_tmp, ACT.Copy).then_inc(b1_part, 1)
            act.wait_ge(ff_z, 1)
            link(act.activation(ff_t, fox_l, ACT.Abs))
            link(act.activation(ff_t, ff_t, ACT.Exp, scale=-1.0))
            act.activation(ff_t, ff_t, ACT.Ln, bias=1.0).then_inc(ff_ln, 1)
            act.wait_ge(b1_rest, 1)
            for part in (1, 2):
                act.activation(b1_parts[E * part:E * part + E, :], b1_tmp[E * part:E * part + E, :], ACT.Copy
                               ).then_inc(b1_part, 1)
            act.dma_start(mix_gain[:, 0:4], fox_gain[0].rearrange("(c p) -> p c", p=P), allow_slow_non_contiguous=True).then_inc(small_in, 16)
            act.dma_start(mix_gain[:, 4:6], hgrn_gain[0].rearrange("(c p) -> p c", p=P), allow_slow_non_contiguous=True).then_inc(small_in, 16)
            act.dma_start(mix_gain[:, 6:8], pool_scale[0].rearrange("(c p) -> p c", p=P), allow_slow_non_contiguous=True).then_inc(small_in, 16)
            for a in range(2):
                act.dma_start(poolw_sb[:, a, :], pool_w[0, 2 * a:2 * a + 2].rearrange("g c d -> (g c) d")).then_inc(small_in, 16)

            where = {"gf": gfT, "gq": gqT, "gi": gi, "pu": puT, "gg": gg, "fv0": v_sb[:, :, 0:BN],
                     "fv1": v_sb[:, :, BN:2 * BN]}
            by_head = {"fk0": (k_even, k_odd, 0), "fk1": (k_even, k_odd, 2), "fq0": (q_even, q_odd, 0),
                       "fq1": (q_even, q_odd, 2)}

            def take_block(n):
                name = BLOCKS[n][0]
                act.wait_ge(proj_done, n + 1)
                src = psum[:, n % 2, :].rearrange("p (a t) -> p a t", a=2)
                if name in where:
                    act.activation(where[name], src, ACT.Copy).then_inc(proj_out, 1)
                    return
                even, odd, a = by_head[name]
                scale = HD ** -0.5 if name in ("fq0", "fq1") else 1.0
                act.activation(even[0:HD, a:a + 2, :], src[0:HD], ACT.Copy, scale=scale)
                act.activation(odd[HD:P, a:a + 2, :], src[HD:P], ACT.Copy, scale=scale).then_inc(proj_out, 1)

            def level_exp(n):
                act.wait_ge(lvl_arg, n + 1)
                act.activation(hg_e[:, n % 2, :], hg_e[:, n % 2, :], ACT.Exp).then_inc(lvl_exp, 1)

            def head_exp(hd):
                act.wait_ge(score_max, hd + 1)
                for c in range(TC):
                    v = fox_p[:, hd % 2, P * c:P * c + P * (c + 1)]
                    g = row_of(hd, c)
                    act.activation(v, v, ACT.Exp, bias=negmax[:, g:g + 1],
                                   accum_out=rowsum[:, g:g + 1]).then_inc(prob_ready, 1)

            def scaled_out(first, bank, signal):
                for a in range(2):
                    act.activation(oT[first][:, a, :], psum[:, bank, a * T:(a + 1) * T], ACT.Copy,
                                   scale=mix_gain[:, first + a:first + a + 1]).then_inc(signal, 1)

            for s in range(NSLOT):
                nxt = SLOT_LEVEL.get(s + 1)
                if nxt is not None and nxt != 7:
                    level_exp(min(nxt, 7))
                if s % 2 == 1:
                    take_block(s // 2)
                if s == 1:
                    act.wait_ge(proj_out, 1)
                    link(act.activation(hg_t, gfT.rearrange("p a t -> p (a t)"), ACT.Abs))
                    link(act.activation(hg_t, hg_t, ACT.Exp, scale=-1.0))
                    act.activation(hg_t, hg_t, ACT.Ln, bias=1.0).then_inc(hg_ln, 1)
                    act.wait_ge(hg_karg, 1)
                    act.activation(hg_k, hg_k, ACT.Exp).then_inc(hg_kexp, 1)
                    act.wait_ge(hg_targ, 1)
                    act.activation(hg_t, hg_t, ACT.Exp).then_inc(hg_tln, 1)
                    act.wait_ge(hg_targ, 2)
                    act.activation(hg_t, hg_t, ACT.Ln).then_inc(hg_tln, 1)
                if s in SLOT_HEAD:
                    head_exp(SLOT_HEAD[s])
                if s == 5:
                    act.dma_start(gain_b[:, :], norm_moe[0].partition_broadcast(P)).then_inc(late_in, 16)
                    act.dma_start(wr_sb[:, :, :], w_router[0].rearrange("(k p) e -> p k e", p=P)).then_inc(late_in, 16)
                    act.dma_start(br_sb[:, :], b_router[0].partition_broadcast(P)).then_inc(late_in, 16)
                    act.dma_start(moe_gain, norm_moe[0].rearrange("(k p) -> p k", p=P), allow_slow_non_contiguous=True
                                  ).then_inc(late_in, 16)
                    act.dma_start(b2_sb[:, :], b2[0]).then_inc(late_in, 16)
                if s == SLOT_DIV0:
                    act.wait_ge(fox_div, 1)
                    act.activation(fox_sq[0], fox_o[:, 0, :], ACT.Square).then_inc(fox_sqd, 1)
                if s == SLOT_POOL:
                    act.wait_ge(pool_mm, 1)
                    act.wait_ge(small_in, 80)
                    for g in range(2):
                        for a in range(2):
                            rows = slice(HD * g, HD * g + HD)
                            act.activation(oT[6][rows, a, :], psum[rows, 4 - g, a * T:(a + 1) * T], ACT.Copy,
                                           scale=mix_gain[rows, 6 + a:7 + a]).then_inc(pool_out, 1)
                if s == SLOT_HG_OUT:
                    act.wait_ge(hg_copied, 1)
                    act.activation(hg_e[:, 0, :], hg_o, ACT.Square).then_inc(hg_sq, 1)
                    act.wait_ge(foxT_mm, 1)
                    scaled_out(0, 4, foxT_out)
            act.wait_ge(proj_out, NB)
            act.activation(hg_t, gg.rearrange("p c n -> p (c n)"), ACT.Exp, scale=-1.0).then_inc(silu_exp, 1)
            act.wait_ge(fox_div, 2)
            act.activation(fox_sq[1], fox_o[:, 1, :], ACT.Square).then_inc(fox_sqd, 1)
            act.wait_ge(hgT_mm, 1)
            scaled_out(4, 2, hgT_out)
            act.wait_ge(foxT_mm, 2)
            scaled_out(2, 7, foxT_out)
            def scaled_rows(c):
                act.wait_ge(rstd2, c + 1)
                act.activation(xn[:, c, :], h[:, c, :], ACT.Copy, scale=rstd[:, c:c + 1]).then_inc(xn2_scaled, 1)

            act.wait_ge(h1_ready, 1)
            act.activation(xn[:, 0, :], h[:, 0, :], ACT.Square, accum_out=ss[:, 0:1]).then_inc(sumsq2, 1)
            act.wait_ge(h1T_mm, 1)
            act.activation(h1T[:, 0:4, 0:P], psum[:, 5, :].rearrange("p (a t) -> p a t", a=4), ACT.Copy
                           ).then_inc(h1T_act, 1)
            act.wait_ge(h1_ready, 2)
            act.activation(xn[:, 1, row_half[0]], h[:, 1, row_half[0]], ACT.Square, accum_out=ss[:, 1:2]).then_inc(sumsq2, 1)
            act.wait_ge(h1T_mm, 2)
            act.activation(h1T[:, 0:4, P:T], psum[:, 2, :].rearrange("p (a t) -> p a t", a=4), ACT.Copy
                           ).then_inc(h1T_act, 1)
            act.wait_ge(sumsq2, 1)
            scaled_rows(0)
            act.wait_ge(h1_ready, 3)
            act.activation(xn[:, 1, row_half[1]], h[:, 1, row_half[1]], ACT.Square, accum_out=ss_rest).then_inc(sumsq2, 1)
            act.wait_ge(h1T_mm, 3)
            act.activation(h1T[:, 6:8, P:T], psum[:, 5, 0:T].rearrange("p (a t) -> p a t", a=2), ACT.Copy
                           ).then_inc(h1T_act, 1)
            act.wait_ge(sumsq2, 3)
            scaled_rows(1)
            for c in range(TC):
                act.wait_ge(top_ready, c + 1)
                act.activation(expo[:, c, :], logit[:, c, :], ACT.Exp, bias=negtop[:, c:c + 1]).then_inc(gate_exp, 1)

            def before_down(i):
                gathered(i)
                transposed(i - 1)

            def gathered(i):
                act.wait_ge(gather_mm, i + 1)
                act.activation(xe, psum[:, 0, :].rearrange("p (k s) -> p k s", k=KC), ACT.Copy).then_inc(xe_ready, 1)

            def transposed(i):
                act.wait_ge(actT_mm, i + 1)
                act.activation(actT, psum[:, 1, :].rearrange("p (j s) -> p j s", j=4), ACT.Copy).then_inc(actT_ready, 1)
                act.wait_ge(comb_mm, i + 1)
                act.activation(comb, psum[:, 2, 0:T].rearrange("p (c t) -> p c t", c=TC), ACT.Copy).then_inc(comb_ready, 1)

            def sigmoid(i):
                act.wait_ge(glu_ready, i + 1)
                act.activation(sig, glu, ACT.Sigmoid, scale=ALPHA).then_inc(sig_ready, 1)

            def y_copy(i):
                act.wait_ge(w2_used, 4 * i + 4)
                act.activation(y_sb, psum[:, 5, :], ACT.Copy).then_inc(y_ready, 1)

            for chunks, bank, signal in (((4, 6), 0, xe_first), ((6, 8), 6, xe_first), ((0, 4), 7, xe_ready)):
                if bank == 7:
                    act.wait_ge(gather_mm, 1)
                else:
                    act.wait_ge(gather_first, chunks[0] // 2 - 1)
                act.activation(xe[:, chunks[0]:chunks[1], :],
                               psum[:, bank, chunks[0] * SLOTS:chunks[1] * SLOTS].rearrange("p (k s) -> p k s", s=SLOTS),
                               ACT.Copy).then_inc(signal, 1)
            act.wait_ge(xn2_ready, TC)
            act.dma_start(gain_b[:, :], norm_final.partition_broadcast(P)).then_inc(finalgain_in, 16)
            act.wait_ge(count_ready, 1)
            extra = act.value_load(extra_pairs[0:1, 0:1], min_val=0, max_val=(PASSES - 1) * E // 2)
            pairs = extra + E // 2
            n = extra * 2 + E
            gathered(1)
            sigmoid(0)
            transposed(0)
            act.wait_ge(gateT_mm, 1)
            act.activation(gateT, psum[0:E, 0, 0:T], ACT.Copy).then_inc(gateT_out, 1)
            sigmoid(1)
            y_copy(0)
            with act.Fori(2, n - 1) as i:
                before_down(i)
                sigmoid(i)
                y_copy(i - 1)
            act.wait_ge(w1_used, KC * (n - 1))
            before_down(n - 1)
            y_copy(n - 2)
            sigmoid(n - 1)
            transposed(n - 1)
            y_copy(n - 1)
            for c in range(TC):
                for g in range(2):
                    act.wait_ge(last_added, 2 * c + g + 1)
                    act.activation(squares[:, c, row_half[g]], h[:, c, row_half[g]], ACT.Square,
                                   accum_out=last_ss[:, 2 * c + g:2 * c + g + 1]).then_inc(sumsq3, 1)
            for c in range(TC):
                act.wait_ge(rstd3, c + 1)
                act.wait_ge(weighted, c + 1)
                act.activation(xn[:, c, row_half[1]], xn[:, c, row_half[1]], ACT.Copy, scale=rstd[:, c:c + 1]
                               ).then_inc(final_act, 1)

        @block.vector
        def _(dve):
            done = [0]

            def link(ins):
                done[0] += 1
                ins.then_inc(dve_chain, 1)
                dve.wait_ge(dve_chain, done[0])

            link(dve.memset(wff[:, :, :], 0.0))
            link(dve.memset(ffb_row, 0.0))
            dve.memset(ones_row, 1.0)
            for c in range(TC):
                dve.wait_ge(rstd_ready, c + 1)
                dve.tensor_scalar(xn[:, c, :], h[:, c, :], rstd[:, c:c + 1], None, ALU.mult).then_inc(xn_ready, 1)
            dve.wait_ge(ff_in, 32)
            for q in range(4):
                dve.tensor_copy(wff[:, :, 32 * q:32 * q + FOX_H], wff_cols)
                ins = dve.tensor_copy(ffb_row[:, 32 * q:32 * q + FOX_H], ffb_in_row)
            ins.then_inc(wff_ready, 1)
            dve.wait_ge(xT_done, TC)
            dve.wait_ge(mixgain_in, 16)
            for k in range(4, KC):
                ins = dve.tensor_scalar(hT[:, k, :], psum[:, 2 + k // 2, (k % 2) * T:(k % 2 + 1) * T],
                                        first_gain[:, k:k + 1], None, ALU.mult)
                if k % 2:
                    ins.then_inc(hT_ready, 1)
            dve.wait_ge(b1_part, 1)
            dve.tensor_tensor(b1_tmp, b1_tmp, b1_parts[:, :], ALU.subtract).then_inc(b1_rest, 1)
            dve.wait_ge(ff_done, 1)
            dve.tensor_copy(fox_l, psum[:, 6, 0:T]).then_inc(ff_z, 1)
            dve.wait_ge(ff_ln, 1)
            dve.wait_ge(consts, 1)
            link(dve.scalar_tensor_tensor(out=ff_t, in0=fox_l, scalar=0.0, in1=ff_t, op0=ALU.min, op1=ALU.subtract))
            link(dve.memset(hg_a[:, 0:T], 1.0))
            link(dve.tensor_tensor_scan(fox_l, hg_a[:, 0:T], ff_t, 0.0, ALU.mult, ALU.add))
            dve.wait_ge(b1_part, 3)
            last_part = slice(2 * E, 3 * E)
            dve.tensor_tensor(b1_tmp[last_part], b1_tmp[last_part], b1_parts[last_part, :], ALU.subtract
                              ).then_inc(b1_rest, 1)
            dve.wait_ge(b1_rest, 2)
            dve.tensor_copy(b1_parts[last_part, :], b1_tmp[last_part]).then_inc(b1_part, 1)
            dve.wait_ge(lb_in, 16)
            link(dve.tensor_tensor(lbe, lbraw, lbraw, ALU.subtract))
            link(dve.tensor_scalar(lbe, lbe, 1.0, None, ALU.add))
            link(dve.reciprocal(lbp, lbe))
            link(dve.tensor_tensor(lbp, lbe, lbp, ALU.mult))
            link(dve.tensor_tensor(lb, lbp, lbp, ALU.subtract))
            link(dve.tensor_scalar(one_lb, lb, -1.0, 1.0, ALU.mult, ALU.add))
            gf = gfT.rearrange("p a t -> p (a t)")
            dve.wait_ge(hg_ln, 1)
            link(dve.scalar_tensor_tensor(out=hg_a, in0=gf, scalar=0.0, in1=hg_t, op0=ALU.min, op1=ALU.subtract))
            dve.tensor_tensor(hg_k, hg_a, gf, ALU.subtract).then_inc(hg_karg, 1)
            dve.tensor_scalar(hg_t, hg_a, -1.0, 40.0, ALU.mult, ALU.min).then_inc(hg_targ, 1)
            dve.wait_ge(hg_tln, 1)
            for a in range(2):
                v = hg_t[:, a * T:(a + 1) * T]
                ins = dve.tensor_scalar(v, v, lb[:, a:a + 1], one_lb[:, a:a + 1], ALU.mult, ALU.add)
            ins.then_inc(hg_targ, 1)
            dve.wait_ge(hg_kexp, 1)
            for a in range(2):
                v = hg_k[:, a * T:(a + 1) * T]
                link(dve.tensor_scalar(v, v, one_lb[:, a:a + 1], None, ALU.mult))
            dve.wait_ge(hg_tln, 2)
            link(dve.tensor_tensor(gf, hg_a, hg_t, ALU.add))
            link(dve.tensor_tensor_scan(hg_a, restart[:, :], gf, 0.0, ALU.mult, ALU.add))

            gq = gqT.rearrange("p a t -> p (a t)")

            def halves(v, half):
                w = v.rearrange("p (n b) -> p n b", b=2 * half)
                return w[:, :, 0:half], w[:, :, half:2 * half]

            def level_args(n):
                half = LEVELS[n]
                if n >= 2:
                    dve.wait_ge(lvl_dec, n - 1)
                lo_a, hi_a = halves(hg_a, half)
                lo_e, hi_e = halves(hg_e[:, n % 2, :], half)
                end = lo_a[:, :, half - 1:half].to_broadcast([P, 2 * T // (2 * half), half])
                dve.tensor_tensor(lo_e, end, lo_a, ALU.subtract)
                if half == CHUNK:
                    dve.tensor_copy(hi_e, hi_a).then_inc(lvl_arg, 1)
                else:
                    dve.tensor_tensor(hi_e, hi_a, end, ALU.subtract).then_inc(lvl_arg, 1)

            def level_decayed(n):
                half = LEVELS[n]
                dve.wait_ge(lvl_exp, n + 1)
                if n >= 2:
                    dve.wait_ge(lvl_mm, n - 1)
                lo_e, hi_e = halves(hg_e[:, n % 2, :], half)
                lo_d, hi_d = halves(hg_d[:, n % 2, :], half)
                dve.tensor_tensor(lo_d, halves(hg_k, half)[0], lo_e, ALU.mult)
                dve.tensor_tensor(hi_d, halves(gq, half)[1], hi_e, ALU.mult).then_inc(lvl_dec, 1)

            def level_take(n):
                dve.wait_ge(lvl_mm, n + 1)
                mask = lvl_mask[:, n, :].bitcast(I16).unsqueeze(1).to_broadcast([P, 8, P])
                dve.copy_predicated(hg_s, mask, psum[:, 3:5, :].rearrange("p a (b t) -> p (a b) t", t=P)
                                    ).then_inc(lvl_taken, 1)

            def cross_args(n):
                a2 = hg_a.rearrange("p (a t) -> p a t", a=2)
                e2 = hg_e[:, n % 2, :].rearrange("p (a t) -> p a t", a=2)
                end0 = a2[:, :, 63:64]
                end1 = a2[:, :, 127:128]
                link(dve.tensor_tensor(ref2.unsqueeze(2), end0, end1, ALU.add))
                dve.tensor_tensor(e2[:, :, 0:64], ref2.unsqueeze(2).to_broadcast([P, 2, 64]), a2[:, :, 0:64], ALU.subtract)
                dve.tensor_tensor(e2[:, :, 64:128], end1.to_broadcast([P, 2, 64]), a2[:, :, 64:128], ALU.subtract)
                dve.tensor_copy(e2[:, :, 128:192], a2[:, :, 128:192])
                dve.tensor_tensor(e2[:, :, 192:256], a2[:, :, 192:256], a2[:, :, 191:192].to_broadcast([P, 2, 64]),
                                  ALU.add).then_inc(lvl_arg, 1)

            def cross_decayed(n):
                dve.wait_ge(lvl_exp, n + 1)
                dve.wait_ge(lvl_mm, n - 1)
                e2 = hg_e[:, n % 2, :].rearrange("p (a t) -> p a t", a=2)
                d2 = hg_d[:, n % 2, :].rearrange("p (a t) -> p a t", a=2)
                dve.tensor_tensor(d2[:, :, 0:P], hg_k.rearrange("p (a t) -> p a t", a=2)[:, :, 0:P], e2[:, :, 0:P], ALU.mult)
                dve.tensor_tensor(d2[:, :, P:T], gqT[:, :, P:T], e2[:, :, P:T], ALU.mult).then_inc(lvl_dec, 1)

            def masked_max(hd):
                dve.wait_ge(score_mm, hd + 1)
                for c in range(TC):
                    g = row_of(hd, c)
                    v = fox_p[:, hd % 2, P * c:P * c + P * (c + 1)]
                    ins = dve.tensor_tensor_reduce(out=v, in0=psum[:, 7, P * c:P * c + P * (c + 1)],
                                                   in1=causal[:, P * (1 - c):], scale=1.0, scalar=-3e38,
                                                   op0=ALU.add, op1=ALU.max, accum_out=negmax[:, g:g + 1])
                    link(ins)
                    ins = dve.tensor_scalar(negmax[:, g:g + 1], negmax[:, g:g + 1], -1.0, None, ALU.mult)
                ins.then_inc(score_max, 1)

            def probT_copy(hd):
                dve.wait_ge(probT_mm, hd + 1)
                if hd >= 2:
                    dve.wait_ge(pv_mm, hd - 1)
                dve.tensor_copy(fox_pt[:, hd % 2, :], psum[:, 2, 0:3 * P]).then_inc(probT_ready, 1)

            def fox_divide(g):
                dve.wait_ge(pv_mm, 4 * g + 4)
                link(dve.reciprocal(rowinv[:, 8 * g:8 * g + 8], rowsum[:, 8 * g:8 * g + 8]))
                inv = rowinv[:, 8 * g:8 * g + 8].rearrange("p (c j) -> p c j", c=TC).unsqueeze(3)
                dve.tensor_tensor(fox_o[:, g, :].rearrange("p (c j d) -> p c j d", c=TC, j=4),
                                  psum[:, 5:7, g * T:(g + 1) * T].rearrange("p c (j d) -> p c j d", d=HD),
                                  inv.to_broadcast([P, TC, 4, HD]), ALU.mult).then_inc(fox_div, 1)

            def fox_variance(g):
                dve.wait_ge(fox_sqd, g + 1)
                m = fox_ms[:, 8 * g:8 * g + 8]
                link(dve.tensor_reduce(m, fox_sq[g].rearrange("p (g d) -> p g d", d=HD), AX, ALU.add))
                dve.tensor_scalar(m, m, 1.0 / HD, EPS, ALU.mult, ALU.add).then_inc(fox_var, 1)

            def fox_normalise(g):
                dve.wait_ge(fox_rstd, g + 1)
                v = fox_o[:, g, :].rearrange("p (g d) -> p g d", d=HD)
                dve.tensor_tensor(v, v, fox_r2[:, 8 * g:8 * g + 8].unsqueeze(2).to_broadcast([P, 8, HD]), ALU.mult
                                  ).then_inc(fox_ready, 1)

            dve.wait_ge(masks_ready, 1)
            for s in range(NSLOT):
                ahead, after, now = SLOT_LEVEL.get(s + 1), SLOT_LEVEL.get(s + 2), SLOT_LEVEL.get(s)
                if s == 4:
                    dve.wait_ge(proj_out, 2)
                if s == 5:
                    odd, even = slice(0, HD), slice(HD, P)
                    for rows, k_side in ((even, k_even), (odd, k_odd)):
                        for j in range(4):
                            ins = dve.tensor_scalar(k_side[rows, j, :], fox_l[rows], r_neg[rows, j:j + 1],
                                                    r_one[rows, j:j + 1], ALU.mult, ALU.add)
                    link(ins)
                    link(dve.tensor_scalar(fox_l, fox_l, l_scale, l_shift, ALU.mult, ALU.add))
                    for rows, q_side in ((even, q_even), (odd, q_odd)):
                        ins = dve.tensor_copy(q_side[rows, :, :], fox_l[rows].unsqueeze(1).to_broadcast([HD, 4, T]))
                    ins.then_inc(fox_lr, 1)
                if ahead == 8:
                    cross_decayed(7)
                elif ahead is not None and ahead < 7:
                    level_decayed(ahead)
                if s - 1 in SLOT_HEAD:
                    probT_copy(SLOT_HEAD[s - 1])
                if s in SLOT_HEAD:
                    masked_max(SLOT_HEAD[s])
                if now == 8:
                    dve.wait_ge(lvl_mm, 9)
                    dve.tensor_copy(hg_x_rows, psum[:, 3:5, 0:T]).then_inc(lvl_taken, 1)
                elif now is not None:
                    level_take(now)
                if after == 8:
                    dve.wait_ge(lvl_dec, 6)
                    cross_args(7)
                elif after is not None and after < 7:
                    level_args(after)
                if s == 8:
                    dve.wait_ge(consts, 2)
                    dve.reciprocal(win_inv, win_inv).then_inc(pooled_ready, 1)
                if s == SLOT_DIV0:
                    fox_divide(0)
                if s == SLOT_VAR0:
                    fox_variance(0)
                if s == SLOT_NORM0:
                    fox_normalise(0)
                if s == SLOT_HG_OUT:
                    dve.wait_ge(hg_mm, 1)
                    dve.tensor_copy(hg_o, psum[:, 3, :]).then_inc(hg_copied, 1)
                    dve.wait_ge(hg_sq, 1)
                    link(dve.tensor_reduce(hg_ms, hg_e[:, 0, :].rearrange("p (g d) -> p g d", d=HD), AX, ALU.add))
                    dve.tensor_scalar(hg_ms, hg_ms, 1.0 / HD, EPS, ALU.mult, ALU.add).then_inc(hg_var, 1)
            fox_divide(1)
            dve.wait_ge(silu_exp, 1)
            link(dve.tensor_scalar(hg_t, hg_t, 1.0, None, ALU.add))
            link(dve.reciprocal(hg_t, hg_t))
            fox_variance(1)
            link(dve.tensor_tensor(hg_t, hg_t, gg.rearrange("p c n -> p (c n)"), ALU.mult))
            link(dve.tensor_tensor(hg_t, hg_o, hg_t, ALU.mult))
            dve.wait_ge(hg_rstd, 1)
            dve.tensor_tensor(hg_o.rearrange("p (g d) -> p g d", d=HD), hg_t.rearrange("p (g d) -> p g d", d=HD),
                              hg_r2.unsqueeze(2).to_broadcast([P, 8, HD]), ALU.mult).then_inc(hg_ready, 1)
            fox_normalise(1)
            def residual(c, cols, banks):
                dve.tensor_tensor(h[:, c, cols], h[:, c, cols], psum[:, banks, :].rearrange("p a n -> p (a n)"),
                                  ALU.add).then_inc(h1_ready, 1)

            def route(c):
                dve.wait_ge(logit_mm, c + 1)
                dve.wait_ge(rstd2, c + 1)
                link(dve.scalar_tensor_tensor(out=logit[:, c, :], in0=psum[:, c, 0:E], scalar=rstd[:, c:c + 1],
                                              in1=br_sb[:, :], op0=ALU.mult, op1=ALU.add))
                link(dve.max(out=top8[:, c, :], in_=logit[:, c, :]))
                dve.tensor_scalar(negtop[:, c:c + 1], top8[:, c, 0:1], -1.0, None, ALU.mult).then_inc(top_ready, 1)
                fourth = top8[:, c, TOPK - 1:TOPK]
                dve.tensor_scalar(strict[:, c, :], logit[:, c, :], fourth, None, ALU.is_gt)
                link(dve.tensor_scalar(tie[:, c, :], logit[:, c, :], fourth, None, ALU.is_equal))
                dve.tensor_reduce(nstrict[:, c:c + 1], strict[:, c, :], AX, ALU.add)
                link(dve.tensor_tensor_scan(tie_n[:, c, :], ones_bf[:, 0:E], tie[:, c, :], 0.0, ALU.mult, ALU.add))
                link(dve.tensor_scalar(need[:, c:c + 1], nstrict[:, c:c + 1], -1.0, float(TOPK), ALU.mult, ALU.add))
                link(dve.scalar_tensor_tensor(out=tie[:, c, :], in0=tie_n[:, c, :], scalar=need[:, c:c + 1],
                                              in1=tie[:, c, :], op0=ALU.is_le, op1=ALU.mult))
                dve.tensor_tensor(chosen_b[:, c, :], strict[:, c, :], tie[:, c, :], ALU.add).then_inc(chosen_ready, 1)
                link(dve.tensor_tensor(chosen[:, c, :], strict[:, c, :], tie[:, c, :], ALU.add))

            dve.wait_ge(late_in, 80)
            dve.tensor_tensor(wr_sb[:, :, :], wr_sb[:, :, :], moe_gain.unsqueeze(2).to_broadcast([P, KC, E]), ALU.mult
                              ).then_inc(wr_ready, 1)
            dve.wait_ge(mix_mm, 1)
            residual(0, slice(0, D), slice(0, 2))
            dve.wait_ge(consts, 2)
            dve.tensor_scalar(which[:, 0, :], ones_bf[0:3 * E, 0:SLOTS], expert_id[:, 0:1], None, ALU.mult
                              ).then_inc(which_first, 1)
            dve.wait_ge(mix_mm, 2)
            residual(1, slice(0, D // 2), slice(3, 4))
            dve.wait_ge(h1T_mm, 1)
            dve.tensor_copy(h1T[:, 4:8, 0:P], psum[:, 6, :].rearrange("p (a t) -> p a t", a=4)).then_inc(h1T_dve, 1)
            route(0)
            dve.wait_ge(mix_mm, 3)
            residual(1, slice(D // 2, D), slice(4, 5))
            dve.wait_ge(h1T_mm, 3)
            dve.tensor_copy(h1T[:, 4:6, P:T], psum[:, 7, 0:T].rearrange("p (a t) -> p a t", a=2)).then_inc(h1T_dve, 1)
            route(1)
            dve.wait_ge(rank_mm, 1)
            for c in range(TC):
                ins = dve.scalar_tensor_tensor(out=rank_t[:, c, 0:E], in0=psum[:, 2, c * E:(c + 1) * E], scalar=1.0,
                                               in1=chosen[:, c, :], op0=ALU.add, op1=ALU.mult)
            link(ins)

            def select(i, b, reuse=True, which_too=True):
                if reuse:
                    dve.wait_ge(comb_mm, i - 1)
                for c in range(TC):
                    ins = dve.tensor_scalar(pick[:, b, c, :], iota2[:, 0, :], rank_t[:, c, bass.ds(i, 1)], None,
                                            ALU.is_equal)
                if which_too:
                    ins = dve.tensor_scalar(which[:, b, :], ones_bf[0:3 * E, 0:SLOTS], expert_id[:, bass.ds(i, 1)],
                                            None, ALU.mult)
                ins.then_inc(sel_ready, 1)

            def weight(i, b):
                for c in range(TC):
                    dve.tensor_scalar(put[:, b, c, :].rearrange("p (a s) -> p a s", a=2), iota2[:, :, :],
                                      rank_t[:, c, bass.ds(i, 1)], gate_t[:, c, bass.ds(i, 1)], ALU.is_equal, ALU.mult)

            def activate(i, reuse=True):
                pairs = psum[:, 3:5, :].rearrange("p a (f two) -> p (a f) two", two=2)
                dve.wait_ge(w1_used, KC * i + KC)
                if reuse:
                    dve.wait_ge(act_ready, i)
                dve.tensor_scalar(glu, pairs[:, :, 0], LIMIT, None, ALU.min).then_inc(glu_ready, 1)
                dve.tensor_scalar(lin, pairs[:, :, 1], -LIMIT, LIMIT, ALU.max, ALU.min).then_inc(lin_ready, 1)
                dve.wait_ge(lin_ready, i + 1)
                dve.wait_ge(glu_ready, i + 1)
                dve.scalar_tensor_tensor(out=lin, in0=lin, scalar=1.0, in1=glu, op0=ALU.add, op1=ALU.mult
                                         ).then_inc(gated, 1)
                dve.wait_ge(gated, i + 1)
                dve.wait_ge(sig_ready, i + 1)
                if reuse:
                    dve.wait_ge(actT_mm, i)
                dve.tensor_tensor(act_r, lin, sig, ALU.mult).then_inc(act_ready, 1)

            def add_up(i, second=1):
                for n_done, c in enumerate((1, 0) if second == 1 else (0, 1)):
                    dve.wait_ge(put_mm, TC * i + n_done + 1)
                    dve.tensor_tensor(h[:, c, :], h[:, c, :],
                                      psum[:, (6, second)[c]:(8, second + 2)[c], :].rearrange("p a n -> p (a n)"),
                                      ALU.add).then_inc(put_added, 1)
                dve.wait_ge(put_added, TC * i + TC)

            select(0, 0, reuse=False, which_too=False)
            link(dve.tensor_reduce(nmax, psum[:, 2, 2 * E:3 * E], AX, ALU.max))
            for c in range(TC):
                dve.wait_ge(gate_exp, c + 1)
                link(dve.tensor_tensor(expo[:, c, :], expo[:, c, :], chosen[:, c, :], ALU.mult))
                link(dve.tensor_reduce(gsum[:, c:c + 1], expo[:, c, :], AX, ALU.add))
                link(dve.reciprocal(ginv[:, c:c + 1], gsum[:, c:c + 1]))
                dve.tensor_scalar(gate_t[:, c, :].rearrange("p (a e) -> p a e", e=E),
                                  expo[:, c, :].unsqueeze(1).to_broadcast([P, PASSES, E]), ginv[:, c:c + 1], None,
                                  ALU.mult).then_inc(gate_ready, 1)
            for b in range(1, PASSES):
                ins = dve.tensor_scalar(over[:, b - 1:b], nmax, float(SLOTS * b), float(E // 2), ALU.is_gt, ALU.mult)
            link(ins)
            link(dve.tensor_reduce(nmax, over, AX, ALU.add))
            dve.tensor_copy(extra_pairs[0:1, :], nmax[0:1, :]).then_inc(count_ready, 1)
            for b in range(1, PASSES):
                for c in range(TC):
                    ins = dve.tensor_scalar(rank_t[:, c, b * E:(b + 1) * E], rank_t[:, c, 0:E], float(-SLOTS * b), None,
                                            ALU.add)
            link(ins)
            dve.wait_ge(gate_ready, 2)
            dve.wait_ge(count_ready, 1)
            extra = dve.value_load(extra_pairs[0:1, 0:1], min_val=0, max_val=(PASSES - 1) * E // 2)
            pairs = extra + E // 2
            n = extra * 2 + E
            select(1, 1, reuse=False)
            weight(0, 0)
            activate(0, reuse=False)
            weight(1, 1)
            activate(1)
            with dve.Fori(1, pairs - 1) as j:
                i = j * 2
                for b in range(2):
                    select(i + b, b)
                    weight(i + b, b)
                    add_up(i + b - 2)
                    activate(i + b)
            select(n - 2, 0)
            weight(n - 2, 0)
            add_up(n - 4)
            select(n - 1, 1)
            weight(n - 1, 1)
            activate(n - 2)
            add_up(n - 3)
            activate(n - 1)
            add_up(n - 2, second=3)
            dve.wait_ge(finalgain_in, 16)
            for c in range(TC):
                for g in range(2):
                    dve.wait_ge(last_mm, 2 * c + g + 1)
                    dve.tensor_tensor(h[:, c, row_half[g]], h[:, c, row_half[g]], psum[:, (6, 1)[c] + g, :], ALU.add
                                      ).then_inc(last_added, 1)
            dve.wait_ge(last_added, 4)
            for c in range(TC):
                dve.tensor_tensor(xn[:, c, row_half[1]], h[:, c, row_half[1]], gain_b[:, row_half[1]], ALU.mult
                                  ).then_inc(weighted, 1)
            for c in range(TC):
                dve.wait_ge(rstd3, c + 1)
                dve.scalar_tensor_tensor(out=xn[:, c, row_half[0]], in0=h[:, c, row_half[0]], scalar=rstd[:, c:c + 1],
                                         in1=gain_b[:, row_half[0]], op0=ALU.mult, op1=ALU.mult).then_inc(final_dve, 1)

        @block.tensor
        def _(pe):
            pe.wait_ge(ident_ready, 1)
            for c in range(TC):
                pe.wait_ge(xn_ready, c + 1)
                for k in range(KC):
                    last = pe.transpose(psum[:, 2 + k // 2, (k % 2) * T + c * P:(k % 2) * T + (c + 1) * P],
                                        xn[:, c, k * P:(k + 1) * P], ident[:, :])
                last.then_inc(xT_done, 1)
            pe.wait_ge(hT_ready, 4)
            pe.wait_ge(wff_ready, 1)
            pe.matmul(psum[:, 6, 0:T], ffb_row, ones_row, start=True, stop=False)
            for k in range(KC):
                last = pe.matmul(psum[:, 6, 0:T], wff[:, k, :], hT[:, k, :], start=False, stop=k == KC - 1)
            last.then_inc(ff_done, 1)

            def project(n, half):
                _, _, transposed = BLOCKS[n]
                w = block_sb(n)
                if half == 0:
                    pe.wait_ge(block_in[n], 16)
                    if n >= 2:
                        pe.wait_ge(proj_out, n - 1)
                for k in range(KC):
                    if transposed:
                        lhs, rhs = w[:, k, half * P:(half + 1) * P], hT[:, k, :]
                    else:
                        lhs, rhs = hT[:, k, half * P:(half + 1) * P], w[:, k, :]
                    last = pe.matmul(psum[:, n % 2, half * T:(half + 1) * T], lhs, rhs, start=k == 0,
                                     stop=k == KC - 1)
                if half == 1:
                    last.then_inc(proj_done, 1)

            def level(n):
                if n < 7:
                    pe.wait_ge(lvl_dec, n + 1)
                if n == 0:
                    pe.wait_ge(hT_ready, 4)
                if n >= 1:
                    pe.wait_ge(lvl_taken, n)
                for c in range(TC):
                    for hd in range(HG_H):
                        rows = slice(HD * (hd % 2), HD * (hd % 2) + HD)
                        span = slice((hd // 2) * T + c * P, (hd // 2) * T + (c + 1) * P)
                        if n < 7:
                            lhs, rhs = hg_d[rows, n % 2, span], hg_d[rows, n % 2, span]
                        else:
                            lhs, rhs = hg_k[rows, span], gqT[rows, hd // 2, c * P:(c + 1) * P]
                        j = c * 2 + hd // 2
                        last = pe.matmul(psum[:, 3 + hd % 2, j * P:(j + 1) * P], lhs, rhs, start=True, stop=True)
                last.then_inc(lvl_mm, 1)

            def cross():
                pe.wait_ge(lvl_dec, 8)
                pe.wait_ge(lvl_taken, 8)
                for hd in range(HG_H):
                    rows = slice(HD * (hd % 2), HD * (hd % 2) + HD)
                    o = (hd // 2) * T
                    last = pe.matmul(psum[:, 3 + hd % 2, (hd // 2) * P:(hd // 2 + 1) * P], hg_d[rows, 1, o:o + P],
                                     hg_d[rows, 1, o + P:o + T], start=True, stop=True)
                last.then_inc(lvl_mm, 1)

            def scores(hd):
                q, k = ((q_even, k_even), (q_odd, k_odd))[hd % 2]
                if hd == 0:
                    pe.wait_ge(fox_lr, 1)
                pe.wait_ge(proj_out, 4 if hd < 4 else 8)
                if hd >= 1:
                    pe.wait_ge(score_max, hd)
                for c in range(TC):
                    last = pe.matmul(psum[:, 7, P * c:P * c + P * (c + 1)], q[:, hd // 2, c * P:(c + 1) * P],
                                     k[:, hd // 2, 0:P * (c + 1)], start=True, stop=True)
                last.then_inc(score_mm, 1)

            def probT(hd):
                pe.wait_ge(prob_ready, TC * (hd + 1))
                if hd >= 1:
                    pe.wait_ge(probT_ready, hd)
                for j in range(3):
                    last = pe.transpose(psum[:, 2, j * P:(j + 1) * P], fox_p[:, hd % 2, j * P:(j + 1) * P], ident[:, :])
                last.then_inc(probT_mm, 1)

            def weigh(hd):
                pe.wait_ge(probT_ready, hd + 1)
                pe.wait_ge(proj_out, 5 if hd < 4 else 9)
                if hd == 4:
                    pe.wait_ge(fox_div, 1)
                span = slice(hd * HD, (hd + 1) * HD)
                pe.matmul(psum[:, 5, span], fox_pt[:, hd % 2, 0:P], v_sb[:, 0, span], start=True, stop=True)
                pe.matmul(psum[:, 6, span], fox_pt[:, hd % 2, P:2 * P], v_sb[:, 0, span], start=True, stop=False)
                pe.matmul(psum[:, 6, span], fox_pt[:, hd % 2, 2 * P:3 * P], v_sb[:, 1, span], start=False, stop=True
                          ).then_inc(pv_mm, 1)

            def pooled():
                pe.wait_ge(pooled_ready, 2)
                pe.wait_ge(small_in, 80)
                pe.wait_ge(lvl_taken, 9)
                for g in range(4):
                    rows = slice(HD * (g % 2), HD * (g % 2) + HD)
                    last = pe.matmul(psum[rows, 4 - g % 2, (g // 2) * T:(g // 2 + 1) * T], poolw_sb[rows, g // 2, :],
                                     win_b[rows, g // 2, :], start=True, stop=True)
                last.then_inc(pool_mm, 1)

            def hgrn_out():
                pe.wait_ge(proj_out, 10)
                pe.wait_ge(pool_out, 4)
                for c in range(TC):
                    for g in range(HG_H):
                        o = psum[:, 3, c * T + g * HD:c * T + (g + 1) * HD]
                        last = pe.matmul(o, hg_s[:, (g % 2) * 4 + c * 2 + g // 2, :], gi[:, c, g * HD:(g + 1) * HD],
                                         start=True, stop=c == 0)
                        if c == 1:
                            last = pe.matmul(o, hg_x[:, (g % 2) * 2 + g // 2, :], gi[:, 0, g * HD:(g + 1) * HD],
                                             start=False, stop=True)
                last.then_inc(hg_mm, 1)

            def fox_transpose(g, bank):
                pe.wait_ge(fox_ready, g + 1)
                for a in range(2):
                    for c in range(TC):
                        last = pe.transpose(psum[:, bank, a * T + c * P:a * T + (c + 1) * P],
                                            fox_o[:, g, c * T + a * P:c * T + (a + 1) * P], ident[:, :])
                last.then_inc(foxT_mm, 1)

            for s in range(NSLOT):
                project(s // 2, s % 2)
                if s - 1 in SLOT_HEAD:
                    probT(SLOT_HEAD[s - 1])
                if s - 2 in SLOT_HEAD:
                    weigh(SLOT_HEAD[s - 2])
                if s in SLOT_HEAD:
                    scores(SLOT_HEAD[s])
                if SLOT_LEVEL.get(s) == 8:
                    cross()
                elif s in SLOT_LEVEL:
                    level(SLOT_LEVEL[s])
                if s == SLOT_POOL:
                    pooled()
                if s == SLOT_HG_OUT:
                    hgrn_out()
                    fox_transpose(0, 4)

            def mix(c, chunks, halves=(0, 1)):
                for k in chunks:
                    for half in halves:
                        last = pe.matmul(psum[:, (0, 3)[c] + half, :], oT[k - k % 2][:, k % 2, c * P:(c + 1) * P],
                                         w2_ring[:, 1, k, half * 512:(half + 1) * 512], start=k == 6, stop=k == 3)
                return last

            for n in range(4):
                pe.wait_ge(wout_in[n], 16)
            pe.wait_ge(foxT_out, 2)
            pe.wait_ge(hg_copied, 1)
            mix(1, (6, 7, 0, 1))
            pe.wait_ge(proj_out, NB)
            mix(0, (6, 7))
            pe.wait_ge(hg_ready, 1)
            for a in range(2):
                for c in range(TC):
                    last = pe.transpose(psum[:, 2, a * T + c * P:a * T + (c + 1) * P],
                                        hg_o[:, c * T + a * P:c * T + (a + 1) * P], ident[:, :])
            last.then_inc(hgT_mm, 1)
            mix(0, (0, 1)).then_inc(mix_part, 1)
            fox_transpose(1, 7)
            pe.wait_ge(hgT_out, 2)
            mix(0, (4, 5))
            pe.wait_ge(foxT_out, 4)
            mix(0, (2, 3)).then_inc(mix_mm, 1)
            mix(1, (4, 5, 2, 3), (0,)).then_inc(mix_mm, 1)

            def h1_transpose(c, k, bank, j):
                return pe.transpose(psum[:, bank, j * P:(j + 1) * P], h[:, c, k * P:(k + 1) * P], ident[:, :])

            def router(c, chunks):
                for k in chunks:
                    last = pe.matmul(psum[:, c, 0:E], h1T[:, k, c * P:(c + 1) * P], wr_sb[:, k, :],
                                     start=k == 0, stop=k == KC - 1)
                return last

            pe.wait_ge(h1_ready, 1)
            for k in range(KC):
                last = h1_transpose(0, k, 5 + k // 4, k % 4)
            last.then_inc(h1T_mm, 1)
            pe.wait_ge(h1_ready, 2)
            for k in range(4):
                last = h1_transpose(1, k, 2, k)
            last.then_inc(h1T_mm, 1)
            pe.wait_ge(wr_ready, 1)
            pe.wait_ge(h1T_act, 1)
            pe.wait_ge(h1T_dve, 1)
            router(0, range(KC)).then_inc(logit_mm, 1)
            mix(1, (4, 5, 2, 3), (1,)).then_inc(mix_mm, 1)
            pe.wait_ge(h1_ready, 3)
            for k in (4, 5):
                h1_transpose(1, k, 7, k - 4)
            for k in (6, 7):
                last = h1_transpose(1, k, 5, k - 6)
            last.then_inc(h1T_mm, 1)
            pe.wait_ge(h1T_act, 2)
            router(1, range(4))
            pe.wait_ge(h1T_dve, 2)
            router(1, (4, 5))
            pe.wait_ge(h1T_act, 3)
            router(1, (6, 7)).then_inc(logit_mm, 1)
            for _ in range(WARM):
                pe.matmul(psum[:, 6, 0:KC * E], ident[:, :], wr_sb[:, :, :].rearrange("p k e -> p (k e)"), start=True,
                          stop=True)
            pe.wait_ge(chosen_ready, 2)
            pe.matmul(psum[:, 2, 0:E], before[:, :], chosen_b[:, 0, :], start=True, stop=True)
            pe.matmul(psum[:, 2, E:2 * E], ones_bf[:, :], chosen_b[:, 0, :], start=True, stop=False)
            pe.matmul(psum[:, 2, E:2 * E], before[:, :], chosen_b[:, 1, :], start=False, stop=True)
            pe.matmul(psum[:, 2, 2 * E:3 * E], ones_bf[:, :], chosen_b[:, 0, :], start=True, stop=False)
            pe.matmul(psum[:, 2, 2 * E:3 * E], ones_bf[:, :], chosen_b[:, 1, :], start=False, stop=True
                      ).then_inc(rank_mm, 1)

            def gather_chunks(b, chunks, bank):
                for k in chunks:
                    for c in range(TC):
                        last = pe.matmul(psum[:, bank, k * SLOTS:(k + 1) * SLOTS], xn[:, c, k * P:(k + 1) * P],
                                         pick[:, b, c, :], start=c == 0, stop=c == TC - 1)
                return last

            def gather(i, b):
                pe.wait_ge(sel_ready, i + 1)
                gather_chunks(b, range(KC), 0).then_inc(gather_mm, 1)

            def transpose_act(i, b, reuse=True, free=0):
                pe.wait_ge(act_ready, i + 1)
                if reuse:
                    pe.wait_ge(put_added, TC * (i - free) - 1)
                for j in range(4):
                    last = pe.transpose(psum[:, 1, j * P:(j + 1) * P], act_r[:, j * P:(j + 1) * P], ident[:, :])
                last.then_inc(actT_mm, 1)
                for c in range(TC):
                    last = pe.transpose(psum[:, 2, c * P:(c + 1) * P], put[:, b, c, :], ident[:, :])
                last.then_inc(comb_mm, 1)

            def up_bias(b):
                for q in range(2):
                    for g in range(2):
                        pe.matmul(psum[g * SLOTS:(g + 1) * SLOTS, 3 + q, :], which[:, b, :],
                                  b1_parts[:, g * F + q * 512:g * F + (q + 1) * 512], start=True, stop=False)

            def up_chunk(k, w, stop):
                for q in range(2):
                    for g in range(2):
                        last = pe.matmul(psum[g * SLOTS:(g + 1) * SLOTS, 3 + q, :], xe[:, k, :],
                                         w[:, g * F + q * 512:g * F + (q + 1) * 512], start=False, stop=stop)
                last.then_inc(w1_used, 1)

            def up(i, b):
                up_start(i, b)
                up_ring(i, range(KC))

            def up_start(i, b):
                pe.wait_ge(lin_ready, i)
                up_bias(b)
                pe.wait_ge(xe_ready, i + 1)

            def up_ring(i, chunks):
                for k in chunks:
                    pe.wait_ge(w1_in[k], 16 * i if k < EARLY else 16 * i + 16)
                    up_chunk(k, w1_ring[:, k, :], k == KC - 1)

            def down(i, b, loaded, reuse=True):
                pe.wait_ge(actT_ready, i + 1)
                if reuse:
                    pe.wait_ge(y_ready, i)
                for k in range(KC):
                    if k % 2 == 0:
                        pe.wait_ge(w2_in[b][k // 2], loaded)
                    for g in range(2):
                        last = pe.matmul(psum[g * SLOTS:(g + 1) * SLOTS, 5, :],
                                         actT[:, k % 4, (k // 4) * SLOTS:(k // 4 + 1) * SLOTS],
                                         w2_ring[:, b, k, g * 512:(g + 1) * 512], start=k == 0, stop=k == KC - 1)
                    if k % 2:
                        last.then_inc(w2_used, 1)

            def combine(i, reuse=True, start=True, second=1):
                pe.wait_ge(y_ready, i + 1)
                pe.wait_ge(comb_ready, i + 1)
                for c in (1, 0) if second == 1 else (0, 1):
                    if c == 0 and reuse:
                        pe.wait_ge(put_added, TC * i)
                    if c == 1 and second == 3:
                        pe.wait_ge(lin_ready, i + 2)
                    for g in range(2):
                        last = pe.matmul(psum[:, (6, second)[c] + g, :], comb[g * SLOTS:(g + 1) * SLOTS, c, :],
                                         y_sb[g * SLOTS:(g + 1) * SLOTS, :], start=start, stop=True)
                    last.then_inc(put_mm, 1)

            def item(i, b, loaded):
                gather(i, b)
                transpose_act(i - 1, 1 - b)
                up(i, b)
                down(i - 1, 1 - b, loaded)
                combine(i - 1)

            pe.wait_ge(which_first, 1)
            up_bias(0)
            pe.wait_ge(xn2_ready, TC)
            pe.wait_ge(sel_ready, 1)
            gather_chunks(0, (4, 5), 0).then_inc(gather_first, 1)
            gather_chunks(0, (6, 7), 6).then_inc(gather_first, 1)
            for k in range(EARLY, KC):
                pe.wait_ge(xe_first, k // 2 - 1)
                pe.wait_ge(w1_in[k], 16)
                up_chunk(k, w1_ring[:, k, :], False)
            gather_chunks(0, range(4), 7).then_inc(gather_mm, 1)
            pe.wait_ge(xe_ready, 1)
            for k in range(EARLY):
                pe.wait_ge(early_in[k], 16)
                up_chunk(k, w1_early[k], k == EARLY - 1)
            gather(1, 1)
            pe.wait_ge(count_ready, 1)
            extra = pe.value_load(extra_pairs[0:1, 0:1], min_val=0, max_val=(PASSES - 1) * E // 2)
            pairs = extra + E // 2
            n = extra * 2 + E
            up(1, 1)
            transpose_act(0, 0, reuse=False)
            for c in range(TC):
                last = pe.transpose(psum[:, 0, c * P:(c + 1) * P], gate_t[:, c, :], ident[:, :])
            last.then_inc(gateT_mm, 1)
            down(0, 0, 16, reuse=False)
            combine(0, reuse=False)
            with pe.Fori(1, pairs - 1) as j:
                i = j * 2
                item(i, 0, 8 * i)
                item(i + 1, 1, 8 * i + 16)
            gather(n - 2, 0)
            transpose_act(n - 3, 1)
            up_start(n - 2, 0)
            up_ring(n - 2, range(4))
            pe.wait_ge(gateT_out, 1)
            pe.wait_ge(actT_ready, n - 2)
            pe.wait_ge(comb_ready, n - 2)
            pe.wait_ge(put_added, TC * (n - 3))
            for c in range(TC):
                for half in range(2):
                    pe.matmul(psum[:, (6, 1)[c] + half, :], gateT[:, c * P:(c + 1) * P],
                              b2_sb[:, half * 512:(half + 1) * 512], start=True, stop=False)
            up_ring(n - 2, range(4, 6))
            gather(n - 1, 1)
            up_ring(n - 2, range(6, KC))
            down(n - 3, 1, 8 * n - 16)
            combine(n - 3, start=False)
            transpose_act(n - 2, 0)
            down(n - 2, 0, 8 * n)
            up(n - 1, 1)
            combine(n - 2, second=3)
            transpose_act(n - 1, 1, free=1)
            down(n - 1, 1, 8 * n)
            pe.wait_ge(y_ready, n)
            pe.wait_ge(comb_ready, n)
            pe.wait_ge(put_added, TC * (n - 1))
            for c in range(TC):
                for g in range(2):
                    pe.matmul(psum[:, (6, 1)[c] + g, :], comb[g * SLOTS:(g + 1) * SLOTS, c, :],
                              y_sb[g * SLOTS:(g + 1) * SLOTS, :], start=True, stop=True).then_inc(last_mm, 1)


_INS = ["x", "norm_mix", "w_in", "b_fox_f", "fox_gain", "hgrn_lb", "hgrn_gain", "pool_w", "pool_scale", "w_out",
        "norm_moe", "w_router", "b_router", "w1", "b1", "w2", "b2", "norm_final"]


def kernel(**inputs):
    import numpy as _np
    import concourse.bacc as _bacc
    from concourse import mybir as _mybir
    from concourse.bass_utils import run_bass_kernel_spmd as _run

    nc = _bacc.Bacc("TRN2", target_bir_lowering=False, num_devices=1)
    arrays, args = {}, []
    for name in _INS:
        a = _np.ascontiguousarray(inputs[name])
        arrays[f"in_{name}_dram"] = a
        args.append(nc.dram_tensor(f"in_{name}_dram", a.shape, _mybir.dt.from_np(a.dtype), kind="ExternalInput").ap())
    args.append(nc.dram_tensor("out_0_dram", (1, T, D), _mybir.dt.float32, kind="ExternalOutput").ap())
    build(nc, *args)
    r = _run(nc, [arrays], core_ids=[0])
    return r.results[0]["out_0_dram"]
```
